# Optimizing a Trainium2 kernel written in Bass

```python
import jax, jax.numpy as jnp
from jax import lax
import numpy as np

D_MODEL = 1024
BATCH = 1
SEQ = 1024
DEPTH = 2
DEC_BATCH = 8
DEC_SEQ = 8
PAST_LEN = 2048
PAGE_SIZE = 128

BRANCH_W = D_MODEL // 2
N_BRANCHES = 5
N_MIXERS = 4
GLA_HEADS = 4
GLA_DK = BRANCH_W // (2 * GLA_HEADS)
GLA_DV = BRANCH_W // GLA_HEADS
GLA_RANK = 16
GLA_TAU = 16.0
GLA_CHUNK = 64
LRU_W = BRANCH_W
LRU_BLOCKS = 8
LRU_BS = LRU_W // LRU_BLOCKS
CONV_W = 4
LRU_C = 8.0
HEAD_DIM = 64
SWA_HEADS = BRANCH_W // HEAD_DIM
SWA_KV_HEADS = 2
SWA_GROUP = SWA_HEADS // SWA_KV_HEADS
WINDOW = 128
SWA_BLOCK = 128
ROT_DIM = HEAD_DIM // 4
ROPE_THETA = 500000.0
SGU_W = BRANCH_W
SGU_GROUPS = 4
SGU_GC = SGU_W // SGU_GROUPS
SGU_CHUNK = 128
N_MEM = 256
MEM_HEADS = 4
MEM_W = MEM_HEADS * HEAD_DIM
LN_EPS = 1e-5
RMS_EPS = 1e-6
DN_ALPHA = (2 * DEPTH) ** 0.25
DN_BETA = (8 * DEPTH) ** -0.25

IN_SPLITS = (GLA_HEADS * GLA_DK, GLA_HEADS * GLA_DK, GLA_HEADS * GLA_DV, GLA_RANK, BRANCH_W,
             LRU_W, LRU_W,
             SWA_HEADS * HEAD_DIM, SWA_KV_HEADS * HEAD_DIM, SWA_KV_HEADS * HEAD_DIM, BRANCH_W,
             SGU_W, SGU_W, SGU_W,
             MEM_W, MEM_W,
             N_BRANCHES * D_MODEL)
N_IN = sum(IN_SPLITS)

kernel_name = 'hybrid_gla_rglru_swa_gmlp_mem_decoder_step'

def layer_norm(x, g, b):
    xf = x.astype(jnp.float32)
    mu = jnp.mean(xf, axis=-1, keepdims=True)
    var = jnp.mean(jnp.square(xf - mu), axis=-1, keepdims=True)
    return ((xf - mu) * lax.rsqrt(var + LN_EPS) * g + b).astype(x.dtype)

def partial_rope(x, pos):
    half = ROT_DIM // 2
    inv = ROPE_THETA ** (-jnp.arange(half, dtype=jnp.float32) / half)
    ang = pos.astype(jnp.float32)[:, None] * inv[None, :]
    cos = jnp.cos(ang)[None, :, None, :]
    sin = jnp.sin(ang)[None, :, None, :]
    xf = x.astype(jnp.float32)
    x1, x2 = xf[..., :half], xf[..., half:ROT_DIM]
    rot = jnp.concatenate([x1 * cos - x2 * sin, x2 * cos + x1 * sin], axis=-1).astype(x.dtype)
    return jnp.concatenate([rot, x[..., ROT_DIM:]], axis=-1)

def gla_mix(q, k, v, log_a, s0):
    B, T, H, DK = q.shape
    C = min(GLA_CHUNK, T)
    n = T // C

    def blocks(t):
        return jnp.moveaxis(t.reshape(B, n, C, H, t.shape[-1]), 1, 0)

    causal = jnp.tril(jnp.ones((C, C), dtype=bool))[None, :, :, None, None]

    def step(S, inp):
        qc, kc, vc, ac = inp
        b = jnp.cumsum(ac, axis=1)
        o_inter = jnp.einsum('bthk,bhkv->bthv', qc * jnp.exp(b), S)
        diff = jnp.where(causal, b[:, :, None] - b[:, None, :], -jnp.inf)
        att = jnp.einsum('btshk,bshk->bhts', qc[:, :, None] * jnp.exp(diff), kc)
        o_intra = jnp.einsum('bhts,bshv->bthv', att, vc)
        b_last = b[:, -1]
        S = S * jnp.exp(b_last)[..., None] + jnp.einsum(
            'bshk,bshv->bhkv', kc * jnp.exp(b_last[:, None] - b), vc)
        return S, o_inter + o_intra

    s_fin, o = lax.scan(step, s0, (blocks(q), blocks(k), blocks(v), blocks(log_a)))
    return jnp.moveaxis(o, 0, 1).reshape(B, T, H, v.shape[-1]), s_fin

def causal_conv(x, buf, w, b):
    T = x.shape[1]
    xp = jnp.concatenate([buf.astype(x.dtype), x], axis=1)
    y = b
    for j in range(CONV_W):
        y = y + xp[:, j:j + T] * w[j]
    return y, xp[:, -(CONV_W - 1):]

def rg_lru(xc, h0, wr, br, wi, bi, lam):
    B, T, W = xc.shape
    xb = xc.reshape(B, T, LRU_BLOCKS, LRU_BS)
    r = jax.nn.sigmoid(jnp.einsum('btnc,ncd->btnd', xb, wr).reshape(B, T, W) + br)
    i = jax.nn.sigmoid(jnp.einsum('btnc,ncd->btnd', xb, wi).reshape(B, T, W) + bi)
    log_a = (LRU_C * r * jax.nn.log_sigmoid(lam)).astype(jnp.float32)
    a = jnp.exp(log_a)
    u = jnp.sqrt(-jnp.expm1(2.0 * log_a)) * (i * xc).astype(jnp.float32)

    def step(h, inp):
        a_t, u_t = inp
        h = a_t * h + u_t
        return h, h

    h_fin, hs = lax.scan(step, h0.astype(jnp.float32), (jnp.swapaxes(a, 0, 1), jnp.swapaxes(u, 0, 1)))
    return jnp.swapaxes(hs, 0, 1).astype(xc.dtype), h_fin

def swa_sink_attention(q, k, v, k_past, v_past, pos0, sinks):
    B, T = q.shape[:2]
    QB = min(SWA_BLOCK, T)
    nb = T // QB
    k_all = jnp.concatenate([k_past.astype(k.dtype), k], axis=1)
    v_all = jnp.concatenate([v_past.astype(v.dtype), v], axis=1)
    band = jnp.arange(nb)[:, None] * QB + jnp.arange(QB + WINDOW)[None, :]
    kb = k_all[:, band]
    vb = v_all[:, band]
    qb = q.reshape(B, nb, QB, SWA_KV_HEADS, SWA_GROUP, HEAD_DIM)
    q_pos = pos0 + jnp.arange(nb)[:, None] * QB + jnp.arange(QB)[None, :]
    k_pos = pos0 - WINDOW + band
    dist = q_pos[:, :, None] - k_pos[:, None, :]
    mask = (dist >= 0) & (dist <= WINDOW) & (k_pos[:, None, :] >= 0)
    s = jnp.einsum('bnqhgd,bnshd->bnhgqs', qb, kb).astype(jnp.float32) * (HEAD_DIM ** -0.5)
    s = jnp.where(mask[None, :, None, None], s, -jnp.inf)
    sink = jnp.broadcast_to(sinks.reshape(SWA_KV_HEADS, SWA_GROUP, 1, 1).astype(jnp.float32),
                            s.shape[:-1] + (1,))
    p = jax.nn.softmax(jnp.concatenate([s, sink], axis=-1), axis=-1)[..., :-1].astype(v.dtype)
    o = jnp.einsum('bnhgqs,bnshd->bnqhgd', p, vb)
    return o.reshape(B, T, SWA_HEADS * HEAD_DIM), k_all[:, -WINDOW:], v_all[:, -WINDOW:]

def sgu_mix(u, v, ln_g, ln_b, w_s, b_s):
    B, T, _ = u.shape
    vn = layer_norm(v, ln_g, ln_b)
    Tp = -(-T // SGU_CHUNK) * SGU_CHUNK
    vp = jnp.pad(vn, ((0, 0), (0, Tp - T), (0, 0))).reshape(B, Tp // SGU_CHUNK, SGU_CHUNK, SGU_GROUPS, SGU_GC)
    w_c = w_s * jnp.tril(jnp.ones((SGU_CHUNK, SGU_CHUNK), dtype=w_s.dtype))
    mixed = jnp.einsum('gts,bnsgc->bntgc', w_c, vp) + b_s.T[None, None, :, :, None]
    mixed = mixed.reshape(B, Tp, SGU_W)[:, :T]
    return u * mixed, vn

def mem_attention(q, mk, mv):
    B, T = q.shape[:2]
    s = jnp.einsum('bthd,bshd->bhts', q, mk.astype(q.dtype)).astype(jnp.float32) * (HEAD_DIM ** -0.5)
    p = jax.nn.softmax(s, axis=-1).astype(q.dtype)
    return jnp.einsum('bhts,bshd->bthd', p, mv.astype(q.dtype)).reshape(B, T, MEM_W)

def trunk_layer(x, pos0, gla_s0, lru_h0, conv_buf, swa_k_past, swa_v_past, mem_k, mem_v, lp):
    (w_in, gla_wa2, gla_ba, gla_norm_g, lru_conv_w, lru_conv_b, lru_wr, lru_br, lru_wi, lru_bi, lru_L,
     swa_sinks, sgu_ln_g, sgu_ln_b, sgu_w, sgu_b, w_branch, w_branch_mem, w_out, ln_g, ln_b) = lp
    B, T, _ = x.shape
    f32 = jnp.float32
    proj = x @ w_in
    offs = [int(o) for o in np.cumsum(IN_SPLITS)[:-1]]
    (gq, gk, gv, glr, gz, lx, lz, sq, sk, sv, sz, su, svv, suz, mq, mz, gates) = jnp.split(proj, offs, axis=-1)

    log_a = jax.nn.log_sigmoid((glr @ gla_wa2 + gla_ba).astype(f32)) / GLA_TAU
    qh = gq.reshape(B, T, GLA_HEADS, GLA_DK).astype(f32) * (GLA_DK ** -0.5)
    kh = gk.reshape(B, T, GLA_HEADS, GLA_DK).astype(f32)
    vh = gv.reshape(B, T, GLA_HEADS, GLA_DV).astype(f32)
    o, gla_s = gla_mix(qh, kh, vh, log_a.reshape(B, T, GLA_HEADS, GLA_DK), gla_s0.astype(f32))
    o = o * lax.rsqrt(jnp.mean(o * o, axis=-1, keepdims=True) + RMS_EPS) * gla_norm_g
    y_gla = o.reshape(B, T, BRANCH_W).astype(x.dtype) * jax.nn.silu(gz)

    xc, conv_new = causal_conv(lx, conv_buf, lru_conv_w, lru_conv_b)
    h, lru_h = rg_lru(xc, lru_h0, lru_wr, lru_br, lru_wi, lru_bi, lru_L)
    y_lru = h * jax.nn.silu(lz)

    pos = pos0 + jnp.arange(T)
    qs = partial_rope(sq.reshape(B, T, SWA_HEADS, HEAD_DIM), pos)
    ks = partial_rope(sk.reshape(B, T, SWA_KV_HEADS, HEAD_DIM), pos)
    vs = sv.reshape(B, T, SWA_KV_HEADS, HEAD_DIM)
    o_swa, swa_k, swa_v = swa_sink_attention(qs, ks, vs, swa_k_past, swa_v_past, pos0, swa_sinks)
    y_swa = o_swa * jax.nn.silu(sz)

    o_sgu, sgu_v = sgu_mix(su, svv, sgu_ln_g, sgu_ln_b, sgu_w, sgu_b)
    y_sgu = o_sgu * jax.nn.silu(suz)

    o_mem = mem_attention(mq.reshape(B, T, MEM_HEADS, HEAD_DIM), mem_k, mem_v)
    y_mem = o_mem * jax.nn.silu(mz)

    g = jax.nn.sigmoid(gates).reshape(B, T, N_BRANCHES, D_MODEL)
    ys = (y_gla, y_lru, y_swa, y_sgu)
    merged = g[:, :, N_MIXERS] * (y_mem @ w_branch_mem)
    for n in range(N_MIXERS):
        merged = merged + g[:, :, n] * (ys[n] @ w_branch[n])
    out = merged @ w_out
    x_new = layer_norm(DN_ALPHA * x + out, ln_g, ln_b)
    return x_new, (gla_s.astype(x.dtype), lru_h.astype(x.dtype), conv_new, swa_k, swa_v, sgu_v)

def setup_inputs(seed: int = 0) -> dict:
    key = jax.random.key(seed)
    keys = iter(jax.random.split(key, 48))
    f32 = jnp.float32

    def nrm(shape, scale):
        return jax.random.normal(next(keys), shape, f32) * scale

    D = D_MODEL
    inp = {}
    inp['x_prompt'] = nrm((BATCH, SEQ, D), 1.0)
    inp['x_sample'] = nrm((DEC_BATCH, DEC_SEQ, D), 1.0)
    inp['mem_prompt'] = nrm((BATCH, N_MEM, D), 1.0)
    inp['state_gla'] = nrm((DEPTH, DEC_BATCH, GLA_HEADS, GLA_DK, GLA_DV), 0.5)
    inp['state_lru_h'] = nrm((DEPTH, DEC_BATCH, LRU_W), 0.5)
    inp['state_lru_conv'] = nrm((DEPTH, DEC_BATCH, CONV_W - 1, LRU_W), 1.0)
    inp['cache_swa_k'] = nrm((DEPTH, DEC_BATCH, WINDOW, SWA_KV_HEADS, HEAD_DIM), 1.0)
    inp['cache_swa_v'] = nrm((DEPTH, DEC_BATCH, WINDOW, SWA_KV_HEADS, HEAD_DIM), 1.0)
    inp['cache_mem_k'] = nrm((DEPTH, DEC_BATCH, N_MEM, MEM_HEADS, HEAD_DIM), 1.0)
    inp['cache_mem_v'] = nrm((DEPTH, DEC_BATCH, N_MEM, MEM_HEADS, HEAD_DIM), 1.0)
    inp['ln_in_g'] = 1.0 + nrm((D,), 0.02)
    inp['ln_in_b'] = nrm((D,), 0.02)
    inp['w_in'] = nrm((DEPTH, D, N_IN), D ** -0.5)
    inp['gla_wa2'] = nrm((DEPTH, GLA_RANK, GLA_HEADS * GLA_DK), GLA_RANK ** -0.5)
    inp['gla_ba'] = nrm((DEPTH, GLA_HEADS * GLA_DK), 0.1)
    inp['gla_norm_g'] = 1.0 + nrm((DEPTH, GLA_DV), 0.02)
    inp['lru_conv_w'] = nrm((DEPTH, CONV_W, LRU_W), CONV_W ** -0.5)
    inp['lru_conv_b'] = nrm((DEPTH, LRU_W), 0.02)
    inp['lru_wr'] = nrm((DEPTH, LRU_BLOCKS, LRU_BS, LRU_BS), LRU_BS ** -0.5)
    inp['lru_br'] = nrm((DEPTH, LRU_W), 0.02)
    inp['lru_wi'] = nrm((DEPTH, LRU_BLOCKS, LRU_BS, LRU_BS), LRU_BS ** -0.5)
    inp['lru_bi'] = nrm((DEPTH, LRU_W), 0.02)
    a0 = jax.random.uniform(next(keys), (DEPTH, LRU_W), f32, 0.9, 0.999)
    inp['lru_L'] = jnp.log(a0) - jnp.log1p(-a0)
    inp['swa_sinks'] = nrm((DEPTH, SWA_HEADS), 1.0)
    inp['sgu_ln_g'] = 1.0 + nrm((DEPTH, SGU_W), 0.02)
    inp['sgu_ln_b'] = nrm((DEPTH, SGU_W), 0.02)
    inp['sgu_w'] = nrm((DEPTH, SGU_GROUPS, SGU_CHUNK, SGU_CHUNK), SGU_CHUNK ** -0.5)
    inp['sgu_b'] = 1.0 + nrm((DEPTH, SGU_GROUPS, SGU_CHUNK), 0.02)
    inp['w_mem_kv'] = nrm((DEPTH, D, 2 * MEM_W), D ** -0.5)
    inp['w_branch'] = nrm((DEPTH, N_MIXERS, BRANCH_W, D), BRANCH_W ** -0.5 * DN_BETA)
    inp['w_branch_mem'] = nrm((DEPTH, MEM_W, D), MEM_W ** -0.5 * DN_BETA)
    inp['w_out'] = nrm((DEPTH, D, D), D ** -0.5 * DN_BETA)
    inp['ln_g'] = 1.0 + nrm((DEPTH, D), 0.02)
    inp['ln_b'] = nrm((DEPTH, D), 0.02)
    return inp

def reference(x_prompt, x_sample, mem_prompt, state_gla, state_lru_h, state_lru_conv,
              cache_swa_k, cache_swa_v, cache_mem_k, cache_mem_v,
              ln_in_g, ln_in_b, w_in, gla_wa2, gla_ba, gla_norm_g,
              lru_conv_w, lru_conv_b, lru_wr, lru_br, lru_wi, lru_bi, lru_L,
              swa_sinks, sgu_ln_g, sgu_ln_b, sgu_w, sgu_b,
              w_mem_kv, w_branch, w_branch_mem, w_out, ln_g, ln_b):
    dt = x_prompt.dtype
    xp = layer_norm(x_prompt, ln_in_g, ln_in_b)
    xs = layer_norm(x_sample, ln_in_g, ln_in_b)
    gla0 = jnp.zeros((BATCH, GLA_HEADS, GLA_DK, GLA_DV), jnp.float32)
    h0 = jnp.zeros((BATCH, LRU_W), dt)
    conv0 = jnp.zeros((BATCH, CONV_W - 1, LRU_W), dt)
    kv0 = jnp.zeros((BATCH, WINDOW, SWA_KV_HEADS, HEAD_DIM), dt)
    st_p, st_s, mk_p, mv_p = [], [], [], []
    for l in range(DEPTH):
        lp = (w_in[l], gla_wa2[l], gla_ba[l], gla_norm_g[l], lru_conv_w[l], lru_conv_b[l],
              lru_wr[l], lru_br[l], lru_wi[l], lru_bi[l], lru_L[l], swa_sinks[l],
              sgu_ln_g[l], sgu_ln_b[l], sgu_w[l], sgu_b[l], w_branch[l], w_branch_mem[l],
              w_out[l], ln_g[l], ln_b[l])
        mkv = mem_prompt @ w_mem_kv[l]
        mk = mkv[..., :MEM_W].reshape(BATCH, N_MEM, MEM_HEADS, HEAD_DIM)
        mv = mkv[..., MEM_W:].reshape(BATCH, N_MEM, MEM_HEADS, HEAD_DIM)
        xp, sp = trunk_layer(xp, 0, gla0, h0, conv0, kv0, kv0, mk, mv, lp)
        xs, ss = trunk_layer(xs, PAST_LEN, state_gla[l], state_lru_h[l], state_lru_conv[l],
                             cache_swa_k[l], cache_swa_v[l], cache_mem_k[l], cache_mem_v[l], lp)
        st_p.append(sp)
        st_s.append(ss)
        mk_p.append(mk)
        mv_p.append(mv)
    P = [jnp.stack([s[i] for s in st_p]) for i in range(5)]
    S = [jnp.stack([s[i] for s in st_s]) for i in range(6)]
    mem_k_prompt = jnp.stack(mk_p)
    mem_v_prompt = jnp.stack(mv_p)
    return (xp, xs, P[0], S[0], P[1], S[1], P[2], S[2], P[3], S[3], P[4], S[4],
            mem_k_prompt, mem_v_prompt, S[5])


_drawn_inputs = setup_inputs


def setup_inputs(seed=0):
    import zlib

    import numpy as np

    out = dict(_drawn_inputs(seed))
    spreads = {}
    factors = {'cache_mem_k': 8.0,
     'cache_mem_v': 6.792,
     'gla_norm_g': 38.791,
     'lru_br': 8.0,
     'lru_bi': 7.327,
     'swa_sinks': 64.0,
     'sgu_ln_g': 8.194,
     'sgu_ln_b': 8.017,
     'sgu_b': 40.471,
     'w_branch_mem': 6.57}
    for name, (base, spread) in spreads.items():
        noise = np.random.default_rng([zlib.crc32(name.encode()), seed]).standard_normal(out[name].shape)
        drawn = base * np.exp(spread * noise) if base else spread * noise
        out[name] = __import__('jax').numpy.asarray(drawn.astype(out[name].dtype))
    for name, factor in factors.items():
        out[name] = (out[name] * factor).astype(out[name].dtype)
    return out
```

```python
from contextlib import ExitStack

import concourse.bass as bass
from concourse import mybir

F32 = mybir.dt.float32
F32R = mybir.dt.float32r
BF16 = mybir.dt.bfloat16
U32 = mybir.dt.uint32
ALU = mybir.AluOpType
ACT = mybir.ActivationFunctionType
AX_X = mybir.AxisListType.X

P = 128
D = 1024
SEQ = 1024
DEPTH = 2
NB = 8
NS = 8
NSAMP = NB * NS
T = SEQ + NSAMP
KD = D // P
NTT = SEQ // P
STEPS = NTT + 1
CHUNKS = [(0, 364), (364, 728), (728, T)]
NC = len(CHUNKS)
CW = CHUNKS[0][1]
N_MEM = 256
WINDOW = 128
LN_EPS = 1e-5
RMS_EPS = 1e-6
DN_ALPHA = (2 * DEPTH) ** 0.25
HEAD_SCALE = 64 ** -0.5
GLA_TAU = 16.0
NEG = -1.0e30
CLAMP = 80.0 * GLA_TAU

MEM, LRU, SWA, SGU, GLA = range(5)
IN_TILES = [2, 4, 6, 8, 8]
Y_TILES = [2, 4, 4, 4, 4]
GATE_OF = [4, 1, 2, 3, 0]
OUT_SLOT = [0, 0, 0, 0, 4]
LOADS = [2, 0, 6, 8, 7]
NBR = 5

PHASES = [("in", 0, 2), ("z", 0, 2), ("in", 1, 4)]
for _b in range(NBR):
    PHASES.append(("merge", _b, KD))
    if _b + 1 < NBR:
        PHASES.append(("z", _b + 1, Y_TILES[_b + 1]))
    if _b + 2 < NBR:
        PHASES.append(("in", _b + 2, IN_TILES[_b + 2]))
    if _b + 2 == GLA:
        PHASES.append(("rank", GLA, 1))
PHASES.append(("out", 0, KD))


def phase_table():
    table, w8, w4, ring = {}, 0, 0, 0
    units = {"in": 0, "z": 0, "merge": 0, "out": 0}
    for kind, b, n in PHASES:
        table[kind, b] = dict(w8=w8, w4=w4, ring=ring, n=n, **{f"u_{k}": v for k, v in units.items()})
        w8 += n
        ring += n
        if kind in ("merge", "rank"):
            w4 += n if kind == "merge" else 0
            ring += n
        units["in" if kind == "rank" else kind] += NC * n
    return table, w8, w4, ring, units


TABLE, N8, N4, NRING, UNITS = phase_table()
NG = NC * N8
ACT_FREES = UNITS["in"] + UNITS["merge"]
DVE_FREES = UNITS["z"] + UNITS["out"]
TH_UNITS = UNITS["z"] + UNITS["merge"]
P_UNITS = UNITS["merge"]

LEVELS = [(128, 63, True), (64, 31, True), (32, 15, False)]
NLEV = len(LEVELS)
QK = (NLEV + 1) * NTT + 2

LW_WR, LW_WI, LW_CW, LW_CB, LW_BR, LW_BI, LW_LAM, LW_H0, LW_CONV = 0, 128, 256, 260, 261, 262, 263, 264, 272
LW_N = LW_CONV + 3 * NB
NTAIL = 9 + 27


def build(nc, d):
    with ExitStack() as ctx:
        def sb(name, shape, dt=F32):
            return ctx.enter_context(nc.sbuf_tensor(name, shape, dt))

        def sem(name):
            return ctx.enter_context(nc.semaphore(name))

        xh = sb("xh", [P, KD, T], F32R)
        xl = sb("xl", [P, KD, T], BF16)
        yh = sb("yh", [P, 4, T], F32R)
        yl = sb("yl", [P, 4, T], BF16)
        merged = sb("merged", [P, KD, T])
        A = sb("arena", [P, 9, T])
        raw = sb("w_raw", [P, 2, D])
        wh = sb("w_hi", [P, 2, KD, P], F32R)
        wl = sb("w_lo", [P, 2, KD, P], F32R)
        wb = sb("w_bf", [P, 2, KD, P], BF16)
        ident = sb("ident", [P, P])
        ones = sb("ones", [P, P])
        th = sb("th", [P, 2, CW])
        tm = sb("tm", [P, CW])
        tm2 = sb("tm2", [P, CW])
        lnp = sb("lnp", [P, 2 * KD])
        WK = sb("mixer_space", [P, 6000])
        B = [ctx.enter_context(nc.psum_tensor(f"bank{i}", [P, 512], F32)) for i in range(8)]

        s_const = sem("const_loaded")
        s_ones = sem("ones_set")
        z_th = sem("z_tanh_ready")
        mem_cache = sem("mem_cache_loaded")
        raw_full = [sem(f"raw_full{s}") for s in range(2)]
        raw_free = sem("raw_free")
        split_full = sem("split_full")
        split_free = sem("split_free")
        g_full = sem("gate_bank_full")
        g_free_act = sem("gate_bank_free_act")
        g_free_dve = sem("gate_bank_free_dve")
        p_full = sem("branch_bank_full")
        p_free = sem("branch_bank_free")
        y_ready = sem("y_ready")
        x_ready = sem("x_ready")
        m_ready = sem("merged_split")
        x_loaded = sem("x_loaded")
        x_stored = sem("x_stored")
        res_loaded = sem("residual_loaded")
        lnp_loaded = sem("ln_params_loaded")
        ln_sum = sem("ln_sum")
        ln_mean = sem("ln_mean")
        ln_cent = sem("ln_centered")
        ln_sq = sem("ln_squares")
        ln_var = sem("ln_var")
        ln_rec = sem("ln_reciprocal")
        ln_rstd = sem("ln_rstd")
        ln_norm = sem("ln_normalised")
        ln_aff = sem("ln_affine")
        mkv_in = sem("mkv_inputs")
        mkv_ps = sem("mkv_product")
        mkv_sb = sem("mkv_copied")
        mkv_out = sem("mkv_stored")
        loaded = [sem(f"mixer{b}_loaded") for b in range(NBR)]
        stored = sem("states_stored")

        s_held = {e: sem(f"held_{e}") for e in ("pe", "dve", "pool")}

        def hold(eng, name):
            eng.sem_inc(s_held[name], 1)

        def carve():
            at = [0]

            def take(*dims):
                n = 1
                for x in dims:
                    n *= x
                ap = WK[:, at[0]:at[0] + n]
                at[0] += n
                assert at[0] <= 6000, at[0]
                if len(dims) == 2:
                    ap = ap.rearrange("p (a b) -> p a b", a=dims[0])
                if len(dims) == 3:
                    ap = ap.rearrange("p (a b c) -> p a b c", a=dims[0], b=dims[1])
                return ap
            return take

        def bc(ap, n):
            return ap.unsqueeze(1).broadcast_to([ap.shape[0], n, ap.shape[1]])

        def bl(ap, n):
            return ap.unsqueeze(2).broadcast_to([ap.shape[0], ap.shape[1], n])

        take = carve()
        m_q = take(2, P)
        m_pr = take(4, 256)
        m_pt = take(8, P)
        m_mx = take(4)
        m_sum = take(4)
        m_qbd = take(2, NB, 32)
        mem_q, mem_scores, mem_max, mem_exp, mem_prob, mem_pt, mem_pta, mem_ptd, mem_o = (
            sem(f"mem_{x}") for x in ("q_staged", "scores", "max", "exp", "prob", "pt", "pt_act", "pt_dve", "o"))

        take = carve()
        s_q = take(4, P)
        s_tq = take(4, P)
        s_k = take(2 * P)
        s_tk = take(P)
        s_v = take(P)
        s_vn = take(2, P)
        s_pr = take(4, 256)
        s_pt = take(8, P)
        s_mx = take(4)
        s_nm = take(4)
        s_es = take(4)
        s_sum = take(4)
        s_sink = take(8)
        s_sinkr = take(1)
        s_rot = take(P)
        s_mask = take(2 * P)
        s_smask = take(4, 192)
        s_qbd = take(NB, NSAMP)
        (swa_vst, swa_rot, swa_qk, swa_scores, swa_max, swa_exp, swa_prob, swa_pt, swa_pta, swa_ptd, swa_o,
         swa_cache, swa_old) = (
            sem(f"swa_{x}") for x in ("v_staged", "rotated", "qk", "scores", "max", "exp", "prob", "pt", "pt_act",
                                      "pt_dve", "o", "cache_loaded", "window_stored"))

        take = carve()
        l_w = take(LW_N)
        l_s4 = take(1)
        l_ns4 = take(1)
        l_h = take(2)
        l_t = take(8)
        l_one = take(1)
        l_pad = take(NB, 11)
        l_ab = take(NB, 9)
        l_ub = take(NB, 9)
        l_hb = take(NB, 9)
        l_tail = take(NTAIL)
        (lru_w, lru_e, lru_l, lru_conv, lru_r, lru_i, lru_ps, lru_act, lru_w2, lru_sq, lru_done, lru_tail) = (
            sem(f"lru_{x}") for x in ("params", "exp_lam", "decay", "conv", "r", "i", "gates_ps", "gates_act",
                                      "radicand", "root", "done", "tail_stored"))

        take = carve()
        g_v = take(4, P)
        g_vn = take(512)
        g_vs = take(512)
        g_bn = take(6)
        g_mv = take(2)
        g_rs = take(1)
        g_lng = take(512)
        g_lnb = take(512)
        g_w = take(4, P)
        g_b = take(4, P)
        g_ws = take(4, NSAMP)
        g_bs = take(4, NSAMP)
        g_m = take(P)
        g_ms = take(NSAMP)
        (sgu_vst, sgu_vt, sgu_var, sgu_rstd, sgu_vn, sgu_mix, sgu_done, sgu_stored) = (
            sem(f"sgu_{x}") for x in ("v_staged", "v_transposed", "var", "rstd", "v_normed", "mixed", "done",
                                      "v_stored"))

        take = carve()
        a_v = take(4, P)
        a_vn = take(512)
        a_x = take(2, P)
        a_e = take(2, P)
        a_b = take(2, P)
        a_dq = take(2, P)
        a_dk = take(2, P)
        a_q = take(2, P)
        a_k = take(2, P)
        a_kn = take(2, P)
        a_att = take(4, P)
        a_S = take(4, P)
        a_sq = a_v.rearrange("p a b -> p (a b)")
        a_rs = take(512)
        a_dec = take(16)
        a_wa = take(2 * P)
        a_ba = take(2)
        a_ng = take(1)
        a_one = take(P)
        a_mask = take(NLEV, P)
        a_smask = take(NSAMP)
        a_reset = take(NSAMP)
        a_hot = take(NB)
        (gla_vst, gla_x, gla_na, gla_e, gla_b, gla_d, gla_ex, gla_qk, gla_att, gla_attm, gla_o, gla_sqr, gla_ss,
         gla_rec, gla_rstd, gla_kh, gla_kt, gla_kn, gla_st, gla_s0, gla_s0up, gla_s0st, gla_km, gla_done,
         gla_stout, gla_sts, gla_os) = (
            sem(f"gla_{x}") for x in ("v_staged", "pre", "negabs", "softplus", "decay_sum", "exponents", "exps", "qk",
                                      "products", "att", "o", "squares", "sumsq", "rec", "rstd", "k_hat",
                                      "k_transposed", "k_natural", "state_ps", "state_loaded", "state_updated",
                                      "state_stored", "k_masked", "done", "prompt_state_stored", "sample_update",
                                      "sample_o"))

        take = carve()
        ln_m = take(NC, CW)
        ln_v = take(NC, CW)

        def swa_caches():
            return A[:, 6:8, :].rearrange("p a t -> p (a t)")[:, 0:NB * 2 * P].rearrange("p (b n) -> p b n", b=NB)

        def sample_states():
            return A[:, 0:4, :].rearrange("p a t -> p (a t)")[:, 0:NB * 4 * P].rearrange(
                "p (b h v) -> p b h v", b=NB, h=4)

        block = ctx.enter_context(nc.Block())

        def ring_items(kind, b, n):
            if kind == "merge":
                return n, (KD, Y_TILES[b])
            if kind == "rank":
                return 1, (KD, 0)
            return n // 2, (KD, KD)

        @block.sync
        def _(sp):
            with sp.Fori(0, DEPTH) as l:
                for kind, b, n in PHASES:
                    t = TABLE[kind, b]
                    pairs, subs = ring_items(kind, b, n)
                    per = 2 if kind in ("in", "z", "out") else 1
                    with sp.Fori(0, pairs) as i:
                        for s in range(2):
                            sp.wait_ge(raw_free, NRING * l + t["ring"] + 2 * i + s + 1)
                            if kind == "merge" and s == 1:
                                src = d["w4"][bass.ds(N4 * l + t["w4"] + i, 1), :, 0:subs[1] * P]
                            else:
                                m = max(subs[s] * P, 16)
                                src = d["w8"][bass.ds(N8 * l + t["w8"] + per * i + (s if per == 2 else 0), 1), :, 0:m]
                            w = src.shape[2]
                            sp.dma_start(raw[:, s, 0:w], src.rearrange("o p n -> p (o n)")).then_inc(raw_full[s], 16)

        @block.gpsimd
        def _(g):
            g.memset(ones[:, :], 1.0).then_inc(s_ones, 1)
            g.sem_inc(raw_free, 2)
            with g.Fori(0, DEPTH) as l:
                for kind, b, n in PHASES:
                    t = TABLE[kind, b]
                    pairs, subs = ring_items(kind, b, n)
                    with g.Fori(0, pairs) as i:
                        for s in range(2):
                            m = subs[s]
                            g.wait_ge(raw_full[s], 16 * (NRING // 2 * l + t["ring"] // 2 + i + 1))
                            g.wait_ge(split_free, NRING * l + t["ring"] + 2 * i + s + 1)
                            hold(g, "pool")
                            if m:
                                r = raw[:, s, 0:m * P]
                                h = wh[:, s, 0:m, :].rearrange("p k n -> p (k n)")
                                lo = wl[:, s, 0:m, :].rearrange("p k n -> p (k n)")
                                bf = wb[:, s, 0:m, :].rearrange("p k n -> p (k n)")
                                g.tensor_scalar(h, r, 1.0, 1.0, ALU.mult, ALU.mult)
                                g.tensor_scalar(bf, r, 1.0, 1.0, ALU.mult, ALU.mult)
                                g.drain()
                                g.tensor_tensor(lo, r, h.bitcast(F32), ALU.subtract)
                            g.drain()
                            g.sem_inc(split_full, 1)
                            g.sem_inc(raw_free, 1)

        @block.tensor
        def _(pe):
            mm = pe.matmul

            def product(bank, s, nk, c, hi, lo):
                a, z = CHUNKS[c]
                out = bank[:, 0:z - a]
                for k in range(nk):
                    mm(out, wh[:, s, k, :], hi[:, k, a:z], start=(k == 0), stop=False)
                for k in range(nk):
                    mm(out, wl[:, s, k, :], hi[:, k, a:z], start=False, stop=False)
                for k in range(nk):
                    last = mm(out, wb[:, s, k, :], lo[:, k, a:z], start=False, stop=(k == nk - 1))
                return last

            def dense(l, kind, b, free, per, base, ready=None):
                t = TABLE[kind, b]
                other = (g_free_dve, DVE_FREES, t["u_z"] + t["u_out"]) if free is g_free_act else \
                    (g_free_act, ACT_FREES, t["u_in"] + t["u_merge"])
                pe.wait_ge(other[0], other[1] * l + other[2] + 3)
                hold(pe, "pe")
                with pe.Fori(0, t["n"] // 2) as i:
                    for s in range(2):
                        pe.wait_ge(split_full, NRING * l + t["ring"] + 2 * i + s + 1)
                        for c in range(NC):
                            pe.wait_ge(free, per * l + base + 2 * NC * i + NC * s + c + 1)
                            last = product(B[c], s, KD, c, xh, xl)
                            last.then_inc(g_full, 1)
                        pe.drain()
                        pe.sem_inc(split_free, 1)

            def merge_start(l, b):
                t = TABLE["merge", b]
                pe.wait_ge(g_free_dve, DVE_FREES * l + t["u_z"] + t["u_out"] + 3)
                pe.wait_ge(y_ready, UNITS["z"] * l + t["u_z"] + 2)
                hold(pe, "pe")

            def merge_unit(l, b, j, c):
                t = TABLE["merge", b]
                q = t["u_merge"] + NC * j
                if c == 0:
                    pe.wait_ge(split_full, NRING * l + t["ring"] + 2 * j + 1)
                pe.wait_ge(g_free_act, ACT_FREES * l + t["u_in"] + q + c + 1)
                product(B[c], 0, KD, c, xh, xl).then_inc(g_full, 1)
                if c == NC - 1:
                    pe.drain()
                    pe.sem_inc(split_free, 1)
                if c == 0:
                    pe.wait_ge(split_full, NRING * l + t["ring"] + 2 * j + 2)
                pe.wait_ge(p_free, P_UNITS * l + q + (2, 1, 3)[c])
                product(B[3 + c % 2], 1, Y_TILES[b], c, yh, yl).then_inc(p_full, 1)
                if c == NC - 1:
                    pe.drain()
                    pe.sem_inc(split_free, 1)

            def layer_norm(n):
                bank = (3, 4, 5)
                for c, (a, z) in enumerate(CHUNKS):
                    for j in range(KD):
                        last = mm(B[bank[c]][:, 0:z - a], ones[:, :], merged[:, j, a:z], start=(j == 0), stop=(j == KD - 1))
                    last.then_inc(ln_sum, 1)
                for c, (a, z) in enumerate(CHUNKS):
                    pe.wait_ge(ln_sq, NC * n + c + 1)
                    for j in range(KD):
                        last = mm(B[(6, 7, 3)[c]][:, 0:z - a], ones[:, :], A[:, j, a:z], start=(j == 0), stop=(j == KD - 1))
                    last.then_inc(ln_var, 1)

            def memory_products():
                W = A[:, 0:4, :].rearrange("p a t -> p (a t)")[:, 0:4096].rearrange("p (k n) -> p k n", k=KD)
                M = A[:, 4:6, :].rearrange("p a t -> p (a t)")[:, 0:2048].rearrange("p (k s) -> p k s", k=KD)
                for l in range(DEPTH):
                    pe.wait_ge(mkv_in, 16 * (l + 2))
                    if l:
                        pe.wait_ge(mkv_sb, l)
                    for p in range(2):
                        for k in range(KD):
                            mm(B[5][:, 256 * p:256 * p + 256], W[:, k, P * p:P * p + P], M[:, k, :],
                               start=(k == 0), stop=(k == KD - 1))
                    for p in range(2):
                        for k in range(KD):
                            last = mm(B[6][:, 256 * p:256 * p + 256], M[:, k, P * p:P * p + P], W[:, k, 256:512],
                                      start=(k == 0), stop=(k == KD - 1))
                    last.then_inc(mkv_ps, 1)

            def mem_step(l, i, fill):
                n = 10 * l + i + 1
                pe.wait_ge(mem_q, n)
                for h in range(4):
                    p, e = h // 2, h % 2
                    last = mm(B[5 + e][:, 256 * p:256 * p + 256], m_q[64 * e:64 * e + 64, p, :],
                              A[64 * e:64 * e + 64, 6, 256 * p:256 * p + 256], start=True, stop=True)
                last.then_inc(mem_scores, 1)
                fill(0)
                pe.wait_ge(mem_prob, n)
                for m in range(4):
                    for st in range(2):
                        last = pe.transpose(B[5 + m // 2][:, (m % 2 * 2 + st) * P:(m % 2 * 2 + st + 1) * P],
                                            m_pr[:, m, st * P:st * P + P], ident[:, :])
                last.then_inc(mem_pt, 1)
                fill(1)
                pe.wait_ge(mem_pta, NTT * l + i + 1)
                pe.wait_ge(mem_ptd, n)
                for m in range(4):
                    e, p = m // 2, m % 2
                    for st in range(2):
                        last = mm(B[7][64 * e:64 * e + 64, P * p:P * p + P],
                                  A[:, 6, 512 + 256 * st + 64 * (2 * p + e):512 + 256 * st + 64 * (2 * p + e) + 64],
                                  m_pt[:, 2 * m + st, :], start=(st == 0), stop=(st == 1))
                last.then_inc(mem_o, 1)
                fill(2)

            def mem_samples(l, g):
                n = 10 * l + NTT + g + 1
                if g:
                    pe.wait_ge(mem_cache, 16 * (l + 1))
                pe.wait_ge(mem_q, n)
                for b in range(4):
                    for p in range(2):
                        last = mm(B[5][32 * b:32 * b + 32, 0:256], m_qbd[:, p, 4 * g + b, :],
                                  A[:, 2 + b, 256 * p:256 * p + 256], start=(p == 0), stop=(p == 1))
                last.then_inc(mem_scores, 1)
                pe.wait_ge(mem_prob, n)
                for st in range(2):
                    last = pe.transpose(B[6][:, st * P:st * P + P], m_pr[:, 0, st * P:st * P + P], ident[:, :])
                last.then_inc(mem_pt, 1)
                pe.wait_ge(mem_ptd, n)
                for b in range(4):
                    for p in range(2):
                        for st in range(2):
                            last = mm(B[7][:, P * p + 32 * b:P * p + 32 * b + 32],
                                      A[:, 2 + b, 512 + 256 * st + P * p:512 + 256 * st + P * p + P],
                                      m_pt[:, st, 32 * b:32 * b + 32], start=(st == 0), stop=(st == 1))
                last.then_inc(mem_o, 1)

            def lru_step(l, ct, fill):
                n = 4 * l + ct + 1
                pe.wait_ge(lru_conv, n)
                for c, (a, z) in enumerate(CHUNKS):
                    if c:
                        pe.wait_ge(lru_act, 3 * 4 * l + 3 * ct + c)
                    mm(B[5][:, 0:z - a], l_w[:, LW_WR:LW_WR + P], A[:, 4, a:z], start=True, stop=True)
                    mm(B[6][:, 0:z - a], l_w[:, LW_WI:LW_WI + P], A[:, 4, a:z], start=True, stop=True)\
                        .then_inc(lru_ps, 1)
                    fill(c)

            def swa_step(l, i, fill):
                n = STEPS * l + i + 1
                pe.wait_ge(swa_vst, n)
                mm(B[5][:, :], s_rot[:, :], A[:, 0:4, bass.ds(P * i, P)], start=True, stop=True)
                mm(B[6][:, 0:P], s_rot[:, :], A[:, 4, bass.ds(P * i, P)], start=True, stop=True)
                pe.transpose(B[6][:, P:2 * P], s_v[:, :], ident[:, :]).then_inc(swa_rot, 1)
                fill(0)
                pe.wait_ge(swa_qk, n)
                for r in range(2):
                    for m in range(2):
                        for e in range(2):
                            last = mm(B[5 + e][:, 256 * m:256 * m + 256], s_q[64 * e:64 * e + 64, 2 * r + m, :],
                                      s_k[64 * e:64 * e + 64, :], start=True, stop=True)
                    last.then_inc(swa_scores, 1)
                    fill(1 + r)
                    pe.wait_ge(swa_prob, (2 * STEPS - 1) * l + 2 * i + r + 1)
                    for m in range(4):
                        for st in range(2):
                            last = pe.transpose(B[5 + m // 2][:, (m % 2 * 2 + st) * P:(m % 2 * 2 + st + 1) * P],
                                                s_pr[:, m, st * P:st * P + P], ident[:, :])
                    last.then_inc(swa_pt, 1)
                    fill(3 + r)
                    pe.wait_ge(swa_pta, (2 * STEPS - 1) * l + 2 * i + r + 1)
                    pe.wait_ge(swa_ptd, (2 * STEPS - 1) * l + 2 * i + r + 1)
                    for m in range(4):
                        e, q = m // 2, m % 2
                        for st in range(2):
                            last = mm(B[7][64 * e:64 * e + 64, P * q:P * q + P], s_vn[:, st, 64 * e:64 * e + 64],
                                      s_pt[:, 2 * m + st, :], start=(st == 0), stop=(st == 1))
                    last.then_inc(swa_o, 1)

            def swa_samples(l):
                n = STEPS * l + STEPS
                pe.wait_ge(swa_vst, n)
                mm(B[5][:, 0:4 * NSAMP], s_rot[:, :], A[:, 0:4, SEQ:T], start=True, stop=True)
                mm(B[6][:, 0:NSAMP], s_rot[:, :], A[:, 4, SEQ:T], start=True, stop=True)
                pe.transpose(B[6][0:NSAMP, P:2 * P], s_v[:, 0:NSAMP], ident[:, :]).then_inc(swa_rot, 1)
                pe.wait_ge(swa_qk, n)
                pe.wait_ge(swa_cache, 16 * (l + 1))
                C = swa_caches()
                for u in range(4):
                    o = 256 * (u % 2)
                    for e in range(2):
                        b = 2 * u + e
                        mm(B[5 + u // 2][64 * e:64 * e + 64, o:o + P], s_qbd[:, b, :], C[:, b, 0:P],
                           start=True, stop=True)
                    last = mm(B[5 + u // 2][:, o + P:o + P + NSAMP],
                              s_qbd[:, 2 * u:2 * u + 2, :].rearrange("p b h -> p (b h)"), s_k[:, 0:NSAMP],
                              start=True, stop=True)
                last.then_inc(swa_scores, 1)
                m = (2 * STEPS - 1) * (l + 1)
                pe.wait_ge(swa_prob, m)
                for u in range(4):
                    pe.transpose(B[5][:, P * u:P * u + P], s_pr[:, u, 0:P], ident[:, :])
                for u in range(4):
                    last = pe.transpose(B[6][0:NSAMP, P * u:P * u + P], s_pr[:, u, P:P + NSAMP], ident[:, :])
                last.then_inc(swa_pt, 1)
                pe.wait_ge(swa_pta, m)
                pe.wait_ge(swa_ptd, m)
                for b in range(NB):
                    u, e = b // 2, b % 2
                    mm(B[7][:, 64 * b:64 * b + 64], C[:, b, P:2 * P], s_pt[:, u, 64 * e:64 * e + 64],
                       start=True, stop=False)
                    last = mm(B[7][:, 64 * b:64 * b + 64], s_vn[0:NSAMP, 1, :], s_pt[0:NSAMP, 4 + u, 64 * e:64 * e + 64],
                              start=False, stop=True)
                last.then_inc(swa_o, 1)

            def sgu_step(l, i, fill):
                n = STEPS * l + i + 1
                pe.wait_ge(sgu_vst, n)
                for j in range(4):
                    last = pe.transpose(B[5][:, P * j:P * j + P], g_v[:, j, :], ident[:, :])
                last.then_inc(sgu_vt, 1)
                fill(0)
                pe.wait_ge(sgu_vn, n)
                for j in range(4):
                    last = mm(B[6][:, P * j:P * j + P], g_vn[:, P * j:P * j + P], g_w[:, j, :], start=True, stop=True)
                last.then_inc(sgu_mix, 1)
                fill(1)
                fill(2)

            def sgu_samples(l):
                n = STEPS * l + STEPS
                pe.wait_ge(sgu_vst, n)
                hold(pe, "pe")
                for j in range(4):
                    last = pe.transpose(B[5][0:NSAMP, P * j:P * j + P], g_v[:, j, 0:NSAMP], ident[:, :])
                last.then_inc(sgu_vt, 1)
                pe.wait_ge(sgu_vn, n)
                for j in range(4):
                    last = mm(B[6][:, NSAMP * j:NSAMP * j + NSAMP], g_vn[0:NSAMP, P * j:P * j + P],
                              g_ws[0:NSAMP, j, :], start=True, stop=True)
                last.then_inc(sgu_mix, 1)

            def gla_rank(l):
                t = TABLE["rank", GLA]
                pe.wait_ge(split_full, NRING * l + t["ring"] + 1)
                for c in range(NC):
                    pe.wait_ge(g_free_act, ACT_FREES * l + t["u_in"] + t["u_merge"] + c + 1)
                    product(B[c], 0, KD, c, xh, xl).then_inc(g_full, 1)
                pe.drain()
                pe.wait_ge(split_full, NRING * l + t["ring"] + 2)
                pe.sem_inc(split_free, 2)

            def gla_core(l, i, n, w, tok, levels, fill, samples):
                pe.wait_ge(gla_vst, n)
                for p in range(2):
                    mm(B[5][:, P * p:P * p + w], a_wa[0:16, P * p:P * p + P],
                       A[0:16, 8, bass.ds(tok, w)], start=True, stop=True)
                for j in range(4):
                    last = pe.transpose(B[6][0:w, P * j:P * j + P], a_v[:, j, 0:w], ident[:, :])
                last.then_inc(gla_x, 1)
                fill(0)
                for v in range(levels):
                    pe.wait_ge(gla_qk, QK * l + (NLEV + 1) * i + v + 1)
                    hold(pe, "pe")
                    for p in range(2):
                        for e in range(2):
                            last = mm(B[5 + e][0:w, P * p:P * p + w], a_k[64 * e:64 * e + 64, p, 0:w],
                                      a_q[64 * e:64 * e + 64, p, 0:w], start=True, stop=True)
                    last.then_inc(gla_att, 1)
                    fill(1 + v)

            def gla_step(l, i, fill):
                n = STEPS * l + i + 1
                gla_core(l, i, n, P, P * i, NLEV, fill, False)
                pe.wait_ge(gla_qk, QK * l + (NLEV + 1) * i + NLEV + 1)
                for h in range(4):
                    p, e = h // 2, h % 2
                    mm(B[7][:, P * h:P * h + P], a_vn[:, P * h:P * h + P], a_att[:, 2 * e + p, :], start=True, stop=False)
                    last = mm(B[7][:, P * h:P * h + P], a_S[:, h, :], a_q[:, p, :], start=False, stop=True)
                last.then_inc(gla_o, 1)
                pe.wait_ge(gla_kh, n)
                hold(pe, "pe")
                for p in range(2):
                    last = pe.transpose(B[5][:, P * p:P * p + P], a_k[:, p, :], ident[:, :])
                last.then_inc(gla_kt, 1)
                fill(4)
                pe.wait_ge(gla_sqr, n)
                mm(B[6][:, :], ones[:, :], a_sq[:, :], start=True, stop=True).then_inc(gla_ss, 1)
                pe.wait_ge(gla_kn, n)
                for p in range(2):
                    last = mm(B[5][:, 256 * p:256 * p + 256], a_kn[:, p, :], a_vn[:, 256 * p:256 * p + 256],
                              start=True, stop=True)
                last.then_inc(gla_st, 1)
                fill(5)

            def gla_samples(l):
                n = STEPS * l + STEPS
                w = NSAMP
                gla_core(l, NTT, n, w, SEQ, 1, lambda c: None, True)
                pe.wait_ge(gla_qk, QK * (l + 1))
                for h in range(4):
                    p, e = h // 2, h % 2
                    mm(B[7][:, P * h:P * h + w], a_vn[0:w, P * h:P * h + P], a_att[0:w, 2 * e + p, 0:w],
                       start=True, stop=True)
                pe.wait_ge(gla_kh, n)
                hold(pe, "pe")
                for p in range(2):
                    last = pe.transpose(B[5][0:w, P * p:P * p + P], a_k[:, p, 0:w], ident[:, :])
                last.then_inc(gla_kt, 1)
                pe.wait_ge(gla_s0, 16 * (l + 1))
                S0 = sample_states()
                for b in range(NB):
                    pe.wait_ge(gla_km, NB * l + b + 1)
                    for h in range(4):
                        mm(B[6][:, P * h + NS * b:P * h + NS * b + NS], S0[:, b, h, :],
                           a_q[:, h // 2, NS * b:NS * b + NS], start=True, stop=True)
                    for p in range(2):
                        last = mm(B[5][:, 256 * p:256 * p + 256], a_dq[0:w, p, :], a_vn[0:w, 256 * p:256 * p + 256],
                                  start=True, stop=True)
                    last.then_inc(gla_sts, 1)
                pe.wait_ge(gla_sqr, n)
                for h in range(4):
                    last = mm(B[6][:, P * h:P * h + w], ones[:, :], a_sq[:, P * h:P * h + w], start=True, stop=True)
                last.then_inc(gla_ss, 1)

            def fills(l, b, j, at):
                def fill(c):
                    if c in at:
                        merge_unit(l, b, j, at.index(c))
                return fill

            pe.sem_inc(split_free, 2)
            pe.wait_ge(s_const, 16)
            pe.wait_ge(s_ones, 1)
            memory_products()
            pe.wait_ge(mkv_sb, DEPTH)
            pe.wait_ge(x_loaded, 16)
            layer_norm(0)
            with pe.Fori(0, DEPTH) as l:
                pe.wait_ge(x_ready, l + 1)
                dense(l, "in", MEM, g_free_act, ACT_FREES, 0)
                pe.wait_ge(loaded[MEM], 32 * (l + 1))
                hold(pe, "pe")
                with pe.Fori(0, NTT) as i:
                    mem_step(l, i, lambda c: None)
                for g in range(2):
                    mem_samples(l, g)
                t = TABLE["z", MEM]
                dense(l, "z", MEM, g_free_dve, DVE_FREES, t["u_z"])
                dense(l, "in", LRU, g_free_act, ACT_FREES, TABLE["in", LRU]["u_in"] + TABLE["in", LRU]["u_merge"])
                for b in range(NBR):
                    merge_start(l, b)
                    if b + 1 == LRU:
                        with pe.Fori(0, 4) as i:
                            for c in range(NC):
                                merge_unit(l, b, 2 * i, c)
                            lru_step(l, i, fills(l, b, 2 * i + 1, [0, 1, 2]))
                    if b + 1 == SWA:
                        swa_step(l, 0, fills(l, b, 0, [0, 1, 3]))
                        with pe.Fori(1, NTT) as i:
                            swa_step(l, i, fills(l, b, i, [0, 1, 3]))
                        swa_samples(l)
                    if b + 1 == SGU:
                        with pe.Fori(0, NTT) as i:
                            sgu_step(l, i, fills(l, b, i, [0, 1, 2]))
                        sgu_samples(l)
                    if b + 1 == GLA:
                        with pe.Fori(0, NTT) as i:
                            gla_step(l, i, fills(l, b, i, [0, 2, 4]))
                        gla_samples(l)
                    if b + 1 == NBR:
                        with pe.Fori(0, KD) as i:
                            for c in range(NC):
                                merge_unit(l, b, i, c)
                    if b + 1 < NBR:
                        dense(l, "z", b + 1, g_free_dve, DVE_FREES, TABLE["z", b + 1]["u_z"])
                    if b + 2 < NBR:
                        t = TABLE["in", b + 2]
                        dense(l, "in", b + 2, g_free_act, ACT_FREES, t["u_in"] + t["u_merge"])
                    if b + 2 == GLA:
                        gla_rank(l)
                pe.wait_ge(m_ready, l + 1)
                dense(l, "out", 0, g_free_dve, DVE_FREES, TABLE["out", 0]["u_z"])
                pe.wait_ge(g_free_dve, DVE_FREES * (l + 1) + 3)
                layer_norm(l + 1)

        @block.scalar
        def _(act):
            a_ = act.activation

            def load(dst, src, s):
                act.dma_start(dst, src).then_inc(s, 16)

            def layer(src, l):
                names = "abcd"[:len(src.shape) - 2]
                return src[bass.ds(l, 1)].rearrange(f"o p {' '.join(names)} -> p (o {names[0]}) {' '.join(names[1:])}")

            def evac(l, kind, b, n):
                t = TABLE[kind, b]

                def tile(item, slot):
                    for c, (a, z) in enumerate(CHUNKS):
                        act.wait_ge(g_full, NG * l + NC * (t["w8"] + item) + c + 1)
                        dst = A[:, slot, a:z] if isinstance(slot, int) else \
                            A[:, bass.ds(slot, 1), a:z].rearrange("p o t -> p (o t)")
                        a_(dst, B[c][:, 0:z - a], ACT.Copy).then_inc(g_free_act, 1)
                if kind == "rank":
                    tile(0, 8)
                    return
                with act.Fori(0, n // 2) as i:
                    for s in range(2):
                        tile(2 * i + s, 2 * i + s)

            def z_tanh(l, b):
                t = TABLE["z", b]
                act.wait_ge(p_free, P_UNITS * l + t["u_merge"] + 2)
                with act.Fori(0, t["n"] // 2) as i:
                    for s in range(2):
                        for c, (a, z) in enumerate(CHUNKS):
                            q = t["u_z"] + 2 * NC * i + NC * s
                            act.wait_ge(g_full, NG * l + NC * (t["w8"] + 2 * i + s) + c + 1)
                            act.wait_ge(y_ready, UNITS["z"] * l + q + (2, 1, 3)[c])
                            a_(th[:, c % 2, 0:z - a], B[c][:, 0:z - a], ACT.Tanh, scale=0.5).then_inc(z_th, 1)

            def merge_start(l, b):
                act.wait_ge(y_ready, UNITS["z"] * l + TABLE["merge", b]["u_z"] + 2)

            def merge_unit(l, b, j, c):
                t = TABLE["merge", b]
                a, z = CHUNKS[c]
                act.wait_ge(g_full, NG * l + NC * (t["w8"] + j) + c + 1)
                act.wait_ge(p_free, P_UNITS * l + t["u_merge"] + NC * j + (2, 1, 3)[c])
                a_(th[:, c % 2, 0:z - a], B[c][:, 0:z - a], ACT.Tanh, scale=0.5).then_inc(g_free_act, 1)

            def fills(l, b, j, at):
                def fill(c):
                    if c in at:
                        merge_unit(l, b, j, at.index(c))
                return fill

            def layer_norm(n):
                for c, (a, z) in enumerate(CHUNKS):
                    act.wait_ge(ln_sum, NC * n + c + 1)
                    a_(ln_m[:, c, 0:z - a], B[3 + c][:, 0:z - a], ACT.Copy, scale=1.0 / D).then_inc(ln_mean, 1)
                for c, (a, z) in enumerate(CHUNKS):
                    act.wait_ge(ln_cent, NC * n + c + 1)
                    a_(A[:, 0:KD, a:z], merged[:, :, a:z], ACT.Square).then_inc(ln_sq, 1)
                for c, (a, z) in enumerate(CHUNKS):
                    act.wait_ge(ln_rec, NC * n + c + 1)
                    a_(ln_v[:, c, 0:z - a], ln_v[:, c, 0:z - a], ACT.Sqrt).then_inc(ln_rstd, 1)
                act.wait_ge(lnp_loaded, 16 * (n + 1))
                for c, (a, z) in enumerate(CHUNKS):
                    act.wait_ge(ln_norm, NC * n + c + 1)
                    for j in range(KD):
                        last = a_(merged[:, j, a:z], merged[:, j, a:z], ACT.Identity,
                                  scale=lnp[:, j:j + 1], bias=lnp[:, KD + j:KD + j + 1])
                    last.then_inc(ln_aff, 1)
                act.wait_ge(ln_aff, NC * (n + 1))
                act.dma_start(d["y"], merged[:, :, :]).then_inc(x_stored, 16)

            def mem_step(l, i, fill):
                n = 10 * l + i + 1
                act.wait_ge(mem_max, n)
                for m in range(4):
                    last = a_(m_pr[:, m, :], B[5 + m // 2][:, 256 * (m % 2):256 * (m % 2) + 256], ACT.Exp,
                              bias=m_mx[:, m:m + 1], scale=HEAD_SCALE, accum_out=m_sum[:, m:m + 1])
                last.then_inc(mem_exp, 1)
                act.wait_ge(mem_pt, n)
                a_(m_pt[:, 0:4, :].rearrange("p a b -> p (a b)"), B[5][:, :], ACT.Copy).then_inc(mem_pta, 1)

            def mem_samples(l, g):
                n = 10 * l + NTT + g + 1
                act.wait_ge(mem_max, n)
                a_(m_pr[:, 0, :], B[5][:, 0:256], ACT.Exp, bias=m_mx[:, 0:1], scale=HEAD_SCALE,
                   accum_out=m_sum[:, 0:1]).then_inc(mem_exp, 1)
                act.wait_ge(mem_o, n)
                if g == 0:
                    act.dma_start(A[:, 2:6, 0:1024], d["memkv"][bass.ds(NB * l + 4, 4)].rearrange("b p n -> p b n"))\
                        .then_inc(mem_cache, 16)

            def lru_params(l, ct):
                load(l_w[:, :], d["lru"][bass.ds(4 * l + ct, 1)].rearrange("o p n -> p (o n)"), lru_w)

            def lru_step(l, ct, fill):
                n = 4 * l + ct + 1
                act.wait_ge(lru_e, n)
                a_(l_t[:, 1:2], l_t[:, 0:1], ACT.Exp).then_inc(lru_l, 1)
                act.wait_ge(lru_i, n)
                for c, (a, z) in enumerate(CHUNKS):
                    act.wait_ge(lru_ps, 3 * (n - 1) + c + 1)
                    a_(A[:, 5, a:z], B[5][:, 0:z - a], ACT.Tanh, scale=0.5, bias=l_h[:, 0:1])
                    a_(A[:, 6, a:z], B[6][:, 0:z - a], ACT.Tanh, scale=0.5, bias=l_h[:, 1:2]).then_inc(lru_act, 1)
                    fill(c)
                act.drain()
                a_(A[:, 8, :], A[:, 5, :], ACT.Exp, scale=l_s4[:, 0:1], bias=l_s4[:, 0:1])
                a_(A[:, 7, :], A[:, 5, :], ACT.Tanh, scale=l_ns4[:, 0:1], bias=l_ns4[:, 0:1]).then_inc(lru_r, 1)
                act.wait_ge(lru_w2, n)
                a_(A[:, 7, :], A[:, 7, :], ACT.Sqrt).then_inc(lru_sq, 1)
                act.wait_ge(lru_done, n)
                act.dma_start(d["lru_tail"][bass.ds(n - 1, 1)].rearrange("o p n -> p (o n)"), l_tail[:, :])\
                    .then_inc(lru_tail, 16)
                act.wait_ge(lru_tail, 16 * n)

            def swa_softmax(l, n, r, w, tiles):
                act.wait_ge(swa_max, r)
                for m in range(4):
                    a_(s_pr[:, m, 0:w], s_pr[:, m, 0:w], ACT.Exp, bias=s_nm[:, m:m + 1], scale=HEAD_SCALE,
                       accum_out=s_sum[:, m:m + 1])
                a_(s_es[:, :], s_es[:, :], ACT.Exp).then_inc(swa_exp, 1)

            def swa_step(l, i, fill):
                n = STEPS * l + i + 1
                fill(0)
                for r in range(2):
                    m = (2 * STEPS - 1) * l + 2 * i + r + 1
                    swa_softmax(l, n, m, 256, 4)
                    fill(1 + r)
                    act.wait_ge(swa_pt, m)
                    a_(s_pt[:, 0:4, :].rearrange("p a b -> p (a b)"), B[5][:, :], ACT.Copy).then_inc(swa_pta, 1)
                    fill(3 + r)

            def swa_samples(l):
                n = STEPS * l + STEPS
                act.wait_ge(swa_qk, n)
                load(swa_caches(), d["swakv"][bass.ds(l, 1)].rearrange("o p b n -> p (o b) n"), swa_cache)
                out = d["swa_new"][bass.ds(l, 1)].rearrange("o p n -> p (o n)")
                act.dma_start(out[:, 0:P], s_k[:, P:2 * P]).then_inc(stored, 16)
                act.dma_start(out[:, P:2 * P], A[:, 5, SEQ - P:SEQ]).then_inc(stored, 16)
                act.dma_start(out[:, 2 * P:2 * P + NSAMP], s_k[:, 0:NSAMP]).then_inc(stored, 16)
                act.dma_start(out[:, 2 * P + NSAMP:2 * P + 2 * NSAMP], A[:, 5, SEQ:T]).then_inc(stored, 16)
                m = (2 * STEPS - 1) * (l + 1)
                swa_softmax(l, n, m, 192, 4)
                act.wait_ge(swa_pt, m)
                a_(s_pt[:, 0:4, :].rearrange("p a b -> p (a b)"), B[5][:, :], ACT.Copy).then_inc(swa_pta, 1)

            def sgu_step(l, i, fill, w=P):
                n = STEPS * l + i + 1
                fill(0)
                act.wait_ge(sgu_var, n)
                a_(g_rs[0:w, :], g_rs[0:w, :], ACT.Sqrt).then_inc(sgu_rstd, 1)
                fill(1)
                fill(2)

            def gla_decays(n, w):
                act.wait_ge(gla_na, n)
                a_(a_e[:, :, 0:w], a_e[:, :, 0:w], ACT.Exp)
                act.drain()
                a_(a_e[:, :, 0:w], a_e[:, :, 0:w], ACT.Ln, bias=1.0).then_inc(gla_e, 1)

            def gla_exps(l, i, v, w, last_level):
                act.wait_ge(gla_d, QK * l + (NLEV + 1) * i + v + 1)
                a_(a_dq[:, :, 0:w], a_dq[:, :, 0:w], ACT.Exp, scale=1.0 / GLA_TAU)
                op = a_(a_dk[:, :, 0:w], a_dk[:, :, 0:w], ACT.Exp, scale=1.0 / GLA_TAU)
                if last_level:
                    op = a_(a_dec[:, :], a_dec[:, :], ACT.Exp, scale=1.0 / GLA_TAU)
                op.then_inc(gla_ex, 1)

            def gla_step(l, i, fill):
                n = STEPS * l + i + 1
                gla_decays(n, P)
                fill(0)
                for v in range(NLEV + 1):
                    gla_exps(l, i, v, P, v == NLEV)
                    if v < NLEV:
                        fill(1 + v)
                act.wait_ge(gla_o, NTT * l + i + 1)
                a_(a_sq[:, :], B[7][:, :], ACT.Square).then_inc(gla_sqr, 1)
                fill(4)
                act.wait_ge(gla_rec, n)
                a_(a_rs[:, :], a_rs[:, :], ACT.Sqrt).then_inc(gla_rstd, 1)
                fill(5)

            def gla_samples(l):
                n = STEPS * l + STEPS
                w = NSAMP
                gla_decays(n, w)
                act.dma_start(d["gla_p"][bass.ds(l, 1)].rearrange("o p h v -> p (o h) v"), a_S[:, :, :])\
                    .then_inc(stored, 16)
                gla_exps(l, NTT, 0, w, False)
                gla_exps(l, NTT, 1, w, True)
                act.wait_ge(gla_kh, n)
                load(sample_states(), d["gla_s0"][bass.ds(l, 1)].rearrange("o p b h v -> p (o b) h v"), gla_s0)
                act.wait_ge(gla_os, l + 1)
                a_(a_sq[:, :].rearrange("p (h t) -> p h t", h=4)[:, :, 0:w],
                   a_vn[:, :].rearrange("p (h t) -> p h t", h=4)[:, :, 0:w], ACT.Square).then_inc(gla_sqr, 1)
                act.dma_start(d["gla_s"][bass.ds(l, 1)].rearrange("o p b h v -> p (o b) h v"), sample_states())\
                    .then_inc(gla_s0st, 16)
                act.wait_ge(gla_rec, n)
                a_(a_rs[:, :], a_rs[:, :], ACT.Sqrt).then_inc(gla_rstd, 1)

            def mixer_loads(l, b):
                if b == SWA:
                    load(A[:, 6:8, :], d["rope"], loaded[b])
                    load(s_rot[:, :], d["rot"], loaded[b])
                    load(s_mask[:, :], d["swa_mask"], loaded[b])
                    load(s_smask[:, :, :], d["swa_smask"], loaded[b])
                    load(s_sink[:, :], layer(d["sink"], l), loaded[b])
                    load(s_sinkr[:, :], layer(d["sinkr"], l), loaded[b])
                if b == SGU:
                    act.wait_ge(stored, 16 * (5 * l + 4))
                    load(g_lng[:, :], d["sgu_g"][bass.ds(l, 1), :].broadcast_to([P, 512]), loaded[b])
                    load(g_lnb[:, :], d["sgu_b"][bass.ds(l, 1), :].broadcast_to([P, 512]), loaded[b])
                    load(g_w[:, :, :], d["sgu_w"][bass.ds(l, 1)].rearrange("o p g t -> p (o g) t"), loaded[b])
                    load(g_ws[0:NSAMP, :, :], d["sgu_ws"][bass.ds(l, 1)].rearrange("o p g t -> p (o g) t"), loaded[b])
                    load(g_b[:, :, :], d["sgu_bs"][bass.ds(l, 1)].broadcast_to([P, 4, P]), loaded[b])
                    load(g_bs[:, :, :], d["sgu_bss"][bass.ds(l, 1)].broadcast_to([P, 4, NSAMP]), loaded[b])
                    load(g_m[:, :], d["tril"], loaded[b])
                    load(g_ms[0:NSAMP, :], d["tril8"], loaded[b])
                if b == GLA:
                    act.wait_ge(sgu_stored, 16 * (l + 1))
                    load(a_wa[0:16, :], d["wa2"][bass.ds(l, 1)].rearrange("o p n -> p (o n)"), loaded[b])
                    load(a_ba[:, :], layer(d["ba"], l), loaded[b])
                    load(a_ng[:, :], layer(d["ng"], l), loaded[b])
                    load(a_mask[:, :, :], d["gla_mask"], loaded[b])
                    load(a_smask[0:NSAMP, :], d["tril8"], loaded[b])
                    load(a_reset[:, :], d["reset"], loaded[b])
                    load(a_hot[0:NSAMP, :], d["hot"], loaded[b])

            act.sem_inc(g_free_act, 3)
            load(ident[:, :], d["ident"], s_const)
            load(A[:, 4:6, :].rearrange("p a t -> p (a t)")[:, 0:2048], d["mem"], mkv_in)
            load(A[:, 0:4, :].rearrange("p a t -> p (a t)")[:, 0:4096], d["w_mem"][0], mkv_in)
            load(merged[:, :, :], d["x"], x_loaded)
            load(lnp[:, :], d["lnp"][0], lnp_loaded)
            act.dma_start(d["swa_old_k"], d["cache_k"][:, :, NS:, :]).then_inc(swa_old, 16)
            act.dma_start(d["swa_old_v"], d["cache_v"][:, :, NS:, :]).then_inc(swa_old, 16)
            for l in range(DEPTH):
                act.wait_ge(mkv_ps, l + 1)
                if l:
                    act.wait_ge(mkv_out, 16 * l)
                else:
                    load(A[:, 0:4, :].rearrange("p a t -> p (a t)")[:, 0:4096], d["w_mem"][1], mkv_in)
                a_(A[:, 6, 0:512], B[5][:, :], ACT.Copy)
                a_(A[:, 6, 512:1024], B[6][:, :], ACT.Copy).then_inc(mkv_sb, 1)
                act.wait_ge(mkv_sb, l + 1)
                act.dma_start(d["mkv"][l], A[:, 6, 0:1024]).then_inc(mkv_out, 16)
            act.wait_ge(mkv_out, 16 * DEPTH)
            layer_norm(0)
            with act.Fori(0, DEPTH) as l:
                act.wait_ge(ln_var, NC * (l + 1))
                act.wait_ge(x_ready, l + 1)
                load(lnp[:, :], d["lnp"][bass.ds(l + 1, 1)].rearrange("o p n -> p (o n)"), lnp_loaded)
                load(A[:, 6, 0:1024], d["mkv"][bass.ds(l, 1)].rearrange("o p n -> p (o n)"), loaded[MEM])
                load(A[:, 2:6, 0:1024], d["memkv"][bass.ds(NB * l, 4)].rearrange("b p n -> p b n"), loaded[MEM])
                evac(l, "in", MEM, 2)
                with act.Fori(0, NTT) as i:
                    mem_step(l, i, lambda c: None)
                for g in range(2):
                    mem_samples(l, g)
                z_tanh(l, MEM)
                act.wait_ge(y_ready, UNITS["z"] * l + TABLE["in", LRU]["u_z"] + 2)
                evac(l, "in", LRU, IN_TILES[LRU])
                for b in range(NBR):
                    merge_start(l, b)
                    if b + 1 == LRU:
                        with act.Fori(0, 4) as i:
                            lru_params(l, i)
                            for c in range(NC):
                                merge_unit(l, b, 2 * i, c)
                            lru_step(l, i, fills(l, b, 2 * i + 1, [0, 1, 2]))
                    if b + 1 == SWA:
                        swa_step(l, 0, fills(l, b, 0, [0, 1, 3]))
                        with act.Fori(1, NTT) as i:
                            swa_step(l, i, fills(l, b, i, [0, 1, 3]))
                        swa_samples(l)
                    if b + 1 == SGU:
                        with act.Fori(0, NTT) as i:
                            sgu_step(l, i, fills(l, b, i, [0, 1, 2]))
                        sgu_step(l, NTT, lambda c: None, NSAMP)
                        act.wait_ge(sgu_vn, STEPS * (l + 1))
                        act.dma_start(d["sgu_v"][bass.ds(l, 1)].rearrange("o p n -> p (o n)"), g_vn[0:NSAMP, :])\
                            .then_inc(sgu_stored, 16)
                    if b + 1 == GLA:
                        with act.Fori(0, NTT) as i:
                            gla_step(l, i, fills(l, b, i, [0, 2, 4]))
                        gla_samples(l)
                    if b + 1 == NBR:
                        with act.Fori(0, KD) as i:
                            for c in range(NC):
                                merge_unit(l, b, i, c)
                    if b + 1 < NBR:
                        z_tanh(l, b + 1)
                        act.wait_ge(y_ready, UNITS["z"] * l + TABLE["z", b + 1]["u_z"] + NC * Y_TILES[b + 1] + 2)
                    if b + 2 < NBR:
                        mixer_loads(l, b + 2)
                        evac(l, "in", b + 2, IN_TILES[b + 2])
                    if b + 2 == GLA:
                        evac(l, "rank", GLA, 1)
                    if b + 1 == GLA:
                        act.wait_ge(gla_s0st, 16 * (l + 1))
                        act.wait_ge(stored, 16 * 5 * (l + 1))
                        act.wait_ge(x_stored, 16 * (l + 1))
                        load(A[:, 0:KD, :], d["y"], res_loaded)
                layer_norm(l + 1)
            act.wait_ge(x_stored, 16 * (DEPTH + 1))
            act.wait_ge(stored, 16 * 5 * DEPTH)
            act.wait_ge(gla_s0st, 16 * DEPTH)
            act.wait_ge(sgu_stored, 16 * DEPTH)
            act.wait_ge(lru_tail, 16 * 4 * DEPTH)
            act.wait_ge(mkv_out, 16 * DEPTH)
            act.wait_ge(swa_old, 32)

        @block.vector
        def _(v):
            tt, ts, stt, cp = v.tensor_tensor, v.tensor_scalar, v.scalar_tensor_tensor, v.tensor_copy

            def inputs_ready(l, kind, b):
                t = TABLE[kind, b]
                v.wait_ge(g_free_act, ACT_FREES * l + t["u_in"] + t["u_merge"] + NC * t["n"] + 3)
                hold(v, "dve")

            def z_phase(l, b):
                t = TABLE["z", b]

                def tile(item, slot):
                    for c, (a, z) in enumerate(CHUNKS):
                        w = z - a
                        o = A[:, bass.ds(OUT_SLOT[b] + slot, 1), a:z].rearrange("p o t -> p (o t)")
                        hi = yh[:, bass.ds(slot, 1), a:z].rearrange("p o t -> p (o t)")
                        lo = yl[:, bass.ds(slot, 1), a:z].rearrange("p o t -> p (o t)")
                        v.wait_ge(z_th, UNITS["z"] * l + t["u_z"] + NC * item + c + 1)
                        stt(tm[:, 0:w], th[:, c % 2, 0:w], 1.0, B[c][:, 0:w], ALU.add, ALU.mult)\
                            .then_inc(g_free_dve, 1)
                        v.drain()
                        stt(tm2[:, 0:w], tm[:, 0:w], 0.5, o, ALU.mult, ALU.mult)
                        v.drain()
                        cp(hi, tm2[:, 0:w])
                        v.drain()
                        tt(lo, tm2[:, 0:w], hi.bitcast(F32), ALU.subtract).then_inc(y_ready, 1)
                        v.drain()
                with v.Fori(0, t["n"] // 2) as i:
                    for s in range(2):
                        tile(2 * i + s, 2 * i + s)

            def merge_unit(l, b, j, c):
                t = TABLE["merge", b]
                a, z = CHUNKS[c]
                w = z - a
                q = NC * j + c
                m = merged[:, bass.ds(j, 1), a:z].rearrange("p o t -> p (o t)")
                v.wait_ge(g_free_act, ACT_FREES * l + t["u_in"] + t["u_merge"] + q + 4)
                v.wait_ge(p_full, P_UNITS * l + t["u_merge"] + q + 1)
                pb = B[3 + c % 2][:, 0:w]
                if b == MEM:
                    stt(m, th[:, c % 2, 0:w], 1.0, pb, ALU.add, ALU.mult).then_inc(p_free, 1)
                else:
                    stt(tm[:, 0:w], th[:, c % 2, 0:w], 1.0, pb, ALU.add, ALU.mult).then_inc(p_free, 1)
                    v.drain()
                    tt(m, m, tm[:, 0:w], ALU.add)
                    v.drain()

            def fills(l, b, j, at):
                def fill(c):
                    if c in at:
                        merge_unit(l, b, j, at.index(c))
                return fill

            def layer_norm(n):
                for c, (a, z) in enumerate(CHUNKS):
                    v.wait_ge(ln_mean, NC * n + c + 1)
                    tt(merged[:, :, a:z], merged[:, :, a:z], bc(ln_m[:, c, 0:z - a], KD), ALU.subtract)\
                        .then_inc(ln_cent, 1)
                for c, (a, z) in enumerate(CHUNKS):
                    v.wait_ge(ln_var, NC * n + c + 1)
                    ts(ln_v[:, c, 0:z - a], B[(6, 7, 3)[c]][:, 0:z - a], 1.0 / D, LN_EPS, ALU.mult, ALU.add)
                    v.drain()
                    v.reciprocal(ln_v[:, c, 0:z - a], ln_v[:, c, 0:z - a]).then_inc(ln_rec, 1)
                for c, (a, z) in enumerate(CHUNKS):
                    v.wait_ge(ln_rstd, NC * n + c + 1)
                    tt(merged[:, :, a:z], merged[:, :, a:z], bc(ln_v[:, c, 0:z - a], KD), ALU.mult)\
                        .then_inc(ln_norm, 1)
                for c, (a, z) in enumerate(CHUNKS):
                    v.wait_ge(ln_aff, NC * n + c + 1)
                    cp(xh[:, :, a:z], merged[:, :, a:z])
                    v.drain()
                    last = tt(xl[:, :, a:z], merged[:, :, a:z], xh[:, :, a:z].bitcast(F32), ALU.subtract)
                last.then_inc(x_ready, 1)

            def mem_step(l, i, fill):
                n = 10 * l + i + 1
                tok = bass.ds(P * i, P)
                cp(m_q[:, :, :], A[:, 0:2, tok]).then_inc(mem_q, 1)
                v.wait_ge(mem_scores, n)
                for e in range(2):
                    v.tensor_reduce(m_mx[:, 2 * e:2 * e + 2], B[5 + e][:, :].rearrange("p (m s) -> p m s", m=2), AX_X,
                                    ALU.max)
                v.drain()
                ts(m_mx[:, :], m_mx[:, :], -HEAD_SCALE, None, ALU.mult).then_inc(mem_max, 1)
                v.wait_ge(mem_exp, n)
                v.reciprocal(m_sum[:, :], m_sum[:, :])
                v.drain()
                tt(m_pr[:, :, :], m_pr[:, :, :], bl(m_sum[:, :], 256), ALU.mult).then_inc(mem_prob, 1)
                v.wait_ge(mem_pt, n)
                cp(m_pt[:, 4:8, :].rearrange("p a b -> p (a b)"), B[6][:, :]).then_inc(mem_ptd, 1)
                v.wait_ge(mem_o, n)
                hold(v, "dve")
                cp(A[:, 0:2, tok], B[7][:, 0:256].rearrange("p (m t) -> p m t", m=2))
                v.drain()

            def mem_samples(l, g):
                n = 10 * l + NTT + g + 1
                if g == 0:
                    for p in range(2):
                        for e in range(2):
                            r = slice(64 * e, 64 * e + 64)
                            h = 2 * p + e
                            last = cp(m_qbd[r, p, :, NS * h:NS * h + NS],
                                      A[r, p, SEQ:T].rearrange("p (b t) -> p b t", b=NB))
                    last.then_inc(mem_q, 1)
                else:
                    v.sem_inc(mem_q, 1)
                v.wait_ge(mem_scores, n)
                v.reduce_max(m_mx[:, 0:1], B[5][:, 0:256], AX_X)
                v.drain()
                ts(m_mx[:, 0:1], m_mx[:, 0:1], -HEAD_SCALE, None, ALU.mult).then_inc(mem_max, 1)
                v.wait_ge(mem_exp, n)
                v.reciprocal(m_sum[:, 0:1], m_sum[:, 0:1])
                v.drain()
                ts(m_pr[:, 0, :], m_pr[:, 0, :], m_sum[:, 0:1], None, ALU.mult).then_inc(mem_prob, 1)
                v.wait_ge(mem_pt, n)
                cp(m_pt[:, 0:2, :].rearrange("p a b -> p (a b)"), B[6][:, 0:256]).then_inc(mem_ptd, 1)
                v.wait_ge(mem_o, n)
                hold(v, "dve")
                for p in range(2):
                    for e in range(2):
                        r = slice(64 * e, 64 * e + 64)
                        h = 2 * p + e
                        cp(A[r, p, SEQ + 32 * g:SEQ + 32 * g + 32].rearrange("p (b t) -> p b t", b=4),
                           B[7][r, P * p:P * p + P].rearrange("p (b h t) -> p b h t", b=4, h=4)[:, :, h, :])
                v.drain()

            def lru_step(l, ct, fill):
                n = 4 * l + ct + 1
                X = A[:, bass.ds(ct, 1), :].rearrange("p o t -> p (o t)")
                xc = A[:, 4, :]
                col = lambda k: l_w[:, k:k + 1]
                v.wait_ge(lru_w, 16 * n)
                stt(l_t[:, 0:1], col(LW_LAM), -1.0, col(LW_LAM), ALU.mult, ALU.min).then_inc(lru_e, 1)
                ts(xc[:, 0:SEQ], X[:, 0:SEQ], col(LW_CW + 3), col(LW_CB), ALU.mult, ALU.add)
                cp(l_pad[:, :, 0:3], l_w[:, LW_CONV:LW_CONV + 3 * NB].rearrange("p (b j) -> p b j", b=NB))
                cp(l_pad[:, :, 3:11], X[:, SEQ:T].rearrange("p (b t) -> p b t", b=NB))
                cp(l_tail[:, 9:12], X[:, SEQ - 3:SEQ])
                cp(l_tail[:, 12:36].rearrange("p (b j) -> p b j", b=NB),
                   X[:, SEQ:T].rearrange("p (b t) -> p b t", b=NB)[:, :, NS - 3:NS])
                xs = xc[:, SEQ:T].rearrange("p (b t) -> p b t", b=NB)
                v.drain()
                ts(xs, l_pad[:, :, 3:11], col(LW_CW + 3), col(LW_CB), ALU.mult, ALU.add)
                for j in (2, 1, 0):
                    k = 3 - j
                    v.drain()
                    stt(xc[:, k:SEQ], X[:, 0:SEQ - k], col(LW_CW + j), xc[:, k:SEQ], ALU.mult, ALU.add)
                    last = stt(xs, l_pad[:, :, j:j + NS], col(LW_CW + j), xs, ALU.mult, ALU.add)
                last.then_inc(lru_conv, 1)
                v.wait_ge(lru_l, n)
                ts(l_t[:, 2:3], l_t[:, 1:2], 2.0, None, ALU.add)
                ts(l_h[:, :], l_w[:, LW_BR:LW_BR + 2], 0.5, None, ALU.mult)
                v.drain()
                v.reciprocal(l_t[:, 2:3], l_t[:, 2:3])
                v.drain()
                tt(l_t[:, 3:4], l_t[:, 1:2], l_t[:, 2:3], ALU.mult)
                v.drain()
                tt(l_t[:, 4:5], l_t[:, 3:4], l_t[:, 3:4], ALU.mult)
                v.drain()
                ts(l_t[:, 5:6], l_t[:, 4:5], 1.0 / 17, 1.0 / 15, ALU.mult, ALU.add)
                for k in (13, 11, 9, 7, 5, 3, 1):
                    v.drain()
                    ts(l_t[:, 5:6], l_t[:, 5:6], l_t[:, 4:5], None, ALU.mult)
                    v.drain()
                    ts(l_t[:, 5:6], l_t[:, 5:6], 1.0 / k, None, ALU.add)
                v.drain()
                stt(l_t[:, 6:7], l_t[:, 3:4], 2.0, l_t[:, 5:6], ALU.mult, ALU.mult)
                v.drain()
                stt(l_t[:, 7:8], col(LW_LAM), 0.0, l_t[:, 6:7], ALU.min, ALU.subtract)
                v.drain()
                ts(l_s4[:, :], l_t[:, 7:8], 4.0, None, ALU.mult)
                ts(l_ns4[:, :], l_t[:, 7:8], -4.0, None, ALU.mult).then_inc(lru_i, 1)
                for c in range(NC):
                    fill(c)
                v.wait_ge(lru_r, n)
                tt(A[:, 5, :], A[:, 8, :], A[:, 8, :], ALU.mult)
                v.drain()
                stt(A[:, 7, :], A[:, 5, :], 1.0, A[:, 7, :], ALU.add, ALU.mult).then_inc(lru_w2, 1)
                stt(A[:, 6, :], A[:, 6, :], 1.0, xc, ALU.add, ALU.mult)
                cp(l_ab[:, :, 1:9], A[:, 8, SEQ:T].rearrange("p (b t) -> p b t", b=NB))
                v.memset(l_ab[:, :, 0:1], 0.0)
                cp(l_ub[:, :, 0:1], l_w[:, LW_H0:LW_H0 + NB].rearrange("p (b o) -> p b o", o=1))
                v.drain()
                v.wait_ge(lru_sq, n)
                stt(A[:, 7, :], A[:, 6, :], 0.5, A[:, 7, :], ALU.mult, ALU.mult)
                v.drain()
                cp(l_ub[:, :, 1:9], A[:, 7, SEQ:T].rearrange("p (b t) -> p b t", b=NB))
                v.tensor_tensor_scan(X[:, 0:SEQ], A[:, 8, 0:SEQ], A[:, 7, 0:SEQ], 0.0, ALU.mult, ALU.add)
                v.drain()
                v.tensor_tensor_scan(l_hb[:, :, :].rearrange("p b t -> p (b t)"), l_ab[:, :, :].rearrange("p b t -> p (b t)"),
                                     l_ub[:, :, :].rearrange("p b t -> p (b t)"), 0.0, ALU.mult, ALU.add)
                v.drain()
                cp(X[:, SEQ:T].rearrange("p (b t) -> p b t", b=NB), l_hb[:, :, 1:9])
                cp(l_tail[:, 0:1], X[:, SEQ - 1:SEQ])
                cp(l_tail[:, 1:9].rearrange("p (b o) -> p b o", o=1), l_hb[:, :, 8:9]).then_inc(lru_done, 1)
                v.drain()

            def swa_rotate(l, n, tok, w):
                kk = s_k[:, P:2 * P] if w == P else s_k[:, 0:w]
                C = A[:, 6, tok]
                S = A[:, 7, tok]
                v.wait_ge(swa_rot, n)
                tt(s_q[:, :, 0:w], A[:, 0:4, tok], bc(C, 4), ALU.mult)
                tt(s_tq[:, :, 0:w], B[5][:, 0:4 * w].rearrange("p (m t) -> p m t", m=4), bc(S, 4), ALU.mult)
                tt(kk, A[:, 4, tok], C, ALU.mult)
                tt(s_tk[:, 0:w], B[6][:, 0:w], S, ALU.mult)
                cp(s_vn[0:w, 1, :], B[6][0:w, P:2 * P])
                v.drain()
                tt(s_q[:, :, 0:w], s_q[:, :, 0:w], s_tq[:, :, 0:w], ALU.add)
                last = tt(kk, kk, s_tk[:, 0:w], ALU.add)
                if w == P:
                    last.then_inc(swa_qk, 1)
                    return
                v.drain()
                for e in range(2):
                    r = slice(64 * e, 64 * e + 64)
                    last = cp(s_qbd[r, :, 32 * e:32 * e + 32].rearrange("p b (i t) -> p b i t", i=4),
                              s_q[r, :, 0:w].rearrange("p i (b t) -> p b i t", b=NB))
                last.then_inc(swa_qk, 1)

            def swa_softmax(m, w, sink):
                v.drain()
                v.tensor_reduce(s_mx[:, :], s_pr[:, :, 0:w], AX_X, ALU.max)
                v.drain()
                stt(s_mx[:, :], s_mx[:, :], HEAD_SCALE, sink, ALU.mult, ALU.max)
                v.drain()
                ts(s_nm[:, :], s_mx[:, :], -1.0, None, ALU.mult)
                tt(s_es[:, :], sink, s_mx[:, :], ALU.subtract).then_inc(swa_max, 1)
                v.wait_ge(swa_exp, m)
                tt(s_sum[:, :], s_sum[:, :], s_es[:, :], ALU.add)
                v.drain()
                v.reciprocal(s_sum[:, :], s_sum[:, :])
                v.drain()
                tt(s_pr[:, :, 0:w], s_pr[:, :, 0:w], bl(s_sum[:, :], w), ALU.mult).then_inc(swa_prob, 1)

            def swa_step(l, i, fill):
                n = STEPS * l + i + 1
                first = isinstance(i, int)
                tok = bass.ds(P * i, P)
                if first:
                    v.memset(s_vn[:, 0, :], 0.0)
                    v.memset(s_k[:, 0:P], 0.0)
                else:
                    cp(s_vn[:, 0, :], s_vn[:, 1, :])
                    cp(s_k[:, 0:P], s_k[:, P:2 * P])
                cp(s_v[:, :], A[:, 5, tok]).then_inc(swa_vst, 1)
                v.drain()
                swa_rotate(l, n, tok, P)
                fill(0)
                for r in range(2):
                    m = (2 * STEPS - 1) * l + 2 * i + r + 1
                    v.wait_ge(swa_scores, m)
                    for e in range(2):
                        sc = B[5 + e][:, :].rearrange("p (m s) -> p m s", m=2)
                        if first:
                            v.memset(s_pr[:, 2 * e:2 * e + 2, 0:P], NEG)
                            tt(s_pr[:, 2 * e:2 * e + 2, P:2 * P], sc[:, :, P:2 * P], bc(s_mask[:, P:2 * P], 2), ALU.add)
                        else:
                            tt(s_pr[:, 2 * e:2 * e + 2, :], sc, bc(s_mask[:, :], 2), ALU.add)
                    swa_softmax(m, 2 * P, s_sink[:, 4 * r:4 * r + 4])
                    fill(1 + r)
                    v.wait_ge(swa_pt, m)
                    cp(s_pt[:, 4:8, :].rearrange("p a b -> p (a b)"), B[6][:, :]).then_inc(swa_ptd, 1)
                    fill(3 + r)
                    v.wait_ge(swa_o, m)
                    hold(v, "dve")
                    cp(A[:, 2 * r:2 * r + 2, tok], B[7][:, 0:2 * P].rearrange("p (m t) -> p m t", m=2))
                    v.drain()

            def swa_samples(l):
                n = STEPS * (l + 1)
                m = (2 * STEPS - 1) * (l + 1)
                w = NSAMP
                cp(s_v[:, 0:w], A[:, 5, SEQ:T])
                v.memset(s_qbd[:, :, :], 0.0).then_inc(swa_vst, 1)
                v.drain()
                swa_rotate(l, n, slice(SEQ, T), w)
                v.wait_ge(swa_scores, m)
                for g in range(2):
                    tt(s_pr[:, 2 * g:2 * g + 2, 0:192], B[5 + g][:, :].rearrange("p (u s) -> p u s", u=2)[:, :, 0:192],
                       s_smask[:, 2 * g:2 * g + 2, :], ALU.add)
                swa_softmax(m, 192, s_sinkr[:, 0:1].broadcast_to([P, 4]))
                v.wait_ge(swa_pt, m)
                cp(s_pt[0:w, 4:8, :].rearrange("p a b -> p (a b)"), B[6][0:w, :]).then_inc(swa_ptd, 1)
                v.wait_ge(swa_o, m)
                for e in range(2):
                    r = slice(64 * e, 64 * e + 64)
                    cp(A[r, 0:4, SEQ:T].rearrange("p i (b t) -> p b i t", b=NB),
                       B[7][r, :].rearrange("p (b h t) -> p b h t", b=NB, h=8)[:, :, 4 * e:4 * e + 4, :])
                v.drain()

            def sgu_step(l, i, fill, w=P):
                n = STEPS * l + i + 1
                tok = bass.ds(P * i, w)
                cp(g_v[:, :, 0:w], A[:, 4:8, tok]).then_inc(sgu_vst, 1)
                fill(0)
                v.wait_ge(sgu_vt, n)
                v.bn_stats(g_bn[0:w, :], B[5][0:w, :])
                v.drain()
                v.bn_aggr(g_mv[0:w, :], g_bn[0:w, :])
                v.drain()
                ts(g_rs[0:w, :], g_mv[0:w, 1:2], LN_EPS, None, ALU.add)
                v.drain()
                v.reciprocal(g_rs[0:w, :], g_rs[0:w, :]).then_inc(sgu_var, 1)
                v.wait_ge(sgu_rstd, n)
                ts(g_vn[0:w, :], B[5][0:w, :], g_mv[0:w, 0:1], g_rs[0:w, :], ALU.subtract, ALU.mult)
                v.drain()
                tt(g_vn[0:w, :], g_vn[0:w, :], g_lng[0:w, :], ALU.mult)
                v.drain()
                tt(g_vn[0:w, :], g_vn[0:w, :], g_lnb[0:w, :], ALU.add).then_inc(sgu_vn, 1)
                fill(1)
                v.wait_ge(sgu_mix, n)
                vs = g_vs[:, 0:4 * w].rearrange("p (g t) -> p g t", g=4)
                tt(vs, B[6][:, 0:4 * w].rearrange("p (g t) -> p g t", g=4), g_b[:, :, :] if w == P else g_bs[:, :, :],
                   ALU.add)
                v.drain()
                tt(A[:, 0:4, tok], A[:, 0:4, tok], vs, ALU.mult)
                v.drain()
                fill(2)

            def ref(w, block, pos):
                s = a_b[:, :, 0:w].rearrange("p h (m t) -> p h m t", t=block)
                return s[:, :, :, pos:pos + 1].broadcast_to([P, 2, w // block, block])

            def blocks(ap, w, block):
                return ap[:, :, 0:w].rearrange("p h (m t) -> p h m t", t=block)

            def gla_core(l, i, n, w, tok, levels, one, mask, fill):
                heads = lambda e: B[5 + e][0:w, 0:2 * P].rearrange("p (h t) -> p h t", h=2)[:, :, 0:w]
                cp(a_v[:, :, 0:w], A[:, 4:8, tok]).then_inc(gla_vst, 1)
                v.wait_ge(gla_x, n)
                for p in range(2):
                    ts(a_x[:, p, 0:w], B[5][:, P * p:P * p + w], a_ba[:, p:p + 1], None, ALU.add)
                cp(a_vn[0:w, :], B[6][0:w, :])
                v.drain()
                stt(a_e[:, :, 0:w], a_x[:, :, 0:w], -1.0, a_x[:, :, 0:w], ALU.mult, ALU.min).then_inc(gla_na, 1)
                fill(0)
                v.wait_ge(gla_e, n)
                stt(a_x[:, :, 0:w], a_x[:, :, 0:w], 0.0, a_e[:, :, 0:w], ALU.min, ALU.subtract)
                v.drain()
                for p in range(2):
                    v.tensor_tensor_scan(a_b[:, p, 0:w], one, a_x[:, p, 0:w], 0.0, ALU.mult, ALU.add)
                v.drain()
                for k, (block, pos, _) in enumerate(levels):
                    at = QK * l + (NLEV + 1) * i + k + 1
                    tt(blocks(a_dq, w, block), blocks(a_b, w, block), ref(w, block, pos), ALU.subtract)
                    v.drain()
                    ts(a_dk[:, :, 0:w], a_dq[:, :, 0:w], -1.0, CLAMP, ALU.mult, ALU.min)
                    v.drain()
                    ts(a_dq[:, :, 0:w], a_dq[:, :, 0:w], CLAMP, None, ALU.min).then_inc(gla_d, 1)
                    v.wait_ge(gla_ex, at)
                    stt(a_q[:, :, 0:w], A[:, 0:2, tok], HEAD_SCALE, a_dq[:, :, 0:w], ALU.mult, ALU.mult)
                    tt(a_k[:, :, 0:w], A[:, 2:4, tok], a_dk[:, :, 0:w], ALU.mult).then_inc(gla_qk, 1)
                    fill(1 + k)
                    v.wait_ge(gla_att, (QK - NTT - 1) * l + NLEV * i + k + 1)
                    hold(v, "dve")
                    for e in range(2):
                        v.copy_predicated(a_att[0:w, 2 * e:2 * e + 2, 0:w], bc(mask(k), 2).bitcast(U32), heads(e))
                block = P if w == P else NS
                cp(a_dq[:, :, 0:w], a_b[:, :, 0:w])
                tt(blocks(a_dk, w, block), ref(w, block, block - 1), blocks(a_b, w, block), ALU.subtract)
                m = w // block
                cp(a_dec[:, 0:2 * m].rearrange("p (h m o) -> p h m o", h=2, o=1),
                   blocks(a_b, w, block)[:, :, :, block - 1:block]).then_inc(gla_d, 1)
                v.wait_ge(gla_ex, QK * l + (NLEV + 1) * i + len(levels) + 1)
                stt(a_q[:, :, 0:w], A[:, 0:2, tok], HEAD_SCALE, a_dq[:, :, 0:w], ALU.mult, ALU.mult)\
                    .then_inc(gla_qk, 1)
                tt(a_k[:, :, 0:w], A[:, 2:4, tok], a_dk[:, :, 0:w], ALU.mult).then_inc(gla_kh, 1)
                v.wait_ge(gla_kt, n)
                cp(a_kn[0:w, :, :], B[5][0:w, 0:2 * P].rearrange("p (h k) -> p h k", h=2)).then_inc(gla_kn, 1)

            def gla_step(l, i, fill):
                n = STEPS * l + i + 1
                tok = bass.ds(P * i, P)
                gla_core(l, i, n, P, tok, LEVELS, a_one[:, :], lambda k: a_mask[:, k, :], fill)
                fill(4)
                v.wait_ge(gla_ss, n)
                ts(a_rs[:, :], B[6][:, :], 1.0 / P, RMS_EPS, ALU.mult, ALU.add)
                v.drain()
                v.reciprocal(a_rs[:, :], a_rs[:, :]).then_inc(gla_rec, 1)
                v.wait_ge(gla_rstd, n)
                stt(A[:, 4:8, tok], B[7][:, :].rearrange("p (h t) -> p h t", h=4), a_ng[:, 0:1],
                    a_rs[:, :].rearrange("p (h t) -> p h t", h=4), ALU.mult, ALU.mult)
                v.wait_ge(gla_st, NTT * l + i + 1)
                for h in range(4):
                    p, e = h // 2, h % 2
                    r = slice(64 * e, 64 * e + 64)
                    stt(a_S[r, h, :], a_S[r, h, :], a_dec[r, p:p + 1],
                        B[5][r, 256 * p + P * e:256 * p + P * e + P], ALU.mult, ALU.add)
                v.drain()
                fill(5)

            def gla_samples(l):
                n = STEPS * l + STEPS
                w = NSAMP
                tok = slice(SEQ, T)
                v.memset(a_att[:, :, :], 0.0)
                v.drain()
                gla_core(l, NTT, n, w, tok, [(NS, NS // 2 - 1, False)], a_reset[:, :], lambda k: a_smask[0:w, :],
                         lambda c: None)
                v.drain()
                v.wait_ge(gla_s0, 16 * (l + 1))
                S0 = sample_states()
                for b in range(NB):
                    ts(a_dq[0:w, :, :], a_kn[0:w, :, :], a_hot[0:w, b:b + 1], None, ALU.mult).then_inc(gla_km, 1)
                    v.wait_ge(gla_sts, NB * l + b + 1)
                    for h in range(4):
                        p, e = h // 2, h % 2
                        r = slice(64 * e, 64 * e + 64)
                        stt(S0[r, b, h, :], S0[r, b, h, :], a_dec[r, NB * p + b:NB * p + b + 1],
                            B[5][r, 256 * p + P * e:256 * p + P * e + P], ALU.mult, ALU.add)
                four = lambda ap: ap.rearrange("p (h t) -> p h t", h=4)[:, :, 0:w]
                cp(four(a_rs[:, :]), four(B[6][:, :]))
                v.drain()
                tt(four(a_vn[:, :]), four(B[7][:, :]), four(a_rs[:, :]), ALU.add).then_inc(gla_os, 1)
                v.wait_ge(gla_ss, n)
                ts(four(a_rs[:, :]), four(B[6][:, :]), 1.0 / P, RMS_EPS, ALU.mult, ALU.add)
                v.drain()
                v.reciprocal(four(a_rs[:, :]), four(a_rs[:, :])).then_inc(gla_rec, 1)
                v.wait_ge(gla_rstd, n)
                stt(A[:, 4:8, tok], four(a_vn[:, :]), a_ng[:, 0:1], four(a_rs[:, :]), ALU.mult, ALU.mult)
                v.drain()

            v.sem_inc(g_free_dve, 3)
            v.sem_inc(p_free, 2)
            v.sem_inc(y_ready, 2)
            layer_norm(0)
            with v.Fori(0, DEPTH) as l:
                v.memset(m_qbd[:, :, :, :], 0.0)
                v.drain()
                inputs_ready(l, "in", MEM)
                with v.Fori(0, NTT) as i:
                    mem_step(l, i, lambda c: None)
                for g in range(2):
                    mem_samples(l, g)
                z_phase(l, MEM)
                inputs_ready(l, "in", LRU)
                v.wait_ge(x_stored, 16 * (l + 1))
                hold(v, "dve")
                for b in range(NBR):
                    if b + 1 == LRU:
                        with v.Fori(0, 4) as i:
                            for c in range(NC):
                                merge_unit(l, b, 2 * i, c)
                            lru_step(l, i, fills(l, b, 2 * i + 1, [0, 1, 2]))
                    if b + 1 == SWA:
                        swa_step(l, 0, fills(l, b, 0, [0, 1, 3]))
                        with v.Fori(1, NTT) as i:
                            swa_step(l, i, fills(l, b, i, [0, 1, 3]))
                        swa_samples(l)
                    if b + 1 == SGU:
                        tt(g_w[:, :, :], g_w[:, :, :], bc(g_m[:, :], 4), ALU.mult)
                        tt(g_ws[0:NSAMP, :, :], g_ws[0:NSAMP, :, :], bc(g_ms[0:NSAMP, :], 4), ALU.mult)
                        v.drain()
                        with v.Fori(0, NTT) as i:
                            sgu_step(l, i, fills(l, b, i, [0, 1, 2]))
                        sgu_step(l, NTT, lambda c: None, NSAMP)
                    if b + 1 == GLA:
                        v.memset(a_S[:, :, :], 0.0)
                        v.memset(a_att[:, :, :], 0.0)
                        v.memset(a_one[:, :], 1.0)
                        v.memset(a_dec[:, :], 0.0)
                        v.drain()
                        with v.Fori(0, NTT) as i:
                            gla_step(l, i, fills(l, b, i, [0, 2, 4]))
                        gla_samples(l)
                    if b + 1 == NBR:
                        with v.Fori(0, KD) as i:
                            for c in range(NC):
                                merge_unit(l, b, i, c)
                    if b + 1 < NBR:
                        z_phase(l, b + 1)
                    if b + 2 < NBR:
                        inputs_ready(l, "in", b + 2)
                        if b + 2 == GLA:
                            inputs_ready(l, "rank", GLA)
                        v.wait_ge(loaded[b + 2], 16 * LOADS[b + 2] * (l + 1))
                        hold(v, "dve")
                v.drain()
                for j in range(KD):
                    ts(xh[:, j, :], merged[:, j, :], 0.5, None, ALU.mult)
                v.drain()
                for j in range(KD):
                    last = stt(xl[:, j, :], merged[:, j, :], 0.5, xh[:, j, :].bitcast(F32), ALU.mult, ALU.subtract)
                last.then_inc(m_ready, 1)
                v.drain()
                t = TABLE["out", 0]
                v.wait_ge(res_loaded, 16 * (l + 1))
                hold(v, "dve")
                with v.Fori(0, KD) as i:
                    for c, (a, z) in enumerate(CHUNKS):
                        v.wait_ge(g_full, NG * l + NC * (t["w8"] + i) + c + 1)
                        one = lambda ap: ap[:, bass.ds(i, 1), a:z].rearrange("p o t -> p (o t)")
                        stt(one(merged), one(A), DN_ALPHA, B[c][:, 0:z - a], ALU.mult, ALU.add).then_inc(g_free_dve, 1)
                layer_norm(l + 1)


OFF = dict(gq=0, gk=256, gv=512, glr=1024, gz=1040, lx=1552, lz=2064, sq=2576, sk=3088, sv=3216, sz=3344,
           su=3856, svv=4368, suz=4880, mq=5392, mz=5648, gates=5904)


def feature_tiles():
    import numpy as np
    span = lambda name, n: [np.arange(OFF[name] + P * i, OFF[name] + P * i + P) for i in range(n)]
    pairs = lambda name: [np.concatenate([np.arange(OFF[name] + 64 * h, OFF[name] + 64 * h + 64) for h in (i, 4 + i)])
                          for i in range(4)]
    inputs = [span("mq", 2), span("lx", 4), pairs("sq") + span("sk", 1) + span("sv", 1),
              span("su", 4) + span("svv", 4), span("gq", 2) + span("gk", 2) + span("gv", 4)]
    zs = [span("mz", 2), span("lz", 4), pairs("sz"), span("suz", 4), span("gz", 4)]
    tiles = []
    for kind, b, n in PHASES:
        if kind == "in":
            tiles += inputs[b]
        if kind == "z":
            tiles += zs[b]
        if kind == "rank":
            tiles.append(np.arange(OFF["glr"], OFF["glr"] + 16))
        if kind == "merge":
            g = OFF["gates"] + D * GATE_OF[b]
            tiles += [np.arange(g + P * j, g + P * j + P) for j in range(KD)]
        if kind == "out":
            tiles += [None] * KD
    return tiles


def constants():
    import numpy as np
    f = np.float32
    i, j = np.arange(P)[:, None], np.arange(P)[None, :]
    c = dict(ident=np.eye(P, dtype=f), tril=(i <= j).astype(f))
    a, b = np.arange(NSAMP)[:, None], np.arange(NSAMP)[None, :]
    c["tril8"] = ((a // NS == b // NS) & (a <= b)).astype(f)
    c["reset"] = np.broadcast_to((b % NS != 0).astype(f), (P, NSAMP)).copy()
    c["hot"] = (a // NS == np.arange(NB)[None, :]).astype(f)
    masks = []
    for blk, _, cross in LEVELS:
        same = i // blk == j // blk
        masks.append(same & (i % blk < blk // 2) & (j % blk >= blk // 2) if cross else same & (i <= j))
    c["gla_mask"] = np.stack(masks, axis=1).astype(f)
    c["swa_mask"] = np.concatenate([np.where(j >= i, 0, NEG), np.where(j <= i, 0, NEG)], axis=1).astype(f)
    sm = np.zeros((P, 4, P + NSAMP), f)
    for row in range(P):
        t = row % NS
        for u in range(4):
            seq = 2 * u + row // 64
            sm[row, u, :P] = np.where(np.arange(P) >= t, 0, NEG)
            sm[row, u, P:] = np.where((b[0] // NS == seq) & (b[0] % NS <= t), 0, NEG)
    c["swa_smask"] = sm
    rot = np.zeros((P, P), f)
    dd = np.arange(P)
    for m in dd[dd % 64 < 8]:
        rot[m + 8, m] = 1
        rot[m, m + 8] = 1
    c["rot"] = rot
    pos = np.concatenate([np.arange(SEQ), np.tile(2048 + np.arange(NS), NB)]).astype(f)
    inv = (f(500000.0) ** (-np.arange(8, dtype=f) / f(8))).astype(f)
    ang = (pos[None, :] * inv[:, None]).astype(f)
    rope = np.zeros((P, 2, T), f)
    rope[:, 0] = 1
    for base in (0, 64):
        rope[base:base + 8, 0] = rope[base + 8:base + 16, 0] = np.cos(ang.astype(np.float64))
        rope[base:base + 8, 1] = -np.sin(ang.astype(np.float64))
        rope[base + 8:base + 16, 1] = np.sin(ang.astype(np.float64))
    c["rope"] = rope
    return c


def kernel(**inputs):
    import numpy as np
    import concourse.bacc as bacc
    from concourse.bass_utils import run_bass_kernel_spmd

    g = {k: np.asarray(v) for k, v in inputs.items()}
    f = np.float32
    arrays = constants()

    def feature_major(x):
        return x.T.reshape(-1, P, x.shape[0]).transpose(1, 0, 2)

    def subtiles(w):
        return w.reshape(-1, P, w.shape[1]).transpose(1, 0, 2)

    arrays["x"] = feature_major(np.concatenate([g["x_prompt"][0], g["x_sample"].reshape(NSAMP, D)]))
    arrays["mem"] = feature_major(g["mem_prompt"][0]).reshape(P, -1)
    arrays["w_mem"] = np.stack([subtiles(w).reshape(P, -1) for w in g["w_mem_kv"]])
    tiles = feature_tiles()
    w8 = np.zeros((DEPTH, N8, P, KD, P), f)
    w4 = np.zeros((DEPTH, N4, P, 4, P), f)
    swa_rows = np.concatenate([np.arange(64 * h, 64 * h + 64) for i in range(4) for h in (i, 4 + i)])
    for l in range(DEPTH):
        win, wout = subtiles(g["w_in"][l]), subtiles(g["w_out"][l])
        j = 0
        for n, cols in enumerate(tiles):
            if cols is None:
                w8[l, n] = wout[:, :, P * j:P * j + P]
                j += 1
            else:
                w8[l, n, :, :, :len(cols)] = win[:, :, cols]
        for b in range(NBR):
            wbr = g["w_branch_mem"][l] if b == MEM else g["w_branch"][l, GATE_OF[b]]
            if b == SWA:
                wbr = wbr[swa_rows]
            for j in range(KD):
                w4[l, KD * b + j, :, :Y_TILES[b]] = subtiles(wbr)[:, :, P * j:P * j + P]
    arrays["w8"] = w8.reshape(DEPTH * N8, P, -1)
    arrays["w4"] = w4.reshape(DEPTH * N4, P, -1)

    def columns(v):
        return v.reshape(-1, P).T

    lnp = [np.concatenate([columns(g["ln_in_g"]), columns(g["ln_in_b"])], axis=1)]
    lnp += [np.concatenate([columns(g["ln_g"][l]), columns(g["ln_b"][l])], axis=1) for l in range(DEPTH)]
    arrays["lnp"] = np.stack(lnp)

    K, V = g["cache_mem_k"], g["cache_mem_v"]
    kt = K.transpose(0, 1, 3, 4, 2).reshape(DEPTH * NB, 2, P, N_MEM).transpose(0, 2, 1, 3)
    vv = V.reshape(DEPTH * NB, 2, P, 256).transpose(0, 2, 1, 3)
    arrays["memkv"] = np.concatenate([kt.reshape(-1, P, 512), vv.reshape(-1, P, 512)], axis=2)
    K, V = g["cache_swa_k"], g["cache_swa_v"]
    kt = K.transpose(0, 3, 4, 1, 2).reshape(DEPTH, P, NB, WINDOW)
    vv = V.reshape(DEPTH, NB, WINDOW, P).transpose(0, 2, 1, 3)
    arrays["swakv"] = np.concatenate([kt, vv], axis=3)
    arrays["cache_k"] = K.reshape(DEPTH, NB, WINDOW, P)
    arrays["cache_v"] = V.reshape(DEPTH, NB, WINDOW, P)
    sinks = g["swa_sinks"]
    order = [4 * e + 2 * r + m for r in range(2) for e in range(2) for m in range(2)]
    arrays["sink"] = np.broadcast_to(sinks[:, None, order], (DEPTH, P, 8))
    arrays["sinkr"] = sinks[:, (np.arange(P) % 64) // NS][:, :, None]

    arrays["sgu_g"], arrays["sgu_b"] = g["sgu_ln_g"], g["sgu_ln_b"]
    wt = g["sgu_w"].transpose(0, 3, 1, 2)
    arrays["sgu_w"] = wt
    ws = np.zeros((DEPTH, NB, NS, 4, NB, NS), f)
    for b in range(NB):
        ws[:, b, :, :, b, :] = wt[:, :NS, :, :NS]
    arrays["sgu_ws"] = ws.reshape(DEPTH, NSAMP, 4, NSAMP)
    arrays["sgu_bs"] = g["sgu_b"]
    arrays["sgu_bss"] = np.tile(g["sgu_b"][:, :, :NS], (1, 1, NB))

    arrays["wa2"] = g["gla_wa2"]
    arrays["ba"] = np.stack([columns(v) for v in g["gla_ba"]])
    arrays["ng"] = g["gla_norm_g"][:, :, None]
    s0 = np.zeros((DEPTH, P, NB, 4, P), f)
    for h in range(4):
        r = 64 * (h % 2)
        s0[:, r:r + 64, :, h] = g["state_gla"][:, :, h].transpose(0, 2, 1, 3)
    arrays["gla_s0"] = s0

    lru = np.zeros((DEPTH, 4, P, LW_N), f)
    for l in range(DEPTH):
        for ct in range(4):
            for e in range(2):
                r = slice(64 * e, 64 * e + 64)
                lru[l, ct, r, LW_WR + 64 * e:LW_WR + 64 * e + 64] = g["lru_wr"][l, 2 * ct + e]
                lru[l, ct, r, LW_WI + 64 * e:LW_WI + 64 * e + 64] = g["lru_wi"][l, 2 * ct + e]
            ch = slice(P * ct, P * ct + P)
            lru[l, ct, :, LW_CW:LW_CW + 4] = g["lru_conv_w"][l, :, ch].T
            for at, name in ((LW_CB, "lru_conv_b"), (LW_BR, "lru_br"), (LW_BI, "lru_bi"), (LW_LAM, "lru_L")):
                lru[l, ct, :, at] = g[name][l, ch]
            lru[l, ct, :, LW_H0:LW_H0 + NB] = g["state_lru_h"][l, :, ch].T
            lru[l, ct, :, LW_CONV:] = g["state_lru_conv"][l, :, :, ch].transpose(2, 0, 1).reshape(P, -1)
    arrays["lru"] = lru.reshape(DEPTH * 4, P, LW_N)

    outs = dict(y=(P, KD, T), mkv=(DEPTH, P, 1024), lru_tail=(DEPTH * 4, P, NTAIL),
                swa_new=(DEPTH, P, 2 * P + 2 * NSAMP), swa_old_k=(DEPTH, NB, WINDOW - NS, P),
                swa_old_v=(DEPTH, NB, WINDOW - NS, P), gla_p=(DEPTH, P, 4, P), gla_s=(DEPTH, P, NB, 4, P),
                sgu_v=(DEPTH, NSAMP, 512))
    nc = bacc.Bacc("TRN2", target_bir_lowering=False, num_devices=1)
    d, feed = {}, {}
    for name, a in arrays.items():
        feed["in_" + name] = np.ascontiguousarray(a)
        d[name] = nc.dram_tensor("in_" + name, a.shape, mybir.dt.from_np(a.dtype), kind="ExternalInput").ap()
    for name, shape in outs.items():
        d[name] = nc.dram_tensor("out_" + name, shape, F32, kind="ExternalOutput").ap()
    build(nc, d)
    got = run_bass_kernel_spmd(nc, [feed], core_ids=[0]).results[0]
    o = {name: np.asarray(got["out_" + name]) for name in outs}

    y = o["y"].transpose(1, 0, 2).reshape(D, T).T
    half = lambda h: slice(64 * (h % 2), 64 * (h % 2) + 64)
    gla_p = np.stack([o["gla_p"][:, half(h), h] for h in range(4)], axis=1)[:, None]
    gla_s = np.stack([o["gla_s"][:, half(h), :, h].transpose(0, 2, 1, 3) for h in range(4)], axis=2)
    tail = o["lru_tail"].reshape(DEPTH, 512, NTAIL)
    lru_p, lru_s = tail[:, :, 0][:, None], tail[:, :, 1:9].transpose(0, 2, 1)
    conv = tail[:, :, 9:].reshape(DEPTH, 512, 9, 3).transpose(0, 2, 3, 1)
    new = o["swa_new"]

    def window(at, n):
        return new[:, :, at:at + n].transpose(0, 2, 1)

    def swa_prompt(at):
        return window(at, P).reshape(DEPTH, 1, WINDOW, 2, 64)

    def swa_sample(at, old):
        return np.concatenate([old, window(at, NSAMP).reshape(DEPTH, NB, NS, P)], axis=2)\
            .reshape(DEPTH, NB, WINDOW, 2, 64)

    mk = o["mkv"][:, :, :512].reshape(DEPTH, P, 2, N_MEM).transpose(0, 3, 2, 1).reshape(DEPTH, 1, N_MEM, 4, 64)
    mv = o["mkv"][:, :, 512:].reshape(DEPTH, P, 2, 256).transpose(0, 2, 1, 3).reshape(DEPTH, 1, N_MEM, 4, 64)
    result = (y[:SEQ].reshape(1, SEQ, D), y[SEQ:].reshape(NB, NS, D), gla_p, gla_s, lru_p, lru_s,
              conv[:, 0:1], conv[:, 1:], swa_prompt(0), swa_sample(2 * P, o["swa_old_k"]),
              swa_prompt(P), swa_sample(2 * P + NSAMP, o["swa_old_v"]), mk, mv,
              o["sgu_v"].reshape(DEPTH, NB, NS, 512))
    return tuple(np.ascontiguousarray(a) for a in result)
```

```python
from contextlib import ExitStack

import concourse.bass as bass
from concourse import mybir

F32 = mybir.dt.float32
F32R = mybir.dt.float32r
BF16 = mybir.dt.bfloat16
U32 = mybir.dt.uint32
ALU = mybir.AluOpType
ACT = mybir.ActivationFunctionType
AX_X = mybir.AxisListType.X

P = 128
D = 1024
SEQ = 1024
DEPTH = 2
NB = 8
NS = 8
NSAMP = NB * NS
T = SEQ + NSAMP
KD = D // P
NTT = SEQ // P
STEPS = NTT + 1
CHUNKS = [(0, 364), (364, 728), (728, T)]
NC = len(CHUNKS)
CW = CHUNKS[0][1]
N_MEM = 256
WINDOW = 128
LN_EPS = 1e-5
RMS_EPS = 1e-6
DN_ALPHA = (2 * DEPTH) ** 0.25
HEAD_SCALE = 64 ** -0.5
GLA_TAU = 16.0
NEG = -1.0e30
CLAMP = 80.0 * GLA_TAU

MEM, LRU, SWA, SGU, GLA = range(5)
IN_TILES = [2, 4, 6, 8, 8]
Y_TILES = [2, 4, 4, 4, 4]
GATE_OF = [4, 1, 2, 3, 0]
OUT_SLOT = [0, 0, 0, 0, 4]
LOADS = [2, 0, 6, 8, 5]
NBR = 5

PHASES = [("in", 0, 2), ("z", 0, 2), ("in", 1, 4)]
for _b in range(NBR):
    PHASES.append(("merge", _b, KD))
    if _b + 1 < NBR:
        PHASES.append(("z", _b + 1, Y_TILES[_b + 1]))
    if _b + 2 < NBR:
        PHASES.append(("in", _b + 2, IN_TILES[_b + 2]))
    if _b + 2 == GLA:
        PHASES.append(("rank", GLA, 1))
PHASES.append(("out", 0, KD))


def phase_table():
    table, w8, w4, ring = {}, 0, 0, 0
    units = {"in": 0, "z": 0, "merge": 0, "out": 0}
    for kind, b, n in PHASES:
        table[kind, b] = dict(w8=w8, w4=w4, ring=ring, n=n, **{f"u_{k}": v for k, v in units.items()})
        w8 += n
        ring += n
        if kind in ("merge", "rank"):
            w4 += n if kind == "merge" else 0
            ring += n
        units["in" if kind == "rank" else kind] += NC * n
    return table, w8, w4, ring, units


TABLE, N8, N4, NRING, UNITS = phase_table()
NG = NC * N8
ACT_FREES = UNITS["in"] + UNITS["merge"]
DVE_FREES = UNITS["z"] + UNITS["out"]
TH_UNITS = UNITS["z"] + UNITS["merge"]
P_UNITS = UNITS["merge"]

HALF = P // 2
LEVELS = [(P, HALF - 1), (HALF, HALF // 2 - 1)]
NLEV = len(LEVELS)

LW_WR, LW_WI, LW_CW, LW_CB, LW_BR, LW_BI, LW_LAM, LW_H0, LW_CONV = 0, 128, 256, 260, 261, 262, 263, 264, 272
LW_N = LW_CONV + 3 * NB
NTAIL = 9 + 27


def build(nc, d):
    with ExitStack() as ctx:
        def sb(name, shape, dt=F32):
            return ctx.enter_context(nc.sbuf_tensor(name, shape, dt))

        def sem(name):
            return ctx.enter_context(nc.semaphore(name))

        xh = sb("xh", [P, KD, T], F32R)
        xl = sb("xl", [P, KD, T], BF16)
        yh = sb("yh", [P, 4, T], F32R)
        yl = sb("yl", [P, 4, T], BF16)
        merged = sb("merged", [P, KD, T])
        A = sb("arena", [P, 9, T])
        raw = sb("w_raw", [P, 2, D])
        wh = sb("w_hi", [P, 2, KD, P], F32R)
        wl = sb("w_lo", [P, 2, KD, P], F32R)
        wb = sb("w_bf", [P, 2, KD, P], BF16)
        ident = sb("ident", [P, P])
        ones = sb("ones", [P, P])
        th = sb("th", [P, 2, CW])
        tm = sb("tm", [P, CW])
        tm2 = sb("tm2", [P, CW])
        lnp = sb("lnp", [P, 2 * KD])
        WK = sb("mixer_space", [P, 6208])
        B = [ctx.enter_context(nc.psum_tensor(f"bank{i}", [P, 512], F32)) for i in range(8)]

        s_const = sem("const_loaded")
        s_ones = sem("ones_set")
        z_th = sem("z_tanh_ready")
        mem_cache = sem("mem_cache_loaded")
        raw_full = [sem(f"raw_full{s}") for s in range(2)]
        raw_free = sem("raw_free")
        split_full = sem("split_full")
        split_free = sem("split_free")
        g_full = sem("gate_bank_full")
        g_free_act = sem("gate_bank_free_act")
        g_free_dve = sem("gate_bank_free_dve")
        p_full = sem("branch_bank_full")
        p_free = sem("branch_bank_free")
        y_ready = sem("y_ready")
        x_ready = sem("x_ready")
        m_ready = sem("merged_split")
        x_loaded = sem("x_loaded")
        x_stored = sem("x_stored")
        res_loaded = sem("residual_loaded")
        lnp_loaded = sem("ln_params_loaded")
        ln_sum = sem("ln_sum")
        ln_mean = sem("ln_mean")
        ln_cent = sem("ln_centered")
        ln_sq = sem("ln_squares")
        ln_var = sem("ln_var")
        ln_rec = sem("ln_reciprocal")
        ln_rstd = sem("ln_rstd")
        ln_norm = sem("ln_normalised")
        ln_aff = sem("ln_affine")
        mkv_in = sem("mkv_inputs")
        mkv_ps = sem("mkv_product")
        mkv_sb = sem("mkv_copied")
        mkv_out = sem("mkv_stored")
        loaded = [sem(f"mixer{b}_loaded") for b in range(NBR)]
        stored = sem("states_stored")

        s_held = {e: sem(f"held_{e}") for e in ("pe", "dve", "pool")}

        def hold(eng, name):
            eng.sem_inc(s_held[name], 1)

        def carve():
            at = [0]

            def take(*dims):
                n = 1
                for x in dims:
                    n *= x
                ap = WK[:, at[0]:at[0] + n]
                at[0] += n
                assert at[0] <= 6208, at[0]
                if len(dims) == 2:
                    ap = ap.rearrange("p (a b) -> p a b", a=dims[0])
                if len(dims) == 3:
                    ap = ap.rearrange("p (a b c) -> p a b c", a=dims[0], b=dims[1])
                return ap
            return take

        def bc(ap, n):
            return ap.unsqueeze(1).broadcast_to([ap.shape[0], n, ap.shape[1]])

        def bl(ap, n):
            return ap.unsqueeze(2).broadcast_to([ap.shape[0], ap.shape[1], n])

        take = carve()
        m_q = [take(2, P) for _ in range(2)]
        m_pr = [take(4, 256) for _ in range(2)]
        m_pt = [take(8, P) for _ in range(2)]
        m_mx = [take(4) for _ in range(2)]
        m_sum = [take(4) for _ in range(2)]
        m_qbd = take(2, NB, 32)
        mem_q, mem_scores, mem_max, mem_exp, mem_prob, mem_pt, mem_pta, mem_ptd, mem_o = (
            sem(f"mem_{x}") for x in ("q_staged", "scores", "max", "exp", "prob", "pt", "pt_act", "pt_dve", "o"))

        take = carve()
        s_q = [take(4, P) for _ in range(2)]
        s_k = take(3, P)
        s_vn = take(3, P)
        s_pr = [take(4, 256) for _ in range(2)]
        s_pt = [take(8, P) for _ in range(2)]
        s_tq = [x[:, 0:2, :].rearrange("p a b -> p (a b)").rearrange("p (a b) -> p a b", a=4) for x in s_pr]
        s_tk = [x[:, 2, 0:P] for x in s_pr]
        s_v = [x[:, 0, :] for x in s_pt]
        s_qbd = s_pr[1].rearrange("p a b -> p (a b)")[:, 0:NB * NSAMP].rearrange("p (b h) -> p b h", b=NB)
        s_mx = [take(4) for _ in range(2)]
        s_nm = [take(4) for _ in range(2)]
        s_es = [take(4) for _ in range(2)]
        s_sum = [take(4) for _ in range(2)]
        s_sink = take(8)
        s_sinkr = take(1)
        s_rot = take(P)
        s_mask = A[:, 8, 0:2 * P]
        s_smask = A[:, 8, 2 * P:2 * P + 4 * 192].rearrange("p (u s) -> p u s", u=4)
        (swa_vst, swa_rot, swa_qk, swa_scores, swa_max, swa_exp, swa_prob, swa_pt, swa_pta, swa_ptd, swa_o,
         swa_cache, swa_old) = (
            sem(f"swa_{x}") for x in ("v_staged", "rotated", "qk", "scores", "max", "exp", "prob", "pt", "pt_act",
                                      "pt_dve", "o", "cache_loaded", "window_stored"))

        take = carve()
        l_w = take(LW_N)
        l_s4 = take(1)
        l_ns4 = take(1)
        l_h = take(2)
        l_t = take(8)
        l_pad = take(NB, 11)
        l_ab = take(NB, 9)
        l_ub = take(NB, 9)
        l_hb = take(NB, 9)
        l_tail = take(NTAIL)
        (lru_w, lru_e, lru_l, lru_conv, lru_r, lru_i, lru_ps, lru_act, lru_w2, lru_sq, lru_done, lru_tail) = (
            sem(f"lru_{x}") for x in ("params", "exp_lam", "exp_lam_done", "conv", "decays_exp", "decay", "gates_ps",
                                      "gates_act", "radicand", "root", "done", "tail_stored"))

        take = carve()
        g_v = [take(4, P) for _ in range(2)]
        g_vn = [take(512) for _ in range(2)]
        g_vs = [take(512) for _ in range(2)]
        g_bn = [take(6) for _ in range(2)]
        g_mv = [take(2) for _ in range(2)]
        g_rs = [take(1) for _ in range(2)]
        g_lng = take(512)
        g_lnb = take(512)
        g_w = take(4, P)
        g_b = take(4, P)
        g_ws = take(4, NSAMP)
        g_bs = take(4, NSAMP)
        g_m = take(P)
        g_ms = take(NSAMP)
        (sgu_vst, sgu_vt, sgu_var, sgu_rstd, sgu_vn, sgu_mix, sgu_stored) = (
            sem(f"sgu_{x}") for x in ("v_staged", "v_transposed", "var", "rstd", "v_normed", "mixed", "v_stored"))

        take = carve()
        a_v = take(4, P)
        a_vn = take(512)
        a_la = take(T)
        a_b = take(2, P)
        a_dq = take(NLEV + 1, 2 * P)
        a_dk = take(NLEV + 1, 2 * P)
        a_x = a_dq.rearrange("p a b -> p (a b)")[:, 0:2 * CW].rearrange("p (a b) -> p a b", a=2)
        a_e = a_dk.rearrange("p a b -> p (a b)")[:, 0:2 * CW].rearrange("p (a b) -> p a b", a=2)
        a_wa = take(2 * P)
        a_kn = a_wa.rearrange("p (a b) -> p a b", a=2)
        a_km = take(2, P)
        a_att = take(4, P)
        a_S = take(4, P)
        a_rs = take(512)
        a_dec = take(16)
        a_ba = take(2)
        a_ng = take(1)
        a_mask = take(P)
        a_smask = take(NSAMP)
        a_reset = a_km.rearrange("p a b -> p (a b)")[:, 0:NSAMP]
        (gla_vst, gla_vt, gla_x, gla_na, gla_e, gla_la, gla_d, gla_ex, gla_qk, gla_att, gla_attm, gla_vn, gla_o, gla_oc,
         gla_sqr, gla_ss, gla_rec, gla_rstd, gla_kh, gla_kt, gla_kn, gla_st, gla_s0, gla_s0st, gla_km, gla_sts,
         gla_os, gla_nd) = (
            sem(f"gla_{x}") for x in ("v_staged", "v_transposed", "pre", "negabs", "softplus", "log_decay", "exponents",
                                      "exps", "qk", "products", "att", "v_rows", "o", "o_copied", "squares", "sumsq",
                                      "rec", "rstd", "k_hat", "k_transposed", "k_rows", "state_ps", "states_loaded",
                                      "states_stored", "k_masked", "sample_update", "sample_o", "normalised"))

        take = carve()
        ln_m = take(NC, CW)
        ln_v = take(NC, CW)

        def swa_caches():
            return A[:, 6:8, :].rearrange("p a t -> p (a t)")[:, 0:NB * 2 * P].rearrange("p (b n) -> p b n", b=NB)

        def sample_states():
            return A[:, 0:4, :].rearrange("p a t -> p (a t)")[:, 0:NB * 4 * P].rearrange(
                "p (b h v) -> p b h v", b=NB, h=4)

        def level(ap, k):
            return ap[:, k, :].rearrange("p (h t) -> p h t", h=2)

        block = ctx.enter_context(nc.Block())

        def ring_items(kind, b, n):
            if kind == "merge":
                return n, (KD, Y_TILES[b])
            if kind == "rank":
                return 1, (KD, 0)
            return n // 2, (KD, KD)

        @block.sync
        def _(sp):
            with sp.Fori(0, DEPTH) as l:
                for kind, b, n in PHASES:
                    t = TABLE[kind, b]
                    pairs, subs = ring_items(kind, b, n)
                    per = 2 if kind in ("in", "z", "out") else 1
                    with sp.Fori(0, pairs) as i:
                        for s in range(2):
                            sp.wait_ge(raw_free, NRING * l + t["ring"] + 2 * i + s + 1)
                            if kind == "merge" and s == 1:
                                src = d["w4"][bass.ds(N4 * l + t["w4"] + i, 1), :, 0:subs[1] * P]
                            else:
                                m = max(subs[s] * P, 16)
                                src = d["w8"][bass.ds(N8 * l + t["w8"] + per * i + (s if per == 2 else 0), 1), :, 0:m]
                            w = src.shape[2]
                            sp.dma_start(raw[:, s, 0:w], src.rearrange("o p n -> p (o n)")).then_inc(raw_full[s], 16)

        @block.gpsimd
        def _(g):
            g.memset(ones[:, :], 1.0).then_inc(s_ones, 1)
            g.sem_inc(raw_free, 2)
            def split(l, t, i, s, m, used, count):
                tile = NRING * l + t["ring"] + 2 * i + s
                g.wait_ge(raw_full[s], 16 * (NRING // 2 * l + t["ring"] // 2 + i + 1))
                g.wait_ge(split_free, 2 * tile + 1)
                hold(g, "pool")
                if m:
                    r = raw[:, s, 0:m * P]
                    h = wh[:, s, 0:m, :].rearrange("p k n -> p (k n)")
                    lo = wl[:, s, 0:m, :].rearrange("p k n -> p (k n)")
                    bf = wb[:, s, 0:m, :].rearrange("p k n -> p (k n)")
                    g.tensor_scalar(h, r, 1.0, 1.0, ALU.mult, ALU.mult).then_inc(split_full, 1)
                    g.drain()
                    g.wait_ge(split_free, 2 * tile + 2)
                    hold(g, "pool")
                    g.tensor_tensor(lo, r, h.bitcast(F32), ALU.subtract).then_inc(split_full, 1)
                    g.wait_ge(used, count)
                    hold(g, "pool")
                    g.tensor_scalar(bf, r, 1.0, 1.0, ALU.mult, ALU.mult).then_inc(split_full, 1)
                    g.drain()
                else:
                    g.wait_ge(split_free, 2 * tile + 2)
                    g.sem_inc(split_full, 3)
                g.sem_inc(raw_free, 1)

            def in_phase(kind, l, t, s, i):
                if kind == "merge":
                    return (p_full, P_UNITS * l + t["u_merge"] + NC * (i + 1)) if s else \
                        (g_full, NG * l + NC * (t["w8"] + i + 1))
                if kind == "rank":
                    return g_full, NG * l + NC * (t["w8"] + 1)
                return g_full, NG * l + NC * (t["w8"] + 2 * i + s + 1)

            with g.Fori(0, DEPTH) as l:
                before = None
                for kind, b, n in PHASES:
                    t = TABLE[kind, b]
                    pairs, subs = ring_items(kind, b, n)
                    for s in range(2):
                        last = (g_free_dve, DVE_FREES * l + 3) if before is None else \
                            in_phase(before[0], l, TABLE[before[:2]], s, ring_items(*before)[0] - 1)
                        split(l, t, 0, s, subs[s], *last)
                    if pairs > 1:
                        with g.Fori(1, pairs) as i:
                            for s in range(2):
                                split(l, t, i, s, subs[s], *in_phase(kind, l, t, s, i - 1))
                    before = (kind, b, n)

        @block.tensor
        def _(pe):
            mm = pe.matmul

            def product(bank, s, nk, c, hi, lo, tile):
                a, z = CHUNKS[c]
                out = bank[:, 0:z - a]
                passes = [(wh, hi), (wl, hi), (wb, lo)]
                for part, (w, x) in enumerate(passes):
                    if c == 0:
                        pe.wait_ge(split_full, 3 * tile + part + 1)
                    for k in range(nk):
                        last = mm(out, w[:, s, k, :], x[:, k, a:z], start=(part == 0 and k == 0),
                                  stop=(part == 2 and k == nk - 1))
                    if c == NC - 1 and part < 2:
                        last.then_inc(split_free, 1)
                return last

            def dense(l, kind, b, free, per, base, ready=None):
                t = TABLE[kind, b]
                other = (g_free_dve, DVE_FREES, t["u_z"] + t["u_out"]) if free is g_free_act else \
                    (g_free_act, ACT_FREES, t["u_in"] + t["u_merge"])
                pe.wait_ge(other[0], other[1] * l + other[2] + 3)
                hold(pe, "pe")
                pe.wait_ge(free, per * l + base + 3)
                hold(pe, "pe")
                with pe.Fori(0, t["n"] // 2) as i:
                    for s in range(2):
                        for c in range(NC):
                            if ready is not None and s == 0:
                                pe.wait_ge(x_ready, ready + c + 1)
                                hold(pe, "pe")
                            pe.wait_ge(free, per * l + base + 2 * NC * i + NC * s + c + 2)
                            product(B[(NC * s + c) % 2], s, KD, c, xh, xl, NRING * l + t["ring"] + 2 * i + s)\
                                .then_inc(g_full, 1)

            def merge_start(l, b):
                t = TABLE["merge", b]
                pe.wait_ge(g_free_dve, DVE_FREES * l + t["u_z"] + t["u_out"] + 3)
                pe.wait_ge(y_ready, UNITS["z"] * l + t["u_z"] + 2)
                hold(pe, "pe")

            def merge_unit(l, b, j, c):
                t = TABLE["merge", b]
                q = t["u_merge"] + NC * j
                tile = NRING * l + t["ring"] + 2 * j
                pe.wait_ge(g_free_act, ACT_FREES * l + t["u_in"] + q + c + (3, 2, 2)[c])
                product(B[c % 2], 0, KD, c, xh, xl, tile).then_inc(g_full, 1)
                pe.wait_ge(p_free, P_UNITS * l + q + c + 2)
                product(B[2], 1, Y_TILES[b], c, yh, yl, tile + 1).then_inc(p_full, 1)

            def layer_norm(n):
                for c, (a, z) in enumerate(CHUNKS):
                    for j in range(KD):
                        last = mm(B[3 + c][:, 0:z - a], ones[:, :], merged[:, j, a:z], start=(j == 0), stop=(j == KD - 1))
                    last.then_inc(ln_sum, 1)
                for c, (a, z) in enumerate(CHUNKS):
                    pe.wait_ge(ln_sq, NC * n + c + 1)
                    for j in range(KD):
                        last = mm(B[(6, 7, 3)[c]][:, 0:z - a], ones[:, :], A[:, j, a:z], start=(j == 0), stop=(j == KD - 1))
                    last.then_inc(ln_var, 1)

            def memory_products():
                W = A[:, 0:4, :].rearrange("p a t -> p (a t)")[:, 0:4096].rearrange("p (k n) -> p k n", k=KD)
                M = A[:, 4:6, :].rearrange("p a t -> p (a t)")[:, 0:2048].rearrange("p (k s) -> p k s", k=KD)
                for l in range(DEPTH):
                    pe.wait_ge(mkv_in, 16 * (l + 2))
                    if l:
                        pe.wait_ge(mkv_sb, l)
                    for p in range(2):
                        for k in range(KD):
                            mm(B[5][:, 256 * p:256 * p + 256], W[:, k, P * p:P * p + P], M[:, k, :],
                               start=(k == 0), stop=(k == KD - 1))
                    for p in range(2):
                        for k in range(KD):
                            last = mm(B[6][:, 256 * p:256 * p + 256], M[:, k, P * p:P * p + P], W[:, k, 256:512],
                                      start=(k == 0), stop=(k == KD - 1))
                    last.then_inc(mkv_ps, 1)

            def mem_pair(l, i):
                for s in range(2):
                    pe.wait_ge(mem_q, 10 * l + 2 * i + s + 1)
                    for h in range(4):
                        p, e = h // 2, h % 2
                        last = mm(B[3 + 2 * s + e][:, 256 * p:256 * p + 256], m_q[s][64 * e:64 * e + 64, p, :],
                                  A[64 * e:64 * e + 64, 6, 256 * p:256 * p + 256], start=True, stop=True)
                    last.then_inc(mem_scores, 1)
                for s in range(2):
                    pe.wait_ge(mem_prob, 10 * l + 2 * i + s + 1)
                    for m in range(4):
                        for st in range(2):
                            last = pe.transpose(B[3 + 2 * s + m // 2][:, (m % 2 * 2 + st) * P:(m % 2 * 2 + st + 1) * P],
                                                m_pr[s][:, m, st * P:st * P + P], ident[:, :])
                    last.then_inc(mem_pt, 1)
                for s in range(2):
                    pe.wait_ge(mem_pta, NTT * l + 2 * i + s + 1)
                    pe.wait_ge(mem_ptd, 10 * l + 2 * i + s + 1)
                    for m in range(4):
                        e, p = m // 2, m % 2
                        for st in range(2):
                            last = mm(B[7][64 * e:64 * e + 64, 256 * s + P * p:256 * s + P * p + P],
                                      A[:, 6, 512 + 256 * st + 64 * (2 * p + e):512 + 256 * st + 64 * (2 * p + e) + 64],
                                      m_pt[s][:, 2 * m + st, :], start=(st == 0), stop=(st == 1))
                    last.then_inc(mem_o, 1)

            def mem_samples(l, g):
                n = 10 * l + NTT + g + 1
                if g:
                    pe.wait_ge(mem_cache, 16 * (l + 1))
                pe.wait_ge(mem_q, n)
                for b in range(4):
                    for p in range(2):
                        last = mm(B[5][32 * b:32 * b + 32, 0:256], m_qbd[:, p, 4 * g + b, :],
                                  A[:, 2 + b, 256 * p:256 * p + 256], start=(p == 0), stop=(p == 1))
                last.then_inc(mem_scores, 1)
                pe.wait_ge(mem_prob, n)
                for st in range(2):
                    last = pe.transpose(B[6][:, st * P:st * P + P], m_pr[0][:, 0, st * P:st * P + P], ident[:, :])
                last.then_inc(mem_pt, 1)
                pe.wait_ge(mem_ptd, n)
                for b in range(4):
                    for p in range(2):
                        for st in range(2):
                            last = mm(B[7][:, P * p + 32 * b:P * p + 32 * b + 32],
                                      A[:, 2 + b, 512 + 256 * st + P * p:512 + 256 * st + P * p + P],
                                      m_pt[0][:, st, 32 * b:32 * b + 32], start=(st == 0), stop=(st == 1))
                last.then_inc(mem_o, 1)

            def lru_step(l, ct, fill):
                n = 4 * l + ct + 1
                pe.wait_ge(lru_conv, n)
                for c, (a, z) in enumerate(CHUNKS):
                    if c:
                        pe.wait_ge(lru_act, 3 * 4 * l + 3 * ct + c)
                    mm(B[5][:, 0:z - a], l_w[:, LW_WR:LW_WR + P], A[:, 4, a:z], start=True, stop=True)
                    mm(B[6][:, 0:z - a], l_w[:, LW_WI:LW_WI + P], A[:, 4, a:z], start=True, stop=True)\
                        .then_inc(lru_ps, 1)
                    fill(c)

            def swa_pair(l, i, fill):
                for s in range(2):
                    pe.wait_ge(swa_vst, STEPS * l + 2 * i + s + 1)
                    tok = bass.ds(2 * P * i + P * s, P)
                    mm(B[3 + 2 * s][:, :], s_rot[:, :], A[:, 0:4, tok], start=True, stop=True)
                    mm(B[4 + 2 * s][:, 0:P], s_rot[:, :], A[:, 4, tok], start=True, stop=True)
                    pe.transpose(B[4 + 2 * s][:, P:2 * P], s_v[s][:, :], ident[:, :]).then_inc(swa_rot, 1)
                fill(0)
                for r in range(2):
                    at = (2 * STEPS - 1) * l + 4 * i + 2 * r
                    for s in range(2):
                        if r == 0:
                            pe.wait_ge(swa_qk, STEPS * l + 2 * i + s + 1)
                        for m in range(2):
                            for e in range(2):
                                last = mm(B[3 + 2 * s + e][:, 256 * m:256 * m + 256],
                                          s_q[s][64 * e:64 * e + 64, 2 * r + m, :],
                                          s_k[64 * e:64 * e + 64, s:s + 2, :], start=True, stop=True)
                        last.then_inc(swa_scores, 1)
                    fill(1 + 3 * r)
                    for s in range(2):
                        pe.wait_ge(swa_prob, at + s + 1)
                        for m in range(4):
                            for st in range(2):
                                last = pe.transpose(
                                    B[3 + 2 * s + m // 2][:, (m % 2 * 2 + st) * P:(m % 2 * 2 + st + 1) * P],
                                    s_pr[s][:, m, st * P:st * P + P], ident[:, :])
                        last.then_inc(swa_pt, 1)
                    fill(2 + 3 * r)
                    for s in range(2):
                        pe.wait_ge(swa_pta, at + s + 1)
                        pe.wait_ge(swa_ptd, at + s + 1)
                        for m in range(4):
                            e, q = m // 2, m % 2
                            for st in range(2):
                                last = mm(B[7][64 * e:64 * e + 64, 256 * s + P * q:256 * s + P * q + P],
                                          s_vn[:, s + st, 64 * e:64 * e + 64],
                                          s_pt[s][:, 2 * m + st, :], start=(st == 0), stop=(st == 1))
                        last.then_inc(swa_o, 1)
                    if r == 0:
                        fill(3)

            def swa_samples(l):
                n = STEPS * l + STEPS
                pe.wait_ge(swa_vst, n)
                mm(B[3][:, 0:4 * NSAMP], s_rot[:, :], A[:, 0:4, SEQ:T], start=True, stop=True)
                mm(B[4][:, 0:NSAMP], s_rot[:, :], A[:, 4, SEQ:T], start=True, stop=True)
                pe.transpose(B[4][0:NSAMP, P:2 * P], s_v[0][:, 0:NSAMP], ident[:, :]).then_inc(swa_rot, 1)
                pe.wait_ge(swa_qk, n)
                pe.wait_ge(swa_cache, 16 * (l + 1))
                C = swa_caches()
                for u in range(4):
                    o = 256 * (u % 2)
                    for e in range(2):
                        b = 2 * u + e
                        mm(B[5 + u // 2][64 * e:64 * e + 64, o:o + P], s_qbd[:, b, :], C[:, b, 0:P],
                           start=True, stop=True)
                    last = mm(B[5 + u // 2][:, o + P:o + P + NSAMP],
                              s_qbd[:, 2 * u:2 * u + 2, :].rearrange("p b h -> p (b h)"), s_k[:, 0, 0:NSAMP],
                              start=True, stop=True)
                last.then_inc(swa_scores, 1)
                m = (2 * STEPS - 1) * (l + 1)
                pe.wait_ge(swa_prob, m)
                for u in range(4):
                    pe.transpose(B[5][:, P * u:P * u + P], s_pr[0][:, u, 0:P], ident[:, :])
                for u in range(4):
                    last = pe.transpose(B[6][0:NSAMP, P * u:P * u + P], s_pr[0][:, u, P:P + NSAMP], ident[:, :])
                last.then_inc(swa_pt, 1)
                pe.wait_ge(swa_pta, m)
                pe.wait_ge(swa_ptd, m)
                for b in range(NB):
                    u, e = b // 2, b % 2
                    mm(B[7][:, 64 * b:64 * b + 64], C[:, b, P:2 * P], s_pt[0][:, u, 64 * e:64 * e + 64],
                       start=True, stop=False)
                    last = mm(B[7][:, 64 * b:64 * b + 64], s_vn[0:NSAMP, 1, :], s_pt[0][0:NSAMP, 4 + u, 64 * e:64 * e + 64],
                              start=False, stop=True)
                last.then_inc(swa_o, 1)

            def sgu_pair(l, i, fill):
                for s in range(2):
                    pe.wait_ge(sgu_vst, STEPS * l + 2 * i + s + 1)
                    for j in range(4):
                        last = pe.transpose(B[3 + 2 * s][:, P * j:P * j + P], g_v[s][:, j, :], ident[:, :])
                    last.then_inc(sgu_vt, 1)
                for k in range(3):
                    fill(k)
                for s in range(2):
                    pe.wait_ge(sgu_vn, STEPS * l + 2 * i + s + 1)
                    for j in range(4):
                        last = mm(B[4 + 2 * s][:, P * j:P * j + P], g_vn[s][:, P * j:P * j + P], g_w[:, j, :],
                                  start=True, stop=True)
                    last.then_inc(sgu_mix, 1)
                for k in range(3, 6):
                    fill(k)

            def sgu_samples(l):
                n = STEPS * l + STEPS
                pe.wait_ge(sgu_vst, n)
                hold(pe, "pe")
                for j in range(4):
                    last = pe.transpose(B[3][0:NSAMP, P * j:P * j + P], g_v[0][:, j, 0:NSAMP], ident[:, :])
                last.then_inc(sgu_vt, 1)
                pe.wait_ge(sgu_vn, n)
                for j in range(4):
                    last = mm(B[4][:, NSAMP * j:NSAMP * j + NSAMP], g_vn[0][0:NSAMP, P * j:P * j + P],
                              g_ws[0:NSAMP, j, :], start=True, stop=True)
                last.then_inc(sgu_mix, 1)

            def gla_rank(l):
                t = TABLE["rank", GLA]
                tile = NRING * l + t["ring"]
                for c in range(NC):
                    pe.wait_ge(g_free_act, ACT_FREES * l + t["u_in"] + t["u_merge"] + c + (3, 2, 2)[c])
                    product(B[c % 2], 0, KD, c, xh, xl, tile).then_inc(g_full, 1)
                pe.drain()
                pe.wait_ge(split_full, 3 * (tile + 2))
                pe.sem_inc(split_free, 2)

            def gla_decays(l):
                pe.wait_ge(loaded[GLA], 16 * LOADS[GLA] * (l + 1))
                pe.wait_ge(g_free_act, ACT_FREES * l + TABLE["rank", GLA]["u_in"] + TABLE["rank", GLA]["u_merge"] + NC + 3)
                for c, (a, z) in enumerate(CHUNKS):
                    if c:
                        pe.wait_ge(gla_na, NC * l + c)
                    for p in range(2):
                        last = mm(B[3 + p][:, 0:z - a], a_wa[0:16, P * p:P * p + P], A[0:16, 8, a:z],
                                  start=True, stop=True)
                    last.then_inc(gla_x, 1)

            def gla_products(n, w, levels):
                pe.wait_ge(gla_qk, n)
                hold(pe, "pe")
                for v in range(levels):
                    for p in range(2):
                        for e in range(2):
                            last = mm(B[3 + e][0:w, 256 * v + P * p:256 * v + P * p + w],
                                      a_dk[64 * e:64 * e + 64, v, P * p:P * p + w],
                                      a_dq[64 * e:64 * e + 64, v, P * p:P * p + w], start=True, stop=True)
                last.then_inc(gla_att, 1)
                for p in range(2):
                    last = pe.transpose(B[5][0:w, P * p:P * p + P], a_dk[:, NLEV, P * p:P * p + w], ident[:, :])
                last.then_inc(gla_kt, 1)

            def gla_values(n, w):
                pe.wait_ge(gla_vst, n)
                hold(pe, "pe")
                for j in range(4):
                    last = pe.transpose(B[6][0:w, P * j:P * j + P], a_v[:, j, 0:w], ident[:, :])
                last.then_inc(gla_vt, 1)

            def gla_sumsq(n):
                pe.wait_ge(gla_sqr, n)
                mm(B[3][:, :], ones[:, :], a_rs, start=True, stop=True).then_inc(gla_ss, 1)

            def gla_step(l, i, fill):
                n = STEPS * l + i + 1
                gla_products(n, P, NLEV)
                fill(0)
                pe.wait_ge(gla_vn, n)
                pe.wait_ge(gla_attm, n)
                if not (isinstance(i, int) and i == 0):
                    pe.wait_ge(gla_oc, NTT * l + i)
                hold(pe, "pe")
                for h in range(4):
                    p, e = h // 2, h % 2
                    mm(B[7][:, P * h:P * h + P], a_vn[:, P * h:P * h + P], a_att[:, 2 * e + p, :], start=True, stop=False)
                    last = mm(B[7][:, P * h:P * h + P], a_S[:, h, :], a_dq[:, NLEV, P * p:P * p + P],
                              start=False, stop=True)
                last.then_inc(gla_o, 1)
                pe.wait_ge(gla_kn, n)
                for p in range(2):
                    last = mm(B[5][:, 256 * p:256 * p + 256], a_kn[:, p, :], a_vn[:, 256 * p:256 * p + 256],
                              start=True, stop=True)
                last.then_inc(gla_st, 1)
                if not (isinstance(i, int) and i == 0):
                    gla_sumsq(n - 1)
                fill(1)
                gla_values(n + 1, NSAMP if isinstance(i, int) and i == NTT - 1 else P)
                fill(2)

            def gla_samples(l):
                n = STEPS * l + STEPS
                w = NSAMP
                gla_sumsq(n - 1)
                pe.wait_ge(gla_rec, n - 1)
                hold(pe, "pe")
                gla_products(n, w, 1)
                pe.wait_ge(gla_vn, n)
                pe.wait_ge(gla_attm, n)
                for h in range(4):
                    p, e = h // 2, h % 2
                    mm(B[7][:, P * h:P * h + w], a_vn[0:w, P * h:P * h + P], a_att[0:w, 2 * e + p, 0:w],
                       start=True, stop=True)
                pe.wait_ge(gla_s0, 16 * (l + 1))
                S0 = sample_states()
                for b in range(NB):
                    pe.wait_ge(gla_km, NB * l + b + 1)
                    for h in range(4):
                        mm(B[6][:, P * h + NS * b:P * h + NS * b + NS], S0[:, b, h, :],
                           a_dq[:, NLEV, P * (h // 2) + NS * b:P * (h // 2) + NS * b + NS], start=True, stop=True)
                    km = (a_km, a_dk[:, 0, :].rearrange("p (a b) -> p a b", a=2))[b % 2]
                    for p in range(2):
                        last = mm(B[(5, 3)[b % 2]][:, 256 * p:256 * p + 256], km[0:w, p, :],
                                  a_vn[0:w, 256 * p:256 * p + 256], start=True, stop=True)
                    last.then_inc(gla_sts, 1)
                pe.wait_ge(gla_sqr, n)
                for h in range(4):
                    last = mm(B[6][:, P * h:P * h + w], ones[:, :], a_rs[:, P * h:P * h + w], start=True, stop=True)
                last.then_inc(gla_ss, 1)

            def fills(l, b, j):
                def fill(k):
                    merge_unit(l, b, j + k // NC, k % NC)
                return fill

            pe.sem_inc(split_free, 4)
            pe.wait_ge(s_const, 16)
            pe.wait_ge(s_ones, 1)
            memory_products()
            pe.wait_ge(mkv_sb, DEPTH)
            pe.wait_ge(x_loaded, 16)
            layer_norm(0)
            with pe.Fori(0, DEPTH) as l:
                dense(l, "in", MEM, g_free_act, ACT_FREES, 0, NC * l)
                pe.wait_ge(loaded[MEM], 32 * (l + 1))
                hold(pe, "pe")
                with pe.Fori(0, NTT // 2) as i:
                    mem_pair(l, i)
                for g in range(2):
                    mem_samples(l, g)
                t = TABLE["z", MEM]
                dense(l, "z", MEM, g_free_dve, DVE_FREES, t["u_z"])
                dense(l, "in", LRU, g_free_act, ACT_FREES, TABLE["in", LRU]["u_in"] + TABLE["in", LRU]["u_merge"])
                for b in range(NBR):
                    merge_start(l, b)
                    if b + 1 == LRU:
                        with pe.Fori(0, 4) as i:
                            for c in range(NC):
                                merge_unit(l, b, 2 * i, c)
                            lru_step(l, i, fills(l, b, 2 * i + 1))
                    if b + 1 == SWA:
                        swa_pair(l, 0, fills(l, b, 0))
                        with pe.Fori(1, NTT // 2) as i:
                            swa_pair(l, i, fills(l, b, 2 * i))
                        swa_samples(l)
                    if b + 1 == SGU:
                        with pe.Fori(0, NTT // 2) as i:
                            sgu_pair(l, i, fills(l, b, 2 * i))
                        sgu_samples(l)
                    if b + 1 == GLA:
                        gla_decays(l)
                        gla_values(STEPS * l + 1, P)
                        gla_step(l, 0, fills(l, b, 0))
                        with pe.Fori(1, NTT - 1) as i:
                            gla_step(l, i, fills(l, b, i))
                        gla_step(l, NTT - 1, fills(l, b, NTT - 1))
                        gla_samples(l)
                    if b + 1 == NBR:
                        with pe.Fori(0, KD) as i:
                            for c in range(NC):
                                merge_unit(l, b, i, c)
                    if b + 1 < NBR:
                        dense(l, "z", b + 1, g_free_dve, DVE_FREES, TABLE["z", b + 1]["u_z"])
                    if b + 2 < NBR:
                        t = TABLE["in", b + 2]
                        dense(l, "in", b + 2, g_free_act, ACT_FREES, t["u_in"] + t["u_merge"])
                    if b + 2 == GLA:
                        gla_rank(l)
                pe.wait_ge(m_ready, l + 1)
                dense(l, "out", 0, g_free_dve, DVE_FREES, TABLE["out", 0]["u_z"])
                pe.wait_ge(g_free_dve, DVE_FREES * (l + 1) + 3)
                layer_norm(l + 1)

        @block.scalar
        def _(act):
            a_ = act.activation

            def load(dst, src, s):
                act.dma_start(dst, src).then_inc(s, 16)

            def layer(src, l):
                names = "abcd"[:len(src.shape) - 2]
                return src[bass.ds(l, 1)].rearrange(f"o p {' '.join(names)} -> p (o {names[0]}) {' '.join(names[1:])}")

            def evac(l, kind, b, n):
                t = TABLE[kind, b]

                def tile(item, slot, s):
                    for c, (a, z) in enumerate(CHUNKS):
                        act.wait_ge(g_full, NG * l + NC * (t["w8"] + item) + c + 1)
                        dst = A[:, slot, a:z] if isinstance(slot, int) else \
                            A[:, bass.ds(slot, 1), a:z].rearrange("p o t -> p (o t)")
                        a_(dst, B[(NC * s + c) % 2][:, 0:z - a], ACT.Copy).then_inc(g_free_act, 1)
                if kind == "rank":
                    tile(0, 8, 0)
                    return
                with act.Fori(0, n // 2) as i:
                    for s in range(2):
                        tile(2 * i + s, 2 * i + s, s)

            def z_tanh(l, b):
                t = TABLE["z", b]
                act.wait_ge(p_free, P_UNITS * l + t["u_merge"] + 2)
                with act.Fori(0, t["n"] // 2) as i:
                    for s in range(2):
                        for c, (a, z) in enumerate(CHUNKS):
                            q = t["u_z"] + 2 * NC * i + NC * s
                            act.wait_ge(g_full, NG * l + NC * (t["w8"] + 2 * i + s) + c + 1)
                            act.wait_ge(y_ready, UNITS["z"] * l + q + (2, 1, 3)[c])
                            a_(th[:, c % 2, 0:z - a], B[(NC * s + c) % 2][:, 0:z - a], ACT.Tanh, scale=0.5)\
                                .then_inc(z_th, 1)

            def merge_start(l, b):
                act.wait_ge(y_ready, UNITS["z"] * l + TABLE["merge", b]["u_z"] + 2)

            def merge_unit(l, b, j, c):
                t = TABLE["merge", b]
                a, z = CHUNKS[c]
                act.wait_ge(g_full, NG * l + NC * (t["w8"] + j) + c + 1)
                act.wait_ge(p_free, P_UNITS * l + t["u_merge"] + NC * j + (2, 1, 3)[c])
                a_(th[:, c % 2, 0:z - a], B[c % 2][:, 0:z - a], ACT.Tanh, scale=0.5).then_inc(g_free_act, 1)

            def fills(l, b, j):
                def fill(k):
                    merge_unit(l, b, j + k // NC, k % NC)
                return fill

            def layer_norm(n):
                for c, (a, z) in enumerate(CHUNKS):
                    act.wait_ge(ln_sum, NC * n + c + 1)
                    a_(ln_m[:, c, 0:z - a], B[3 + c][:, 0:z - a], ACT.Copy, scale=1.0 / D).then_inc(ln_mean, 1)
                for c, (a, z) in enumerate(CHUNKS):
                    act.wait_ge(ln_cent, NC * n + c + 1)
                    a_(A[:, 0:KD, a:z], merged[:, :, a:z], ACT.Square).then_inc(ln_sq, 1)
                for c, (a, z) in enumerate(CHUNKS):
                    act.wait_ge(ln_rec, NC * n + c + 1)
                    a_(ln_v[:, c, 0:z - a], ln_v[:, c, 0:z - a], ACT.Sqrt).then_inc(ln_rstd, 1)
                act.wait_ge(lnp_loaded, 16 * (n + 1))
                for c, (a, z) in enumerate(CHUNKS):
                    act.wait_ge(ln_norm, NC * n + c + 1)
                    for j in range(KD):
                        a_(merged[:, j, a:z], merged[:, j, a:z], ACT.Identity,
                           scale=lnp[:, j:j + 1], bias=lnp[:, KD + j:KD + j + 1])
                    act.drain()
                    a_(xh[:, :, a:z], merged[:, :, a:z], ACT.Copy).then_inc(ln_aff, 1)
                act.wait_ge(ln_aff, NC * (n + 1))
                act.dma_start(d["y"], merged[:, :, :]).then_inc(x_stored, 16)

            def mem_pair(l, i):
                for s in range(2):
                    act.wait_ge(mem_max, 10 * l + 2 * i + s + 1)
                    for m in range(4):
                        last = a_(m_pr[s][:, m, :], B[3 + 2 * s + m // 2][:, 256 * (m % 2):256 * (m % 2) + 256], ACT.Exp,
                                  bias=m_mx[s][:, m:m + 1], scale=HEAD_SCALE, accum_out=m_sum[s][:, m:m + 1])
                    last.then_inc(mem_exp, 1)
                for s in range(2):
                    act.wait_ge(mem_pt, 10 * l + 2 * i + s + 1)
                    a_(m_pt[s][:, 0:4, :].rearrange("p a b -> p (a b)"), B[3 + 2 * s][:, :], ACT.Copy)\
                        .then_inc(mem_pta, 1)

            def mem_samples(l, g):
                n = 10 * l + NTT + g + 1
                act.wait_ge(mem_max, n)
                a_(m_pr[0][:, 0, :], B[5][:, 0:256], ACT.Exp, bias=m_mx[0][:, 0:1], scale=HEAD_SCALE,
                   accum_out=m_sum[0][:, 0:1]).then_inc(mem_exp, 1)
                act.wait_ge(mem_o, n)
                if g == 0:
                    act.dma_start(A[:, 2:6, 0:1024], d["memkv"][bass.ds(NB * l + 4, 4)].rearrange("b p n -> p b n"))\
                        .then_inc(mem_cache, 16)

            def lru_params(l, ct):
                load(l_w[:, :], d["lru"][bass.ds(4 * l + ct, 1)].rearrange("o p n -> p (o n)"), lru_w)

            def lru_step(l, ct, fill):
                n = 4 * l + ct + 1
                act.wait_ge(lru_e, n)
                a_(l_t[:, 1:2], l_t[:, 0:1], ACT.Exp).then_inc(lru_l, 1)
                act.wait_ge(lru_i, n)
                for c, (a, z) in enumerate(CHUNKS):
                    act.wait_ge(lru_ps, 3 * (n - 1) + c + 1)
                    a_(A[:, 5, a:z], B[5][:, 0:z - a], ACT.Tanh, scale=0.5, bias=l_h[:, 0:1])
                    a_(A[:, 6, a:z], B[6][:, 0:z - a], ACT.Tanh, scale=0.5, bias=l_h[:, 1:2]).then_inc(lru_act, 1)
                    fill(c)
                act.drain()
                a_(A[:, 8, :], A[:, 5, :], ACT.Exp, scale=l_s4[:, 0:1], bias=l_s4[:, 0:1])
                a_(A[:, 7, :], A[:, 5, :], ACT.Tanh, scale=l_ns4[:, 0:1], bias=l_ns4[:, 0:1]).then_inc(lru_r, 1)
                act.wait_ge(lru_w2, n)
                a_(A[:, 7, :], A[:, 7, :], ACT.Sqrt).then_inc(lru_sq, 1)
                act.wait_ge(lru_done, n)
                act.dma_start(d["lru_tail"][bass.ds(n - 1, 1)].rearrange("o p n -> p (o n)"), l_tail[:, :])\
                    .then_inc(lru_tail, 16)
                act.wait_ge(lru_tail, 16 * n)

            def swa_exps(s, at, w):
                act.wait_ge(swa_max, at)
                for m in range(4):
                    a_(s_pr[s][:, m, 0:w], s_pr[s][:, m, 0:w], ACT.Exp, bias=s_nm[s][:, m:m + 1], scale=HEAD_SCALE,
                       accum_out=s_sum[s][:, m:m + 1])
                a_(s_es[s][:, :], s_es[s][:, :], ACT.Exp).then_inc(swa_exp, 1)

            def swa_copy(s, at, bank):
                act.wait_ge(swa_pt, at)
                a_(s_pt[s][:, 0:4, :].rearrange("p a b -> p (a b)"), B[bank][:, :], ACT.Copy).then_inc(swa_pta, 1)

            def swa_pair(l, i, fill):
                fill(0)
                for r in range(2):
                    at = (2 * STEPS - 1) * l + 4 * i + 2 * r
                    for s in range(2):
                        swa_exps(s, at + s + 1, 256)
                    fill(1 + 3 * r)
                    for s in range(2):
                        swa_copy(s, at + s + 1, 3 + 2 * s)
                    fill(2 + 3 * r)
                    if r == 0:
                        fill(3)

            def swa_samples(l):
                n = STEPS * l + STEPS
                act.wait_ge(swa_qk, n)
                load(swa_caches(), d["swakv"][bass.ds(l, 1)].rearrange("o p b n -> p (o b) n"), swa_cache)
                out = d["swa_new"][bass.ds(l, 1)].rearrange("o p n -> p (o n)")
                act.dma_start(out[:, 0:P], s_k[:, 2, :]).then_inc(stored, 16)
                act.dma_start(out[:, P:2 * P], A[:, 5, SEQ - P:SEQ]).then_inc(stored, 16)
                act.dma_start(out[:, 2 * P:2 * P + NSAMP], s_k[:, 0, 0:NSAMP]).then_inc(stored, 16)
                act.dma_start(out[:, 2 * P + NSAMP:2 * P + 2 * NSAMP], A[:, 5, SEQ:T]).then_inc(stored, 16)
                m = (2 * STEPS - 1) * (l + 1)
                swa_exps(0, m, 192)
                swa_copy(0, m, 5)

            def sgu_root(s, n, w):
                act.wait_ge(sgu_var, n)
                a_(g_rs[s][0:w, :], g_rs[s][0:w, :], ACT.Sqrt).then_inc(sgu_rstd, 1)

            def sgu_pair(l, i, fill):
                for s in range(2):
                    sgu_root(s, STEPS * l + 2 * i + s + 1, P)
                for k in range(6):
                    fill(k)

            def gla_decays(l):
                for c, (a, z) in enumerate(CHUNKS):
                    w = z - a
                    act.wait_ge(gla_na, NC * l + c + 1)
                    a_(a_e[:, :, 0:w], a_e[:, :, 0:w], ACT.Exp)
                    act.drain()
                    a_(a_e[:, :, 0:w], a_e[:, :, 0:w], ACT.Ln, bias=1.0).then_inc(gla_e, 1)

            def gla_exps(n, w, levels):
                act.wait_ge(gla_d, n)
                for ap in (a_dq, a_dk):
                    for k in range(levels):
                        a_(level(ap, k)[:, :, 0:w], level(ap, k)[:, :, 0:w], ACT.Exp, scale=1.0 / GLA_TAU)
                a_(level(a_dq, NLEV)[:, :, 0:w], a_b[:, :, 0:w], ACT.Exp, scale=1.0 / GLA_TAU)
                a_(level(a_dk, NLEV)[:, :, 0:w], level(a_dk, NLEV)[:, :, 0:w], ACT.Exp, scale=1.0 / GLA_TAU)
                a_(a_dec[:, :], a_dec[:, :], ACT.Exp, scale=1.0 / GLA_TAU).then_inc(gla_ex, 1)

            def gla_rows(n, w):
                act.wait_ge(gla_vt, n)
                a_(a_vn[0:w, :], B[6][0:w, :], ACT.Copy).then_inc(gla_vn, 1)

            def gla_keys(n, w):
                act.wait_ge(gla_kt, n)
                a_(a_kn[0:w, :, :], B[5][0:w, 0:2 * P].rearrange("p (h k) -> p h k", h=2), ACT.Copy).then_inc(gla_kn, 1)

            def gla_squares(l, i):
                act.wait_ge(gla_nd, NTT * l + i + 1)
                a_(a_rs.rearrange("p (h t) -> p h t", h=4), A[:, 4:8, bass.ds(P * i, P)], ACT.Square)\
                    .then_inc(gla_sqr, 1)

            def gla_root(n):
                act.wait_ge(gla_rec, n)
                a_(a_rs, a_rs, ACT.Sqrt).then_inc(gla_rstd, 1)

            def gla_step(l, i, fill):
                n = STEPS * l + i + 1
                first = isinstance(i, int) and i == 0
                w, levels = (NSAMP, 1) if isinstance(i, int) and i == NTT - 1 else (P, NLEV)
                gla_keys(n, P)
                if not first:
                    gla_squares(l, i - 1)
                fill(0)
                act.wait_ge(gla_o, NTT * l + i + 1)
                a_(A[:, 4:8, bass.ds(P * i, P)], B[7][:, :].rearrange("p (h t) -> p h t", h=4), ACT.Copy)\
                    .then_inc(gla_oc, 1)
                fill(1)
                gla_exps(n + 1, w, levels)
                gla_rows(n + 1, w)
                if not first:
                    gla_root(n - 1)
                act.drain()
                fill(2)

            def gla_samples(l):
                n = STEPS * l + STEPS
                w = NSAMP
                act.dma_start(d["gla_p"][bass.ds(l, 1)].rearrange("o p h v -> p (o h) v"), a_S[:, :, :])\
                    .then_inc(stored, 16)
                act.wait_ge(gla_kh, l + 1)
                load(sample_states(), d["gla_s0"][bass.ds(l, 1)].rearrange("o p b h v -> p (o b) h v"), gla_s0)
                gla_squares(l, NTT - 1)
                gla_root(n - 1)
                gla_keys(n, w)
                act.wait_ge(gla_os, l + 1)
                a_(a_rs.rearrange("p (h t) -> p h t", h=4)[:, :, 0:w],
                   a_vn[:, :].rearrange("p (h t) -> p h t", h=4)[:, :, 0:w], ACT.Square).then_inc(gla_sqr, 1)
                act.dma_start(d["gla_s"][bass.ds(l, 1)].rearrange("o p b h v -> p (o b) h v"), sample_states())\
                    .then_inc(gla_s0st, 16)
                gla_root(n)

            def mixer_loads(l, b):
                if b == SWA:
                    load(A[:, 6:8, :], d["rope"], loaded[b])
                    load(s_rot[:, :], d["rot"], loaded[b])
                    load(s_mask, d["swa_mask"], loaded[b])
                    load(s_smask, d["swa_smask"], loaded[b])
                    load(s_sink[:, :], layer(d["sink"], l), loaded[b])
                    load(s_sinkr[:, :], layer(d["sinkr"], l), loaded[b])
                if b == SGU:
                    act.wait_ge(stored, 16 * (5 * l + 4))
                    load(g_lng[:, :], d["sgu_g"][bass.ds(l, 1), :].broadcast_to([P, 512]), loaded[b])
                    load(g_lnb[:, :], d["sgu_b"][bass.ds(l, 1), :].broadcast_to([P, 512]), loaded[b])
                    load(g_w[:, :, :], d["sgu_w"][bass.ds(l, 1)].rearrange("o p g t -> p (o g) t"), loaded[b])
                    load(g_ws[0:NSAMP, :, :], d["sgu_ws"][bass.ds(l, 1)].rearrange("o p g t -> p (o g) t"), loaded[b])
                    load(g_b[:, :, :], d["sgu_bs"][bass.ds(l, 1)].broadcast_to([P, 4, P]), loaded[b])
                    load(g_bs[:, :, :], d["sgu_bss"][bass.ds(l, 1)].broadcast_to([P, 4, NSAMP]), loaded[b])
                    load(g_m[:, :], d["tril"], loaded[b])
                    load(g_ms[0:NSAMP, :], d["tril8"], loaded[b])
                if b == GLA:
                    act.wait_ge(sgu_stored, 16 * (l + 1))
                    load(a_wa[0:16, :], d["wa2"][bass.ds(l, 1)].rearrange("o p n -> p (o n)"), loaded[b])
                    load(a_ba[:, :], layer(d["ba"], l), loaded[b])
                    load(a_ng[:, :], layer(d["ng"], l), loaded[b])
                    load(a_mask, d["gla_mask"], loaded[b])
                    load(a_smask[0:NSAMP, :], d["tril8"], loaded[b])

            act.sem_inc(g_free_act, 3)
            load(ident[:, :], d["ident"], s_const)
            load(A[:, 4:6, :].rearrange("p a t -> p (a t)")[:, 0:2048], d["mem"], mkv_in)
            load(A[:, 0:4, :].rearrange("p a t -> p (a t)")[:, 0:4096], d["w_mem"][0], mkv_in)
            load(merged[:, :, :], d["x"], x_loaded)
            load(lnp[:, :], d["lnp"][0], lnp_loaded)
            act.dma_start(d["swa_old_k"], d["cache_k"][:, :, NS:, :]).then_inc(swa_old, 16)
            act.dma_start(d["swa_old_v"], d["cache_v"][:, :, NS:, :]).then_inc(swa_old, 16)
            for l in range(DEPTH):
                act.wait_ge(mkv_ps, l + 1)
                if l:
                    act.wait_ge(mkv_out, 16 * l)
                else:
                    load(A[:, 0:4, :].rearrange("p a t -> p (a t)")[:, 0:4096], d["w_mem"][1], mkv_in)
                a_(A[:, 6, 0:512], B[5][:, :], ACT.Copy)
                a_(A[:, 6, 512:1024], B[6][:, :], ACT.Copy).then_inc(mkv_sb, 1)
                act.wait_ge(mkv_sb, l + 1)
                act.dma_start(d["mkv"][l], A[:, 6, 0:1024]).then_inc(mkv_out, 16)
            act.wait_ge(mkv_out, 16 * DEPTH)
            layer_norm(0)
            with act.Fori(0, DEPTH) as l:
                act.wait_ge(ln_var, NC * (l + 1))
                act.wait_ge(x_ready, NC * (l + 1))
                load(lnp[:, :], d["lnp"][bass.ds(l + 1, 1)].rearrange("o p n -> p (o n)"), lnp_loaded)
                load(A[:, 6, 0:1024], d["mkv"][bass.ds(l, 1)].rearrange("o p n -> p (o n)"), loaded[MEM])
                load(A[:, 2:6, 0:1024], d["memkv"][bass.ds(NB * l, 4)].rearrange("b p n -> p b n"), loaded[MEM])
                evac(l, "in", MEM, 2)
                with act.Fori(0, NTT // 2) as i:
                    mem_pair(l, i)
                for g in range(2):
                    mem_samples(l, g)
                z_tanh(l, MEM)
                act.wait_ge(y_ready, UNITS["z"] * l + TABLE["in", LRU]["u_z"] + 2)
                evac(l, "in", LRU, IN_TILES[LRU])
                for b in range(NBR):
                    merge_start(l, b)
                    if b + 1 == LRU:
                        with act.Fori(0, 4) as i:
                            lru_params(l, i)
                            for c in range(NC):
                                merge_unit(l, b, 2 * i, c)
                            lru_step(l, i, fills(l, b, 2 * i + 1))
                    if b + 1 == SWA:
                        swa_pair(l, 0, fills(l, b, 0))
                        with act.Fori(1, NTT // 2) as i:
                            swa_pair(l, i, fills(l, b, 2 * i))
                        swa_samples(l)
                    if b + 1 == SGU:
                        with act.Fori(0, NTT // 2) as i:
                            sgu_pair(l, i, fills(l, b, 2 * i))
                        sgu_root(0, STEPS * (l + 1), NSAMP)
                        act.wait_ge(sgu_vn, STEPS * (l + 1))
                        act.dma_start(d["sgu_v"][bass.ds(l, 1)].rearrange("o p n -> p (o n)"), g_vn[0][0:NSAMP, :])\
                            .then_inc(sgu_stored, 16)
                    if b + 1 == GLA:
                        gla_decays(l)
                        gla_exps(STEPS * l + 1, P, NLEV)
                        gla_rows(STEPS * l + 1, P)
                        gla_step(l, 0, fills(l, b, 0))
                        with act.Fori(1, NTT - 1) as i:
                            gla_step(l, i, fills(l, b, i))
                        gla_step(l, NTT - 1, fills(l, b, NTT - 1))
                        gla_samples(l)
                    if b + 1 == NBR:
                        with act.Fori(0, KD) as i:
                            for c in range(NC):
                                merge_unit(l, b, i, c)
                    if b + 1 < NBR:
                        z_tanh(l, b + 1)
                        act.wait_ge(y_ready, UNITS["z"] * l + TABLE["z", b + 1]["u_z"] + NC * Y_TILES[b + 1] + 2)
                    if b + 2 < NBR:
                        mixer_loads(l, b + 2)
                        evac(l, "in", b + 2, IN_TILES[b + 2])
                    if b + 2 == GLA:
                        evac(l, "rank", GLA, 1)
                    if b + 1 == GLA:
                        act.wait_ge(gla_s0st, 16 * (l + 1))
                        act.wait_ge(stored, 16 * 5 * (l + 1))
                        act.wait_ge(x_stored, 16 * (l + 1))
                        load(A[:, 0:KD, :], d["y"], res_loaded)
                layer_norm(l + 1)
            act.wait_ge(x_stored, 16 * (DEPTH + 1))
            act.wait_ge(stored, 16 * 5 * DEPTH)
            act.wait_ge(gla_s0st, 16 * DEPTH)
            act.wait_ge(sgu_stored, 16 * DEPTH)
            act.wait_ge(lru_tail, 16 * 4 * DEPTH)
            act.wait_ge(mkv_out, 16 * DEPTH)
            act.wait_ge(swa_old, 32)

        @block.vector
        def _(v):
            tt, ts, stt, cp = v.tensor_tensor, v.tensor_scalar, v.scalar_tensor_tensor, v.tensor_copy

            def inputs_ready(l, kind, b):
                t = TABLE[kind, b]
                v.wait_ge(g_free_act, ACT_FREES * l + t["u_in"] + t["u_merge"] + NC * t["n"] + 3)
                hold(v, "dve")

            def z_phase(l, b):
                t = TABLE["z", b]

                def tile(item, slot, s):
                    for c, (a, z) in enumerate(CHUNKS):
                        w = z - a
                        o = A[:, bass.ds(OUT_SLOT[b] + slot, 1), a:z].rearrange("p o t -> p (o t)")
                        hi = yh[:, bass.ds(slot, 1), a:z].rearrange("p o t -> p (o t)")
                        lo = yl[:, bass.ds(slot, 1), a:z].rearrange("p o t -> p (o t)")
                        v.wait_ge(z_th, UNITS["z"] * l + t["u_z"] + NC * item + c + 1)
                        stt(tm[:, 0:w], th[:, c % 2, 0:w], 1.0, B[(NC * s + c) % 2][:, 0:w], ALU.add, ALU.mult)\
                            .then_inc(g_free_dve, 1)
                        v.drain()
                        stt(tm2[:, 0:w], tm[:, 0:w], 0.5, o, ALU.mult, ALU.mult)
                        v.drain()
                        cp(hi, tm2[:, 0:w])
                        v.drain()
                        tt(lo, tm2[:, 0:w], hi.bitcast(F32), ALU.subtract).then_inc(y_ready, 1)
                        v.drain()
                with v.Fori(0, t["n"] // 2) as i:
                    for s in range(2):
                        tile(2 * i + s, 2 * i + s, s)

            def merge_unit(l, b, j, c):
                t = TABLE["merge", b]
                a, z = CHUNKS[c]
                w = z - a
                q = NC * j + c
                m = merged[:, bass.ds(j, 1), a:z].rearrange("p o t -> p (o t)")
                v.wait_ge(g_free_act, ACT_FREES * l + t["u_in"] + t["u_merge"] + q + 4)
                v.wait_ge(p_full, P_UNITS * l + t["u_merge"] + q + 1)
                pb = B[2][:, 0:w]
                if b == MEM:
                    stt(m, th[:, c % 2, 0:w], 1.0, pb, ALU.add, ALU.mult).then_inc(p_free, 1)
                else:
                    stt(tm[:, 0:w], th[:, c % 2, 0:w], 1.0, pb, ALU.add, ALU.mult).then_inc(p_free, 1)
                    v.drain()
                    tt(m, m, tm[:, 0:w], ALU.add)
                    v.drain()

            def fills(l, b, j):
                def fill(k):
                    merge_unit(l, b, j + k // NC, k % NC)
                return fill

            def layer_norm(n):
                for c, (a, z) in enumerate(CHUNKS):
                    v.wait_ge(ln_mean, NC * n + c + 1)
                    tt(merged[:, :, a:z], merged[:, :, a:z], bc(ln_m[:, c, 0:z - a], KD), ALU.subtract)\
                        .then_inc(ln_cent, 1)
                for c, (a, z) in enumerate(CHUNKS):
                    v.wait_ge(ln_var, NC * n + c + 1)
                    ts(ln_v[:, c, 0:z - a], B[(6, 7, 3)[c]][:, 0:z - a], 1.0 / D, LN_EPS, ALU.mult, ALU.add)
                    v.drain()
                    v.reciprocal(ln_v[:, c, 0:z - a], ln_v[:, c, 0:z - a]).then_inc(ln_rec, 1)
                for c, (a, z) in enumerate(CHUNKS):
                    v.wait_ge(ln_rstd, NC * n + c + 1)
                    tt(merged[:, :, a:z], merged[:, :, a:z], bc(ln_v[:, c, 0:z - a], KD), ALU.mult)\
                        .then_inc(ln_norm, 1)
                for c, (a, z) in enumerate(CHUNKS):
                    v.wait_ge(ln_aff, NC * n + c + 1)
                    tt(xl[:, :, a:z], merged[:, :, a:z], xh[:, :, a:z].bitcast(F32), ALU.subtract)\
                        .then_inc(x_ready, 1)

            def mem_pair(l, i):
                tok = lambda s: bass.ds(2 * P * i + P * s, P)
                n = lambda s: 10 * l + 2 * i + s + 1
                for s in range(2):
                    cp(m_q[s][:, :, :], A[:, 0:2, tok(s)]).then_inc(mem_q, 1)
                for s in range(2):
                    v.wait_ge(mem_scores, n(s))
                    for e in range(2):
                        v.tensor_reduce(m_mx[s][:, 2 * e:2 * e + 2],
                                        B[3 + 2 * s + e][:, :].rearrange("p (m s) -> p m s", m=2), AX_X, ALU.max)
                    v.drain()
                    ts(m_mx[s][:, :], m_mx[s][:, :], -HEAD_SCALE, None, ALU.mult).then_inc(mem_max, 1)
                for s in range(2):
                    v.wait_ge(mem_exp, n(s))
                    v.reciprocal(m_sum[s][:, :], m_sum[s][:, :])
                    v.drain()
                    tt(m_pr[s][:, :, :], m_pr[s][:, :, :], bl(m_sum[s][:, :], 256), ALU.mult).then_inc(mem_prob, 1)
                for s in range(2):
                    v.wait_ge(mem_pt, n(s))
                    cp(m_pt[s][:, 4:8, :].rearrange("p a b -> p (a b)"), B[4 + 2 * s][:, :]).then_inc(mem_ptd, 1)
                v.wait_ge(mem_o, n(1))
                hold(v, "dve")
                for s in range(2):
                    cp(A[:, 0:2, tok(s)], B[7][:, 256 * s:256 * s + 256].rearrange("p (m t) -> p m t", m=2))
                v.drain()

            def mem_samples(l, g):
                n = 10 * l + NTT + g + 1
                if g == 0:
                    for p in range(2):
                        for e in range(2):
                            r = slice(64 * e, 64 * e + 64)
                            h = 2 * p + e
                            last = cp(m_qbd[r, p, :, NS * h:NS * h + NS],
                                      A[r, p, SEQ:T].rearrange("p (b t) -> p b t", b=NB))
                    last.then_inc(mem_q, 1)
                else:
                    v.sem_inc(mem_q, 1)
                v.wait_ge(mem_scores, n)
                v.reduce_max(m_mx[0][:, 0:1], B[5][:, 0:256], AX_X)
                v.drain()
                ts(m_mx[0][:, 0:1], m_mx[0][:, 0:1], -HEAD_SCALE, None, ALU.mult).then_inc(mem_max, 1)
                v.wait_ge(mem_exp, n)
                v.reciprocal(m_sum[0][:, 0:1], m_sum[0][:, 0:1])
                v.drain()
                ts(m_pr[0][:, 0, :], m_pr[0][:, 0, :], m_sum[0][:, 0:1], None, ALU.mult).then_inc(mem_prob, 1)
                v.wait_ge(mem_pt, n)
                cp(m_pt[0][:, 0:2, :].rearrange("p a b -> p (a b)"), B[6][:, 0:256]).then_inc(mem_ptd, 1)
                v.wait_ge(mem_o, n)
                hold(v, "dve")
                for p in range(2):
                    for e in range(2):
                        r = slice(64 * e, 64 * e + 64)
                        h = 2 * p + e
                        cp(A[r, p, SEQ + 32 * g:SEQ + 32 * g + 32].rearrange("p (b t) -> p b t", b=4),
                           B[7][r, P * p:P * p + P].rearrange("p (b h t) -> p b h t", b=4, h=4)[:, :, h, :])
                v.drain()

            def lru_step(l, ct, fill):
                n = 4 * l + ct + 1
                X = A[:, bass.ds(ct, 1), :].rearrange("p o t -> p (o t)")
                xc = A[:, 4, :]
                col = lambda k: l_w[:, k:k + 1]
                v.wait_ge(lru_w, 16 * n)
                stt(l_t[:, 0:1], col(LW_LAM), -1.0, col(LW_LAM), ALU.mult, ALU.min).then_inc(lru_e, 1)
                ts(xc[:, 0:SEQ], X[:, 0:SEQ], col(LW_CW + 3), col(LW_CB), ALU.mult, ALU.add)
                cp(l_pad[:, :, 0:3], l_w[:, LW_CONV:LW_CONV + 3 * NB].rearrange("p (b j) -> p b j", b=NB))
                cp(l_pad[:, :, 3:11], X[:, SEQ:T].rearrange("p (b t) -> p b t", b=NB))
                cp(l_tail[:, 9:12], X[:, SEQ - 3:SEQ])
                cp(l_tail[:, 12:36].rearrange("p (b j) -> p b j", b=NB),
                   X[:, SEQ:T].rearrange("p (b t) -> p b t", b=NB)[:, :, NS - 3:NS])
                xs = xc[:, SEQ:T].rearrange("p (b t) -> p b t", b=NB)
                v.drain()
                ts(xs, l_pad[:, :, 3:11], col(LW_CW + 3), col(LW_CB), ALU.mult, ALU.add)
                for j in (2, 1, 0):
                    k = 3 - j
                    v.drain()
                    stt(xc[:, k:SEQ], X[:, 0:SEQ - k], col(LW_CW + j), xc[:, k:SEQ], ALU.mult, ALU.add)
                    last = stt(xs, l_pad[:, :, j:j + NS], col(LW_CW + j), xs, ALU.mult, ALU.add)
                last.then_inc(lru_conv, 1)
                v.wait_ge(lru_l, n)
                ts(l_t[:, 2:3], l_t[:, 1:2], 2.0, None, ALU.add)
                ts(l_h[:, :], l_w[:, LW_BR:LW_BR + 2], 0.5, None, ALU.mult)
                v.drain()
                v.reciprocal(l_t[:, 2:3], l_t[:, 2:3])
                v.drain()
                tt(l_t[:, 3:4], l_t[:, 1:2], l_t[:, 2:3], ALU.mult)
                v.drain()
                tt(l_t[:, 4:5], l_t[:, 3:4], l_t[:, 3:4], ALU.mult)
                v.drain()
                ts(l_t[:, 5:6], l_t[:, 4:5], 1.0 / 17, 1.0 / 15, ALU.mult, ALU.add)
                for k in (13, 11, 9, 7, 5, 3, 1):
                    v.drain()
                    ts(l_t[:, 5:6], l_t[:, 5:6], l_t[:, 4:5], None, ALU.mult)
                    v.drain()
                    ts(l_t[:, 5:6], l_t[:, 5:6], 1.0 / k, None, ALU.add)
                v.drain()
                stt(l_t[:, 6:7], l_t[:, 3:4], 2.0, l_t[:, 5:6], ALU.mult, ALU.mult)
                v.drain()
                stt(l_t[:, 7:8], col(LW_LAM), 0.0, l_t[:, 6:7], ALU.min, ALU.subtract)
                v.drain()
                ts(l_s4[:, :], l_t[:, 7:8], 4.0, None, ALU.mult)
                ts(l_ns4[:, :], l_t[:, 7:8], -4.0, None, ALU.mult).then_inc(lru_i, 1)
                for c in range(NC):
                    fill(c)
                v.wait_ge(lru_r, n)
                tt(A[:, 5, :], A[:, 8, :], A[:, 8, :], ALU.mult)
                v.drain()
                stt(A[:, 7, :], A[:, 5, :], 1.0, A[:, 7, :], ALU.add, ALU.mult).then_inc(lru_w2, 1)
                stt(A[:, 6, :], A[:, 6, :], 1.0, xc, ALU.add, ALU.mult)
                cp(l_ab[:, :, 1:9], A[:, 8, SEQ:T].rearrange("p (b t) -> p b t", b=NB))
                v.memset(l_ab[:, :, 0:1], 0.0)
                cp(l_ub[:, :, 0:1], l_w[:, LW_H0:LW_H0 + NB].rearrange("p (b o) -> p b o", o=1))
                v.drain()
                v.wait_ge(lru_sq, n)
                stt(A[:, 7, :], A[:, 6, :], 0.5, A[:, 7, :], ALU.mult, ALU.mult)
                v.drain()
                cp(l_ub[:, :, 1:9], A[:, 7, SEQ:T].rearrange("p (b t) -> p b t", b=NB))
                v.tensor_tensor_scan(X[:, 0:SEQ], A[:, 8, 0:SEQ], A[:, 7, 0:SEQ], 0.0, ALU.mult, ALU.add)
                v.drain()
                v.tensor_tensor_scan(l_hb[:, :, :].rearrange("p b t -> p (b t)"), l_ab[:, :, :].rearrange("p b t -> p (b t)"),
                                     l_ub[:, :, :].rearrange("p b t -> p (b t)"), 0.0, ALU.mult, ALU.add)
                v.drain()
                cp(X[:, SEQ:T].rearrange("p (b t) -> p b t", b=NB), l_hb[:, :, 1:9])
                cp(l_tail[:, 0:1], X[:, SEQ - 1:SEQ])
                cp(l_tail[:, 1:9].rearrange("p (b o) -> p b o", o=1), l_hb[:, :, 8:9]).then_inc(lru_done, 1)
                v.drain()

            def swa_rotate(s, n, tok, w):
                kk = s_k[:, s + 1, :] if w == P else s_k[:, 0, 0:w]
                C = A[:, 6, tok]
                S = A[:, 7, tok]
                tq, tk = s_tq[s], s_tk[s]
                v.wait_ge(swa_rot, n)
                tt(s_q[s][:, :, 0:w], A[:, 0:4, tok], bc(C, 4), ALU.mult)
                tt(tq[:, :, 0:w], B[3 + 2 * s][:, 0:4 * w].rearrange("p (m t) -> p m t", m=4), bc(S, 4), ALU.mult)
                tt(kk, A[:, 4, tok], C, ALU.mult)
                tt(tk[:, 0:w], B[4 + 2 * s][:, 0:w], S, ALU.mult)
                cp(s_vn[0:w, s + 1, :], B[4 + 2 * s][0:w, P:2 * P])
                v.drain()
                tt(s_q[s][:, :, 0:w], s_q[s][:, :, 0:w], tq[:, :, 0:w], ALU.add)
                last = tt(kk, kk, tk[:, 0:w], ALU.add)
                if w == P:
                    last.then_inc(swa_qk, 1)
                    return
                v.drain()
                for e in range(2):
                    r = slice(64 * e, 64 * e + 64)
                    last = cp(s_qbd[r, :, 32 * e:32 * e + 32].rearrange("p b (i t) -> p b i t", i=4),
                              s_q[s][r, :, 0:w].rearrange("p i (b t) -> p b i t", b=NB))
                last.then_inc(swa_qk, 1)

            def swa_maxima(s, w, sink):
                v.drain()
                v.tensor_reduce(s_mx[s][:, :], s_pr[s][:, :, 0:w], AX_X, ALU.max)
                v.drain()
                stt(s_mx[s][:, :], s_mx[s][:, :], HEAD_SCALE, sink, ALU.mult, ALU.max)
                v.drain()
                ts(s_nm[s][:, :], s_mx[s][:, :], -1.0, None, ALU.mult)
                tt(s_es[s][:, :], sink, s_mx[s][:, :], ALU.subtract).then_inc(swa_max, 1)

            def swa_normalise(s, at, w):
                v.wait_ge(swa_exp, at)
                tt(s_sum[s][:, :], s_sum[s][:, :], s_es[s][:, :], ALU.add)
                v.drain()
                v.reciprocal(s_sum[s][:, :], s_sum[s][:, :])
                v.drain()
                tt(s_pr[s][:, :, 0:w], s_pr[s][:, :, 0:w], bl(s_sum[s][:, :], w), ALU.mult).then_inc(swa_prob, 1)

            def swa_pair(l, i, fill):
                tok = lambda s: bass.ds(2 * P * i + P * s, P)
                start = isinstance(i, int)
                if start:
                    v.memset(s_vn[:, 0, :], 0.0)
                    v.memset(s_k[:, 0, :], 0.0)
                else:
                    cp(s_vn[:, 0, :], s_vn[:, 2, :])
                    cp(s_k[:, 0, :], s_k[:, 2, :])
                for s in range(2):
                    cp(s_v[s][:, 0:P], A[:, 5, tok(s)]).then_inc(swa_vst, 1)
                v.drain()
                for s in range(2):
                    swa_rotate(s, STEPS * l + 2 * i + s + 1, tok(s), P)
                fill(0)
                for r in range(2):
                    at = (2 * STEPS - 1) * l + 4 * i + 2 * r
                    for s in range(2):
                        v.wait_ge(swa_scores, at + s + 1)
                        for e in range(2):
                            sc = B[3 + 2 * s + e][:, :].rearrange("p (m s) -> p m s", m=2)
                            pr = s_pr[s][:, 2 * e:2 * e + 2, :]
                            if start and s == 0:
                                v.memset(pr[:, :, 0:P], NEG)
                                tt(pr[:, :, P:2 * P], sc[:, :, P:2 * P], bc(s_mask[:, P:2 * P], 2), ALU.add)
                            else:
                                tt(pr, sc, bc(s_mask, 2), ALU.add)
                        swa_maxima(s, 2 * P, s_sink[:, 4 * r:4 * r + 4])
                    for s in range(2):
                        swa_normalise(s, at + s + 1, 2 * P)
                    fill(1 + 3 * r)
                    for s in range(2):
                        v.wait_ge(swa_pt, at + s + 1)
                        cp(s_pt[s][:, 4:8, :].rearrange("p a b -> p (a b)"), B[4 + 2 * s][:, :]).then_inc(swa_ptd, 1)
                    fill(2 + 3 * r)
                    v.wait_ge(swa_o, at + 2)
                    hold(v, "dve")
                    for s in range(2):
                        cp(A[:, 2 * r:2 * r + 2, tok(s)],
                           B[7][:, 256 * s:256 * s + 256].rearrange("p (m t) -> p m t", m=2))
                    v.drain()
                    if r == 0:
                        fill(3)

            def swa_samples(l):
                n = STEPS * (l + 1)
                m = (2 * STEPS - 1) * (l + 1)
                w = NSAMP
                cp(s_v[0][:, 0:w], A[:, 5, SEQ:T])
                v.memset(s_qbd[:, :, :], 0.0).then_inc(swa_vst, 1)
                v.drain()
                swa_rotate(0, n, slice(SEQ, T), w)
                v.wait_ge(swa_scores, m)
                for g in range(2):
                    tt(s_pr[0][:, 2 * g:2 * g + 2, 0:192], B[5 + g][:, :].rearrange("p (u s) -> p u s", u=2)[:, :, 0:192],
                       s_smask[:, 2 * g:2 * g + 2, :], ALU.add)
                swa_maxima(0, 192, s_sinkr[:, 0:1].broadcast_to([P, 4]))
                swa_normalise(0, m, 192)
                v.wait_ge(swa_pt, m)
                cp(s_pt[0][0:w, 4:8, :].rearrange("p a b -> p (a b)"), B[6][0:w, :]).then_inc(swa_ptd, 1)
                v.wait_ge(swa_o, m)
                for e in range(2):
                    r = slice(64 * e, 64 * e + 64)
                    cp(A[r, 0:4, SEQ:T].rearrange("p i (b t) -> p b i t", b=NB),
                       B[7][r, :].rearrange("p (b h t) -> p b h t", b=NB, h=8)[:, :, 4 * e:4 * e + 4, :])
                v.drain()

            def sgu_norm(s, n, w):
                rows = B[3 + 2 * s][0:w, :]
                v.wait_ge(sgu_vt, n)
                v.bn_stats(g_bn[s][0:w, :], rows)
                v.drain()
                v.bn_aggr(g_mv[s][0:w, :], g_bn[s][0:w, :])
                v.drain()
                ts(g_rs[s][0:w, :], g_mv[s][0:w, 1:2], LN_EPS, None, ALU.add)
                v.drain()
                v.reciprocal(g_rs[s][0:w, :], g_rs[s][0:w, :]).then_inc(sgu_var, 1)

            def sgu_affine(s, n, w):
                v.wait_ge(sgu_rstd, n)
                vn = g_vn[s][0:w, :]
                ts(vn, B[3 + 2 * s][0:w, :], g_mv[s][0:w, 0:1], g_rs[s][0:w, :], ALU.subtract, ALU.mult)
                v.drain()
                tt(vn, vn, g_lng[0:w, :], ALU.mult)
                v.drain()
                tt(vn, vn, g_lnb[0:w, :], ALU.add).then_inc(sgu_vn, 1)

            def sgu_gate(s, n, w, tok):
                v.wait_ge(sgu_mix, n)
                vs = g_vs[s][:, 0:4 * w].rearrange("p (g t) -> p g t", g=4)
                tt(vs, B[4 + 2 * s][:, 0:4 * w].rearrange("p (g t) -> p g t", g=4),
                   g_b[:, :, :] if w == P else g_bs[:, :, :], ALU.add)
                v.drain()
                tt(A[:, 0:4, tok], A[:, 0:4, tok], vs, ALU.mult)

            def sgu_pair(l, i, fill):
                tok = lambda s: bass.ds(2 * P * i + P * s, P)
                n = lambda s: STEPS * l + 2 * i + s + 1
                for s in range(2):
                    cp(g_v[s][:, :, :], A[:, 4:8, tok(s)]).then_inc(sgu_vst, 1)
                for s in range(2):
                    sgu_norm(s, n(s), P)
                for s in range(2):
                    sgu_affine(s, n(s), P)
                for k in range(3):
                    fill(k)
                for s in range(2):
                    sgu_gate(s, n(s), P, tok(s))
                for k in range(3, 6):
                    fill(k)
                v.drain()

            def sgu_samples(l):
                n = STEPS * (l + 1)
                w = NSAMP
                cp(g_v[0][:, :, 0:w], A[:, 4:8, SEQ:T]).then_inc(sgu_vst, 1)
                sgu_norm(0, n, w)
                sgu_affine(0, n, w)
                sgu_gate(0, n, w, slice(SEQ, T))
                v.drain()

            def ref(w, block, pos):
                s = a_b[:, :, 0:w].rearrange("p h (m t) -> p h m t", t=block)
                return s[:, :, :, pos:pos + 1].broadcast_to([P, 2, w // block, block])

            def blocks(ap, w, block):
                return ap[:, :, 0:w].rearrange("p h (m t) -> p h m t", t=block)

            def gla_decays(l):
                for c, (a, z) in enumerate(CHUNKS):
                    w = z - a
                    v.wait_ge(gla_x, NC * l + c + 1)
                    for p in range(2):
                        ts(a_x[:, p, 0:w], B[3 + p][:, 0:w], a_ba[:, p:p + 1], None, ALU.add)
                    v.drain()
                    stt(a_e[:, :, 0:w], a_x[:, :, 0:w], -1.0, a_x[:, :, 0:w], ALU.mult, ALU.min).then_inc(gla_na, 1)
                    v.wait_ge(gla_e, NC * l + c + 1)
                    for p, la in enumerate((A[:, 8, a:z], a_la[:, a:z])):
                        stt(la, a_x[:, p, 0:w], 0.0, a_e[:, p, 0:w], ALU.min, ALU.subtract)
                    v.drain()

            def gla_front(n, w, tok, levels, one, block):
                cp(a_v[:, :, 0:w], A[:, 4:8, tok]).then_inc(gla_vst, 1)
                v.tensor_tensor_scan(a_b[:, 0, 0:w], one, A[:, 8, tok], 0.0, ALU.mult, ALU.add)
                v.tensor_tensor_scan(a_b[:, 1, 0:w], one, a_la[:, tok], 0.0, ALU.mult, ALU.add)
                v.drain()
                for k, (size, pos) in enumerate(levels):
                    tt(blocks(level(a_dq, k), w, size), blocks(a_b, w, size), ref(w, size, pos), ALU.subtract)
                tt(blocks(level(a_dk, NLEV), w, block), ref(w, block, block - 1), blocks(a_b, w, block), ALU.subtract)
                m = w // block
                cp(a_dec[:, 0:2 * m].rearrange("p (h m o) -> p h m o", h=2, o=1),
                   blocks(a_b, w, block)[:, :, :, block - 1:block])
                v.drain()
                for k in range(len(levels)):
                    q, kk = level(a_dq, k)[:, :, 0:w], level(a_dk, k)[:, :, 0:w]
                    ts(kk, q, -1.0, CLAMP, ALU.mult, ALU.min)
                v.drain()
                for k in range(len(levels)):
                    q = level(a_dq, k)[:, :, 0:w]
                    last = ts(q, q, CLAMP, None, ALU.min)
                last.then_inc(gla_d, 1)

            def gla_scale(n, w, tok, levels):
                v.wait_ge(gla_ex, n)
                for k in [*range(levels), NLEV]:
                    q, kk = level(a_dq, k)[:, :, 0:w], level(a_dk, k)[:, :, 0:w]
                    stt(q, A[:, 0:2, tok], HEAD_SCALE, q, ALU.mult, ALU.mult)
                    last = tt(kk, A[:, 2:4, tok], kk, ALU.mult)
                last.then_inc(gla_qk, 1)

            def gla_attention(n, w, k, mask):
                v.wait_ge(gla_att, n)
                hold(v, "dve")
                ps = [B[3 + e][0:w, :].rearrange("p (k h t) -> p k h t", k=2, h=2)[:, :, :, 0:w] for e in range(2)]
                if k:
                    for e in range(2):
                        cp(a_att[0:HALF, 2 * e:2 * e + 2, HALF:w], ps[e][0:HALF, 0, :, HALF:w])
                    v.drain()
                for e in range(2):
                    last = v.copy_predicated(a_att[0:w, 2 * e:2 * e + 2, 0:w], bc(mask, 2).bitcast(U32), ps[e][:, k])
                last.then_inc(gla_attm, 1)

            four = lambda ap, w: ap.rearrange("p (h t) -> p h t", h=4)[:, :, 0:w]

            def gla_variance(n, w, bank):
                v.wait_ge(gla_ss, n)
                ts(four(a_rs, w), four(B[bank][:, :], w), 1.0 / P, RMS_EPS, ALU.mult, ALU.add)
                v.drain()
                v.reciprocal(four(a_rs, w), four(a_rs, w)).then_inc(gla_rec, 1)

            def gla_norm(n, i):
                v.wait_ge(gla_rstd, n)
                o = A[:, 4:8, bass.ds(P * i, P)]
                stt(o, o, a_ng[:, 0:1], four(a_rs, P), ALU.mult, ALU.mult).then_inc(gla_nd, 1)

            def gla_sample_front(l):
                v.memset(a_att[:, :, :], 0.0)
                v.memset(a_reset, 1.0)
                v.drain()
                v.memset(a_reset.rearrange("p (b t) -> p b t", t=NS)[:, :, 0:1], 0.0)
                v.drain()
                gla_front(STEPS * (l + 1), NSAMP, slice(SEQ, T), [(NS, NS // 2 - 1)], a_reset, NS)

            def gla_sample_scale(l):
                v.wait_ge(gla_ex, STEPS * (l + 1))
                hold(v, "dve")
                for k in (0, NLEV):
                    q, kk = level(a_dq, k)[:, :, 0:NSAMP], level(a_dk, k)[:, :, 0:NSAMP]
                    stt(q, A[:, 0:2, SEQ:T], HEAD_SCALE, q, ALU.mult, ALU.mult)
                    last = tt(kk, A[:, 2:4, SEQ:T], kk, ALU.mult)
                last.then_inc(gla_qk, 1)
                v.drain()
                v.sem_inc(gla_kh, 1)

            def gla_step(l, i, fill):
                n = STEPS * l + i + 1
                after = bass.ds(P * i + P, P)
                first = isinstance(i, int) and i == 0
                final = isinstance(i, int) and i == NTT - 1
                gla_attention(n, P, 1, a_mask)
                fill(0)
                v.wait_ge(gla_st, NTT * l + i + 1)
                hold(v, "dve")
                for h in range(4):
                    p, e = h // 2, h % 2
                    r = slice(64 * e, 64 * e + 64)
                    stt(a_S[r, h, :], a_S[r, h, :], a_dec[r, p:p + 1],
                        B[5][r, 256 * p + P * e:256 * p + P * e + P], ALU.mult, ALU.add)
                v.drain()
                if final:
                    gla_sample_front(l)
                else:
                    gla_front(n + 1, P, after, LEVELS, ones[:, :], P)
                fill(1)
                if not first:
                    gla_variance(n - 1, P, 3)
                if final:
                    gla_sample_scale(l)
                else:
                    gla_scale(n + 1, P, after, NLEV)
                fill(2)
                if not first:
                    gla_norm(n - 1, i - 1)
                v.drain()

            def gla_samples(l):
                n = STEPS * l + STEPS
                w = NSAMP
                tok = slice(SEQ, T)
                gla_variance(n - 1, P, 3)
                gla_norm(n - 1, NTT - 1)
                v.drain()
                gla_attention(n, w, 0, a_smask[0:w, :])
                v.wait_ge(gla_kn, n)
                S0 = sample_states()
                for b in range(NB):
                    km = (a_km, level(a_dk, 0))[b % 2]
                    ts(km[0:w, :, :], a_kn[0:w, :, :], a_smask[0:w, NS * b + NS - 1:NS * b + NS], None, ALU.mult).then_inc(gla_km, 1)
                    if b == 0:
                        v.wait_ge(gla_s0, 16 * (l + 1))
                        hold(v, "dve")
                    if b:
                        gla_sample_update(l, S0, b - 1)
                gla_sample_update(l, S0, NB - 1)
                cp(four(a_rs, w), four(B[6][:, :], w))
                v.drain()
                tt(four(a_vn, w), four(B[7][:, :], w), four(a_rs, w), ALU.add).then_inc(gla_os, 1)
                gla_variance(n, w, 6)
                v.wait_ge(gla_rstd, n)
                stt(A[:, 4:8, tok], four(a_vn, w), a_ng[:, 0:1], four(a_rs, w), ALU.mult, ALU.mult)
                v.drain()

            def gla_sample_update(l, S0, b):
                v.wait_ge(gla_sts, NB * l + b + 1)
                for h in range(4):
                    p, e = h // 2, h % 2
                    r = slice(64 * e, 64 * e + 64)
                    stt(S0[r, b, h, :], S0[r, b, h, :], a_dec[r, NB * p + b:NB * p + b + 1],
                        B[(5, 3)[b % 2]][r, 256 * p + P * e:256 * p + P * e + P], ALU.mult, ALU.add)

            v.sem_inc(g_free_dve, 3)
            v.sem_inc(p_free, 2)
            v.sem_inc(y_ready, 2)
            v.sem_inc(gla_nd, 1)
            layer_norm(0)
            with v.Fori(0, DEPTH) as l:
                v.memset(m_qbd[:, :, :, :], 0.0)
                v.drain()
                inputs_ready(l, "in", MEM)
                with v.Fori(0, NTT // 2) as i:
                    mem_pair(l, i)
                for g in range(2):
                    mem_samples(l, g)
                z_phase(l, MEM)
                inputs_ready(l, "in", LRU)
                v.wait_ge(x_stored, 16 * (l + 1))
                hold(v, "dve")
                for b in range(NBR):
                    if b + 1 == LRU:
                        with v.Fori(0, 4) as i:
                            for c in range(NC):
                                merge_unit(l, b, 2 * i, c)
                            lru_step(l, i, fills(l, b, 2 * i + 1))
                    if b + 1 == SWA:
                        swa_pair(l, 0, fills(l, b, 0))
                        with v.Fori(1, NTT // 2) as i:
                            swa_pair(l, i, fills(l, b, 2 * i))
                        swa_samples(l)
                    if b + 1 == SGU:
                        tt(g_w[:, :, :], g_w[:, :, :], bc(g_m[:, :], 4), ALU.mult)
                        tt(g_ws[0:NSAMP, :, :], g_ws[0:NSAMP, :, :], bc(g_ms[0:NSAMP, :], 4), ALU.mult)
                        v.drain()
                        with v.Fori(0, NTT // 2) as i:
                            sgu_pair(l, i, fills(l, b, 2 * i))
                        sgu_samples(l)
                    if b + 1 == GLA:
                        v.memset(a_S[:, :, :], 0.0)
                        v.memset(a_att[:, :, :], 0.0)
                        v.memset(a_dec[:, :], 0.0)
                        v.drain()
                        gla_decays(l)
                        gla_front(STEPS * l + 1, P, slice(0, P), LEVELS, ones[:, :], P)
                        gla_scale(STEPS * l + 1, P, slice(0, P), NLEV)
                        gla_step(l, 0, fills(l, b, 0))
                        with v.Fori(1, NTT - 1) as i:
                            gla_step(l, i, fills(l, b, i))
                        gla_step(l, NTT - 1, fills(l, b, NTT - 1))
                        gla_samples(l)
                    if b + 1 == NBR:
                        with v.Fori(0, KD) as i:
                            for c in range(NC):
                                merge_unit(l, b, i, c)
                    if b + 1 < NBR:
                        z_phase(l, b + 1)
                    if b + 2 < NBR:
                        inputs_ready(l, "in", b + 2)
                        if b + 2 == GLA:
                            inputs_ready(l, "rank", GLA)
                        v.wait_ge(loaded[b + 2], 16 * LOADS[b + 2] * (l + 1))
                        hold(v, "dve")
                v.drain()
                for j in range(KD):
                    ts(xh[:, j, :], merged[:, j, :], 0.5, None, ALU.mult)
                v.drain()
                for j in range(KD):
                    last = stt(xl[:, j, :], merged[:, j, :], 0.5, xh[:, j, :].bitcast(F32), ALU.mult, ALU.subtract)
                last.then_inc(m_ready, 1)
                v.drain()
                t = TABLE["out", 0]
                v.wait_ge(res_loaded, 16 * (l + 1))
                hold(v, "dve")
                with v.Fori(0, KD // 2) as i:
                  for s in range(2):
                    for c, (a, z) in enumerate(CHUNKS):
                        v.wait_ge(g_full, NG * l + NC * (t["w8"] + 2 * i + s) + c + 1)
                        one = lambda ap: ap[:, bass.ds(2 * i + s, 1), a:z].rearrange("p o t -> p (o t)")
                        stt(one(merged), one(A), DN_ALPHA, B[(NC * s + c) % 2][:, 0:z - a], ALU.mult, ALU.add).then_inc(g_free_dve, 1)
                layer_norm(l + 1)


OFF = dict(gq=0, gk=256, gv=512, glr=1024, gz=1040, lx=1552, lz=2064, sq=2576, sk=3088, sv=3216, sz=3344,
           su=3856, svv=4368, suz=4880, mq=5392, mz=5648, gates=5904)


def feature_tiles():
    import numpy as np
    span = lambda name, n: [np.arange(OFF[name] + P * i, OFF[name] + P * i + P) for i in range(n)]
    pairs = lambda name: [np.concatenate([np.arange(OFF[name] + 64 * h, OFF[name] + 64 * h + 64) for h in (i, 4 + i)])
                          for i in range(4)]
    inputs = [span("mq", 2), span("lx", 4), pairs("sq") + span("sk", 1) + span("sv", 1),
              span("su", 4) + span("svv", 4), span("gq", 2) + span("gk", 2) + span("gv", 4)]
    zs = [span("mz", 2), span("lz", 4), pairs("sz"), span("suz", 4), span("gz", 4)]
    tiles = []
    for kind, b, n in PHASES:
        if kind == "in":
            tiles += inputs[b]
        if kind == "z":
            tiles += zs[b]
        if kind == "rank":
            tiles.append(np.arange(OFF["glr"], OFF["glr"] + 16))
        if kind == "merge":
            g = OFF["gates"] + D * GATE_OF[b]
            tiles += [np.arange(g + P * j, g + P * j + P) for j in range(KD)]
        if kind == "out":
            tiles += [None] * KD
    return tiles


def constants():
    import numpy as np
    f = np.float32
    i, j = np.arange(P)[:, None], np.arange(P)[None, :]
    c = dict(ident=np.eye(P, dtype=f), tril=(i <= j).astype(f))
    a, b = np.arange(NSAMP)[:, None], np.arange(NSAMP)[None, :]
    c["tril8"] = ((a // NS == b // NS) & (a <= b)).astype(f)
    c["gla_mask"] = ((i // HALF == j // HALF) & (i <= j)).astype(f)
    c["swa_mask"] = np.concatenate([np.where(j >= i, 0, NEG), np.where(j <= i, 0, NEG)], axis=1).astype(f)
    sm = np.zeros((P, 4, P + NSAMP), f)
    for row in range(P):
        t = row % NS
        for u in range(4):
            seq = 2 * u + row // 64
            sm[row, u, :P] = np.where(np.arange(P) >= t, 0, NEG)
            sm[row, u, P:] = np.where((b[0] // NS == seq) & (b[0] % NS <= t), 0, NEG)
    c["swa_smask"] = sm
    rot = np.zeros((P, P), f)
    dd = np.arange(P)
    for m in dd[dd % 64 < 8]:
        rot[m + 8, m] = 1
        rot[m, m + 8] = 1
    c["rot"] = rot
    pos = np.concatenate([np.arange(SEQ), np.tile(2048 + np.arange(NS), NB)]).astype(f)
    inv = (f(500000.0) ** (-np.arange(8, dtype=f) / f(8))).astype(f)
    ang = (pos[None, :] * inv[:, None]).astype(f)
    rope = np.zeros((P, 2, T), f)
    rope[:, 0] = 1
    for base in (0, 64):
        rope[base:base + 8, 0] = rope[base + 8:base + 16, 0] = np.cos(ang.astype(np.float64))
        rope[base:base + 8, 1] = -np.sin(ang.astype(np.float64))
        rope[base + 8:base + 16, 1] = np.sin(ang.astype(np.float64))
    c["rope"] = rope
    return c


def kernel(**inputs):
    import numpy as np
    import concourse.bacc as bacc
    from concourse.bass_utils import run_bass_kernel_spmd

    g = {k: np.asarray(v) for k, v in inputs.items()}
    f = np.float32
    arrays = constants()

    def feature_major(x):
        return x.T.reshape(-1, P, x.shape[0]).transpose(1, 0, 2)

    def subtiles(w):
        return w.reshape(-1, P, w.shape[1]).transpose(1, 0, 2)

    arrays["x"] = feature_major(np.concatenate([g["x_prompt"][0], g["x_sample"].reshape(NSAMP, D)]))
    arrays["mem"] = feature_major(g["mem_prompt"][0]).reshape(P, -1)
    arrays["w_mem"] = np.stack([subtiles(w).reshape(P, -1) for w in g["w_mem_kv"]])
    tiles = feature_tiles()
    w8 = np.zeros((DEPTH, N8, P, KD, P), f)
    w4 = np.zeros((DEPTH, N4, P, 4, P), f)
    swa_rows = np.concatenate([np.arange(64 * h, 64 * h + 64) for i in range(4) for h in (i, 4 + i)])
    for l in range(DEPTH):
        win, wout = subtiles(g["w_in"][l]), subtiles(g["w_out"][l])
        j = 0
        for n, cols in enumerate(tiles):
            if cols is None:
                w8[l, n] = wout[:, :, P * j:P * j + P]
                j += 1
            else:
                w8[l, n, :, :, :len(cols)] = win[:, :, cols]
        for b in range(NBR):
            wbr = g["w_branch_mem"][l] if b == MEM else g["w_branch"][l, GATE_OF[b]]
            if b == SWA:
                wbr = wbr[swa_rows]
            for j in range(KD):
                w4[l, KD * b + j, :, :Y_TILES[b]] = subtiles(wbr)[:, :, P * j:P * j + P]
    arrays["w8"] = w8.reshape(DEPTH * N8, P, -1)
    arrays["w4"] = w4.reshape(DEPTH * N4, P, -1)

    def columns(v):
        return v.reshape(-1, P).T

    lnp = [np.concatenate([columns(g["ln_in_g"]), columns(g["ln_in_b"])], axis=1)]
    lnp += [np.concatenate([columns(g["ln_g"][l]), columns(g["ln_b"][l])], axis=1) for l in range(DEPTH)]
    arrays["lnp"] = np.stack(lnp)

    K, V = g["cache_mem_k"], g["cache_mem_v"]
    kt = K.transpose(0, 1, 3, 4, 2).reshape(DEPTH * NB, 2, P, N_MEM).transpose(0, 2, 1, 3)
    vv = V.reshape(DEPTH * NB, 2, P, 256).transpose(0, 2, 1, 3)
    arrays["memkv"] = np.concatenate([kt.reshape(-1, P, 512), vv.reshape(-1, P, 512)], axis=2)
    K, V = g["cache_swa_k"], g["cache_swa_v"]
    kt = K.transpose(0, 3, 4, 1, 2).reshape(DEPTH, P, NB, WINDOW)
    vv = V.reshape(DEPTH, NB, WINDOW, P).transpose(0, 2, 1, 3)
    arrays["swakv"] = np.concatenate([kt, vv], axis=3)
    arrays["cache_k"] = K.reshape(DEPTH, NB, WINDOW, P)
    arrays["cache_v"] = V.reshape(DEPTH, NB, WINDOW, P)
    sinks = g["swa_sinks"]
    order = [4 * e + 2 * r + m for r in range(2) for e in range(2) for m in range(2)]
    arrays["sink"] = np.broadcast_to(sinks[:, None, order], (DEPTH, P, 8))
    arrays["sinkr"] = sinks[:, (np.arange(P) % 64) // NS][:, :, None]

    arrays["sgu_g"], arrays["sgu_b"] = g["sgu_ln_g"], g["sgu_ln_b"]
    wt = g["sgu_w"].transpose(0, 3, 1, 2)
    arrays["sgu_w"] = wt
    ws = np.zeros((DEPTH, NB, NS, 4, NB, NS), f)
    for b in range(NB):
        ws[:, b, :, :, b, :] = wt[:, :NS, :, :NS]
    arrays["sgu_ws"] = ws.reshape(DEPTH, NSAMP, 4, NSAMP)
    arrays["sgu_bs"] = g["sgu_b"]
    arrays["sgu_bss"] = np.tile(g["sgu_b"][:, :, :NS], (1, 1, NB))

    arrays["wa2"] = g["gla_wa2"]
    arrays["ba"] = np.stack([columns(v) for v in g["gla_ba"]])
    arrays["ng"] = g["gla_norm_g"][:, :, None]
    s0 = np.zeros((DEPTH, P, NB, 4, P), f)
    for h in range(4):
        r = 64 * (h % 2)
        s0[:, r:r + 64, :, h] = g["state_gla"][:, :, h].transpose(0, 2, 1, 3)
    arrays["gla_s0"] = s0

    lru = np.zeros((DEPTH, 4, P, LW_N), f)
    for l in range(DEPTH):
        for ct in range(4):
            for e in range(2):
                r = slice(64 * e, 64 * e + 64)
                lru[l, ct, r, LW_WR + 64 * e:LW_WR + 64 * e + 64] = g["lru_wr"][l, 2 * ct + e]
                lru[l, ct, r, LW_WI + 64 * e:LW_WI + 64 * e + 64] = g["lru_wi"][l, 2 * ct + e]
            ch = slice(P * ct, P * ct + P)
            lru[l, ct, :, LW_CW:LW_CW + 4] = g["lru_conv_w"][l, :, ch].T
            for at, name in ((LW_CB, "lru_conv_b"), (LW_BR, "lru_br"), (LW_BI, "lru_bi"), (LW_LAM, "lru_L")):
                lru[l, ct, :, at] = g[name][l, ch]
            lru[l, ct, :, LW_H0:LW_H0 + NB] = g["state_lru_h"][l, :, ch].T
            lru[l, ct, :, LW_CONV:] = g["state_lru_conv"][l, :, :, ch].transpose(2, 0, 1).reshape(P, -1)
    arrays["lru"] = lru.reshape(DEPTH * 4, P, LW_N)

    outs = dict(y=(P, KD, T), mkv=(DEPTH, P, 1024), lru_tail=(DEPTH * 4, P, NTAIL),
                swa_new=(DEPTH, P, 2 * P + 2 * NSAMP), swa_old_k=(DEPTH, NB, WINDOW - NS, P),
                swa_old_v=(DEPTH, NB, WINDOW - NS, P), gla_p=(DEPTH, P, 4, P), gla_s=(DEPTH, P, NB, 4, P),
                sgu_v=(DEPTH, NSAMP, 512))
    nc = bacc.Bacc("TRN2", target_bir_lowering=False, num_devices=1)
    d, feed = {}, {}
    for name, a in arrays.items():
        feed["in_" + name] = np.ascontiguousarray(a)
        d[name] = nc.dram_tensor("in_" + name, a.shape, mybir.dt.from_np(a.dtype), kind="ExternalInput").ap()
    for name, shape in outs.items():
        d[name] = nc.dram_tensor("out_" + name, shape, F32, kind="ExternalOutput").ap()
    build(nc, d)
    got = run_bass_kernel_spmd(nc, [feed], core_ids=[0]).results[0]
    o = {name: np.asarray(got["out_" + name]) for name in outs}

    y = o["y"].transpose(1, 0, 2).reshape(D, T).T
    half = lambda h: slice(64 * (h % 2), 64 * (h % 2) + 64)
    gla_p = np.stack([o["gla_p"][:, half(h), h] for h in range(4)], axis=1)[:, None]
    gla_s = np.stack([o["gla_s"][:, half(h), :, h].transpose(0, 2, 1, 3) for h in range(4)], axis=2)
    tail = o["lru_tail"].reshape(DEPTH, 512, NTAIL)
    lru_p, lru_s = tail[:, :, 0][:, None], tail[:, :, 1:9].transpose(0, 2, 1)
    conv = tail[:, :, 9:].reshape(DEPTH, 512, 9, 3).transpose(0, 2, 3, 1)
    new = o["swa_new"]

    def window(at, n):
        return new[:, :, at:at + n].transpose(0, 2, 1)

    def swa_prompt(at):
        return window(at, P).reshape(DEPTH, 1, WINDOW, 2, 64)

    def swa_sample(at, old):
        return np.concatenate([old, window(at, NSAMP).reshape(DEPTH, NB, NS, P)], axis=2)\
            .reshape(DEPTH, NB, WINDOW, 2, 64)

    mk = o["mkv"][:, :, :512].reshape(DEPTH, P, 2, N_MEM).transpose(0, 3, 2, 1).reshape(DEPTH, 1, N_MEM, 4, 64)
    mv = o["mkv"][:, :, 512:].reshape(DEPTH, P, 2, 256).transpose(0, 2, 1, 3).reshape(DEPTH, 1, N_MEM, 4, 64)
    result = (y[:SEQ].reshape(1, SEQ, D), y[SEQ:].reshape(NB, NS, D), gla_p, gla_s, lru_p, lru_s,
              conv[:, 0:1], conv[:, 1:], swa_prompt(0), swa_sample(2 * P, o["swa_old_k"]),
              swa_prompt(P), swa_sample(2 * P + NSAMP, o["swa_old_v"]), mk, mv,
              o["sgu_v"].reshape(DEPTH, NB, NS, 512))
    return tuple(np.ascontiguousarray(a) for a in result)
```

```python
from contextlib import ExitStack

import concourse.bass as bass
from concourse import mybir

F32 = mybir.dt.float32
F32R = mybir.dt.float32r
BF16 = mybir.dt.bfloat16
U32 = mybir.dt.uint32
ALU = mybir.AluOpType
ACT = mybir.ActivationFunctionType
AX_X = mybir.AxisListType.X

P = 128
D = 1024
SEQ = 1024
DEPTH = 2
NB = 8
NS = 8
NSAMP = NB * NS
T = SEQ + NSAMP
KD = D // P
NTT = SEQ // P
STEPS = NTT + 1
CHUNKS = [(0, 364), (364, 728), (728, T)]
NC = len(CHUNKS)
CW = CHUNKS[0][1]
N_MEM = 256
WINDOW = 128
LN_EPS = 1e-5
RMS_EPS = 1e-6
DN_ALPHA = (2 * DEPTH) ** 0.25
HEAD_SCALE = 64 ** -0.5
GLA_TAU = 16.0
NEG = -1.0e30
CLAMP = 80.0 * GLA_TAU

MEM, LRU, SWA, SGU, GLA = range(5)
IN_TILES = [2, 4, 6, 8, 8]
Y_TILES = [2, 4, 4, 4, 4]
GATE_OF = [4, 1, 2, 3, 0]
OUT_SLOT = [0, 0, 0, 0, 4]
LOADS = [2, 0, 6, 8, 5]
NBR = 5

PHASES = [("in", 0, 2), ("in", 1, 4), ("z", 0, 2)]
for _b in range(NBR):
    PHASES.append(("merge", _b, KD))
    if _b + 1 < NBR:
        PHASES.append(("z", _b + 1, Y_TILES[_b + 1]))
    if _b + 2 < NBR:
        PHASES.append(("in", _b + 2, IN_TILES[_b + 2]))
    if _b + 2 == GLA:
        PHASES.append(("rank", GLA, 1))
PHASES.append(("out", 0, KD))


def phase_table():
    table, w8, w4, ring = {}, 0, 0, 0
    units = {"in": 0, "z": 0, "merge": 0, "out": 0}
    for kind, b, n in PHASES:
        table[kind, b] = dict(w8=w8, w4=w4, ring=ring, n=n, **{f"u_{k}": v for k, v in units.items()})
        w8 += n
        ring += n
        if kind in ("merge", "rank"):
            w4 += n if kind == "merge" else 0
            ring += n
        units["in" if kind == "rank" else kind] += NC * n
    return table, w8, w4, ring, units


TABLE, N8, N4, NRING, UNITS = phase_table()
NG = NC * N8
ACT_FREES = UNITS["in"] + UNITS["merge"]
DVE_FREES = UNITS["z"] + UNITS["out"]
TH_UNITS = UNITS["z"] + UNITS["merge"]
P_UNITS = UNITS["merge"]

HALF = P // 2
LEVELS = [(P, HALF - 1), (HALF, HALF // 2 - 1)]
NLEV = len(LEVELS)

LW_WR, LW_WI, LW_CW, LW_CB, LW_BR, LW_BI, LW_LAM, LW_H0, LW_CONV = 0, 128, 256, 260, 261, 262, 263, 264, 272
LW_N = LW_CONV + 3 * NB
NTAIL = 9 + 27


def build(nc, d):
    with ExitStack() as ctx:
        def sb(name, shape, dt=F32):
            return ctx.enter_context(nc.sbuf_tensor(name, shape, dt))

        def sem(name):
            return ctx.enter_context(nc.semaphore(name))

        xh = sb("xh", [P, KD, T], F32R)
        xl = sb("xl", [P, KD, T], BF16)
        yh = sb("yh", [P, 4, T], F32R)
        yl = sb("yl", [P, 4, T], BF16)
        merged = sb("merged", [P, KD, T])
        A = sb("arena", [P, 9, T])
        raw = sb("w_raw", [P, 2, D])
        wh = sb("w_hi", [P, 2, KD, P], F32R)
        wl = sb("w_lo", [P, 2, KD, P], F32R)
        wb = sb("w_bf", [P, 2, KD, P], BF16)
        ident = sb("ident", [P, P])
        ones = sb("ones", [P, P])
        th = sb("th", [P, 2, CW])
        tm = sb("tm", [P, CW])
        tm2 = sb("tm2", [P, CW])
        lnp = sb("lnp", [P, 2 * KD])
        WK = sb("mixer_space", [P, 6208])
        B = [ctx.enter_context(nc.psum_tensor(f"bank{i}", [P, 512], F32)) for i in range(8)]

        s_const = sem("const_loaded")
        s_ones = sem("ones_set")
        z_th = sem("z_tanh_ready")
        mem_cache = sem("mem_cache_loaded")
        raw_full = [sem(f"raw_full{s}") for s in range(2)]
        raw_free = sem("raw_free")
        split_full = sem("split_full")
        split_free = sem("split_free")
        g_full = sem("gate_bank_full")
        g_free_act = sem("gate_bank_free_act")
        g_free_dve = sem("gate_bank_free_dve")
        p_full = sem("branch_bank_full")
        p_free = sem("branch_bank_free")
        y_ready = sem("y_ready")
        x_high = sem("x_high_part")
        x_ready = sem("x_ready")
        merged_sum = sem("merged_summed")
        merged_high = sem("merged_high_part")
        m_ready = sem("merged_split")
        x_loaded = sem("x_loaded")
        x_stored = sem("x_stored")
        res_loaded = sem("residual_loaded")
        lnp_loaded = sem("ln_params_loaded")
        ln_sum = sem("ln_sum")
        ln_mean = sem("ln_mean")
        ln_cent = sem("ln_centered")
        ln_sq = sem("ln_squares")
        ln_var = sem("ln_var")
        ln_rec = sem("ln_reciprocal")
        ln_rstd = sem("ln_rstd")
        ln_norm = sem("ln_normalised")
        ln_aff = sem("ln_affine")
        mkv_in = sem("mkv_inputs")
        mkv_ps = sem("mkv_product")
        mkv_sb = sem("mkv_copied")
        mkv_out = sem("mkv_stored")
        loaded = [sem(f"mixer{b}_loaded") for b in range(NBR)]
        stored = sem("states_stored")

        s_held = {e: sem(f"held_{e}") for e in ("pe", "dve", "pool")}

        def hold(eng, name):
            eng.sem_inc(s_held[name], 1)

        def carve():
            at = [0]

            def take(*dims):
                n = 1
                for x in dims:
                    n *= x
                ap = WK[:, at[0]:at[0] + n]
                at[0] += n
                assert at[0] <= 6208, at[0]
                if len(dims) == 2:
                    ap = ap.rearrange("p (a b) -> p a b", a=dims[0])
                if len(dims) == 3:
                    ap = ap.rearrange("p (a b c) -> p a b c", a=dims[0], b=dims[1])
                return ap
            return take

        def bc(ap, n):
            return ap.unsqueeze(1).broadcast_to([ap.shape[0], n, ap.shape[1]])

        def bl(ap, n):
            return ap.unsqueeze(2).broadcast_to([ap.shape[0], ap.shape[1], n])

        take = carve()
        m_q = [take(2, P) for _ in range(2)]
        m_pr = [take(4, 256) for _ in range(2)]
        m_pt = [take(8, P) for _ in range(2)]
        m_mx = [take(4) for _ in range(2)]
        m_sum = [take(4) for _ in range(2)]
        m_qbd = take(2, NB, 32)

        def m_cache(g, b):
            return A[:, 2 + b, 0:1024] if g == 0 else merged[:, b, 0:1024]
        mem_q, mem_scores, mem_max, mem_exp, mem_prob, mem_pt, mem_pta, mem_ptd, mem_o = (
            sem(f"mem_{x}") for x in ("q_staged", "scores", "max", "exp", "prob", "pt", "pt_act", "pt_dve", "o"))

        take = carve()
        s_q = [take(4, P) for _ in range(2)]
        s_k = take(3, P)
        s_vn = take(3, P)
        s_pr = [take(4, 256) for _ in range(2)]
        s_pt = [take(8, P) for _ in range(2)]
        s_tq = [x[:, 0:2, :].rearrange("p a b -> p (a b)").rearrange("p (a b) -> p a b", a=4) for x in s_pr]
        s_tk = [x[:, 2, 0:P] for x in s_pr]
        s_v = [x[:, 0, :] for x in s_pt]
        s_qbd = s_pr[1].rearrange("p a b -> p (a b)")[:, 0:NB * NSAMP].rearrange("p (b h) -> p b h", b=NB)
        s_mx = [take(4) for _ in range(2)]
        s_nm = [take(4) for _ in range(2)]
        s_es = [take(4) for _ in range(2)]
        s_sum = [take(4) for _ in range(2)]
        s_sink = take(8)
        s_sinkr = take(1)
        s_rot = take(P)
        s_tab = take(2, NSAMP)
        s_mask = A[:, 8, 0:2 * P]
        s_smask = A[:, 8, 2 * P:2 * P + 4 * 192].rearrange("p (u s) -> p u s", u=4)
        (swa_vst, swa_rot, swa_qk, swa_scores, swa_max, swa_exp, swa_prob, swa_pt, swa_pta, swa_ptd, swa_o,
         swa_cache, swa_old) = (
            sem(f"swa_{x}") for x in ("v_staged", "rotated", "qk", "scores", "max", "exp", "prob", "pt", "pt_act",
                                      "pt_dve", "o", "cache_loaded", "window_stored"))

        take = carve()
        take(5136)
        l_w = take(LW_N)
        l_s4 = take(1)
        l_ns4 = take(1)
        l_h = take(2)
        l_t = take(8)
        l_pad = take(NB, 11)
        l_ab = take(NB, 9)
        l_ub = take(NB, 9)
        l_hb = take(NB, 9)
        l_tail = take(NTAIL)
        (lru_w, lru_e, lru_l, lru_conv, lru_r, lru_i, lru_ps, lru_act, lru_w2, lru_sq, lru_done, lru_tail) = (
            sem(f"lru_{x}") for x in ("params", "exp_lam", "exp_lam_done", "conv", "decays_exp", "decay", "gates_ps",
                                      "gates_act", "radicand", "root", "done", "tail_stored"))

        take = carve()
        g_v = [take(4, P) for _ in range(2)]
        g_vn = [take(512) for _ in range(2)]
        g_vs = [take(512) for _ in range(2)]
        g_bn = [take(6) for _ in range(2)]
        g_mv = [take(2) for _ in range(2)]
        g_rs = [take(1) for _ in range(2)]
        g_lng = take(512)
        g_lnb = take(512)
        g_w = take(4, P)
        g_b = take(4, P)
        g_ws = take(4, NSAMP)
        g_bs = take(4, NSAMP)
        g_m = take(P)
        g_ms = take(NSAMP)
        (sgu_vst, sgu_vt, sgu_var, sgu_rstd, sgu_vn, sgu_mix, sgu_stored) = (
            sem(f"sgu_{x}") for x in ("v_staged", "v_transposed", "var", "rstd", "v_normed", "mixed", "v_stored"))

        take = carve()
        a_v = take(4, P)
        a_vn = take(512)
        a_la = take(T)
        a_b = take(2, P)
        a_dq = take(NLEV + 1, 2 * P)
        a_dk = take(NLEV + 1, 2 * P)
        a_x = a_dq.rearrange("p a b -> p (a b)")[:, 0:2 * CW].rearrange("p (a b) -> p a b", a=2)
        a_e = a_dk.rearrange("p a b -> p (a b)")[:, 0:2 * CW].rearrange("p (a b) -> p a b", a=2)
        a_wa = take(2 * P)
        a_kn = a_wa.rearrange("p (a b) -> p a b", a=2)
        a_km = take(2, P)
        a_att = take(4, P)
        a_S = take(4, P)
        a_rs = take(512)
        a_dec = take(16)
        a_ba = take(2)
        a_ng = take(1)
        a_mask = take(P)
        a_smask = take(NSAMP)
        a_reset = a_km.rearrange("p a b -> p (a b)")[:, 0:NSAMP]
        (gla_vst, gla_vt, gla_x, gla_na, gla_e, gla_la, gla_d, gla_ex, gla_qk, gla_att, gla_attm, gla_vn, gla_o, gla_oc,
         gla_sqr, gla_ss, gla_rec, gla_rstd, gla_kh, gla_kt, gla_kn, gla_st, gla_s0, gla_s0st, gla_km, gla_sts,
         gla_os, gla_nd) = (
            sem(f"gla_{x}") for x in ("v_staged", "v_transposed", "pre", "negabs", "softplus", "log_decay", "exponents",
                                      "exps", "qk", "products", "att", "v_rows", "o", "o_copied", "squares", "sumsq",
                                      "rec", "rstd", "k_hat", "k_transposed", "k_rows", "state_ps", "states_loaded",
                                      "states_stored", "k_masked", "sample_update", "sample_o", "normalised"))

        take = carve()
        ln_m = take(NC, CW)
        ln_v = take(NC, CW)

        def memory_weights():
            return xl[:, :, :].rearrange("p a t -> p (a t)")[:, 0:8192].bitcast(F32).rearrange("p (k n) -> p k n", k=KD)

        def memory_inputs():
            return WK[:, 4096:6144].rearrange("p (k s) -> p k s", k=KD)

        def swa_caches():
            return A[:, 6:8, :].rearrange("p a t -> p (a t)")[:, 0:NB * 2 * P].rearrange("p (b n) -> p b n", b=NB)

        def sample_states():
            return A[:, 0:4, :].rearrange("p a t -> p (a t)")[:, 0:NB * 4 * P].rearrange(
                "p (b h v) -> p b h v", b=NB, h=4)

        def level(ap, k):
            return ap[:, k, :].rearrange("p (h t) -> p h t", h=2)

        block = ctx.enter_context(nc.Block())

        def ring_items(kind, b, n):
            if kind == "merge":
                return n, (KD, Y_TILES[b])
            if kind == "rank":
                return 1, (KD, 0)
            return n // 2, (KD, KD)

        @block.sync
        def _(sp):
            with sp.Fori(0, DEPTH) as l:
                for kind, b, n in PHASES:
                    t = TABLE[kind, b]
                    pairs, subs = ring_items(kind, b, n)
                    per = 2 if kind in ("in", "z", "out") else 1
                    with sp.Fori(0, pairs) as i:
                        for s in range(2):
                            sp.wait_ge(raw_free, NRING * l + t["ring"] + 2 * i + s + 1)
                            if kind == "merge" and s == 1:
                                src = d["w4"][bass.ds(N4 * l + t["w4"] + i, 1), :, 0:subs[1] * P]
                            else:
                                m = max(subs[s] * P, 16)
                                src = d["w8"][bass.ds(N8 * l + t["w8"] + per * i + (s if per == 2 else 0), 1), :, 0:m]
                            w = src.shape[2]
                            sp.dma_start(raw[:, s, 0:w], src.rearrange("o p n -> p (o n)")).then_inc(raw_full[s], 16)

        @block.gpsimd
        def _(g):
            g.memset(ones[:, :], 1.0).then_inc(s_ones, 1)
            g.sem_inc(raw_free, 2)
            def split(l, t, i, s, m, used, count):
                tile = NRING * l + t["ring"] + 2 * i + s
                g.wait_ge(raw_full[s], 16 * (NRING // 2 * l + t["ring"] // 2 + i + 1))
                g.wait_ge(split_free, 2 * tile + 1)
                hold(g, "pool")
                if m:
                    r = raw[:, s, 0:m * P]
                    h = wh[:, s, 0:m, :].rearrange("p k n -> p (k n)")
                    lo = wl[:, s, 0:m, :].rearrange("p k n -> p (k n)")
                    bf = wb[:, s, 0:m, :].rearrange("p k n -> p (k n)")
                    g.tensor_scalar(h, r, 1.0, 1.0, ALU.mult, ALU.mult).then_inc(split_full, 1)
                    g.drain()
                    g.wait_ge(split_free, 2 * tile + 2)
                    hold(g, "pool")
                    g.tensor_tensor(lo, r, h.bitcast(F32), ALU.subtract).then_inc(split_full, 1)
                    g.wait_ge(used, count)
                    hold(g, "pool")
                    g.tensor_scalar(bf, r, 1.0, 1.0, ALU.mult, ALU.mult).then_inc(split_full, 1)
                    g.drain()
                else:
                    g.wait_ge(split_free, 2 * tile + 2)
                    g.sem_inc(split_full, 3)
                g.sem_inc(raw_free, 1)

            def in_phase(kind, l, t, s, i):
                if kind == "merge":
                    return (p_full, P_UNITS * l + t["u_merge"] + NC * (i + 1)) if s else \
                        (g_full, NG * l + NC * (t["w8"] + i + 1))
                if kind == "rank":
                    return g_full, NG * l + NC * (t["w8"] + 1)
                return g_full, NG * l + NC * (t["w8"] + 2 * i + s + 1)

            with g.Fori(0, DEPTH) as l:
                before = None
                for kind, b, n in PHASES:
                    t = TABLE[kind, b]
                    pairs, subs = ring_items(kind, b, n)
                    for s in range(2):
                        last = (g_free_dve, DVE_FREES * l + 3) if before is None else \
                            in_phase(before[0], l, TABLE[before[:2]], s, ring_items(*before)[0] - 1)
                        split(l, t, 0, s, subs[s], *last)
                    if pairs > 1:
                        with g.Fori(1, pairs) as i:
                            for s in range(2):
                                split(l, t, i, s, subs[s], *in_phase(kind, l, t, s, i - 1))
                    before = (kind, b, n)

        @block.tensor
        def _(pe):
            mm = pe.matmul

            def product(bank, s, nk, c, hi, lo, tile, low=None):
                a, z = CHUNKS[c]
                out = bank[:, 0:z - a]
                passes = [(wh, hi), (wl, hi), (wb, lo)]
                for part, (w, x) in enumerate(passes):
                    if c == 0:
                        pe.wait_ge(split_full, 3 * tile + part + 1)
                    if part == 2 and low is not None:
                        hold(pe, "pe")
                        pe.wait_ge(x_ready, low)
                        hold(pe, "pe")
                    for k in range(nk):
                        last = mm(out, w[:, s, k, :], x[:, k, a:z], start=(part == 0 and k == 0),
                                  stop=(part == 2 and k == nk - 1))
                    if c == NC - 1 and part < 2:
                        last.then_inc(split_free, 1)
                return last

            def dense_start(l, kind, b, free, per, base):
                t = TABLE[kind, b]
                other = (g_free_dve, DVE_FREES, t["u_z"] + t["u_out"]) if free is g_free_act else \
                    (g_free_act, ACT_FREES, t["u_in"] + t["u_merge"])
                pe.wait_ge(other[0], other[1] * l + other[2] + 3)
                hold(pe, "pe")
                pe.wait_ge(free, per * l + base + 3)
                hold(pe, "pe")

            def dense_unit(l, kind, b, free, per, base, i, s, c, low=None):
                pe.wait_ge(free, per * l + base + 2 * NC * i + NC * s + c + 2)
                product(B[(NC * s + c) % 2], s, KD, c, xh, xl, NRING * l + TABLE[kind, b]["ring"] + 2 * i + s, low)\
                    .then_inc(g_full, 1)

            def dense(l, kind, b, free, per, base, ready=None):
                dense_start(l, kind, b, free, per, base)
                with pe.Fori(0, TABLE[kind, b]["n"] // 2) as i:
                    for s in range(2):
                        for c in range(NC):
                            low = None
                            if ready is not None and s == 0:
                                pe.wait_ge(x_high, ready + c + 1)
                                hold(pe, "pe")
                                low = ready + c + 1
                            dense_unit(l, kind, b, free, per, base, i, s, c, low)

            def z_ahead(l, b, c):
                if c == 0:
                    dense_start(l, "z", b, g_free_dve, DVE_FREES, TABLE["z", b]["u_z"])
                dense_unit(l, "z", b, g_free_dve, DVE_FREES, TABLE["z", b]["u_z"], 0, 0, c)

            def z_rest(l, b):
                t = TABLE["z", b]
                z_ahead(l, b, 1)
                for s, c in [(0, 2), (1, 0), (1, 1), (1, 2)]:
                    dense_unit(l, "z", b, g_free_dve, DVE_FREES, t["u_z"], 0, s, c)
                if t["n"] > 2:
                    with pe.Fori(1, t["n"] // 2) as i:
                        for s in range(2):
                            for c in range(NC):
                                dense_unit(l, "z", b, g_free_dve, DVE_FREES, t["u_z"], i, s, c)

            def out_phase(l):
                u = TABLE["out", 0]["u_z"]
                dense_start(l, "out", 0, g_free_dve, DVE_FREES, u)

                def sums(j, start, stop):
                    for c, (a, z) in enumerate(CHUNKS):
                        pe.wait_ge(g_free_dve, DVE_FREES * l + u + NC * j + c + 4)
                        last = mm(B[3 + c][:, 0:z - a], ones[:, :], merged[:, bass.ds(j, 1), a:z].rearrange("p o t -> p (o t)"),
                                  start=start, stop=stop)
                        if stop:
                            last.then_inc(ln_sum, 1)

                def item(i, s):
                    for c in range(NC):
                        dense_unit(l, "out", 0, g_free_dve, DVE_FREES, u, i, s, c)

                for c in range(NC):
                    pe.wait_ge(m_ready, NC * l + c + 1)
                    hold(pe, "pe")
                    dense_unit(l, "out", 0, g_free_dve, DVE_FREES, u, 0, 0, c)
                item(0, 1)
                sums(0, True, False)
                with pe.Fori(1, KD // 2) as i:
                    item(i, 0)
                    sums(2 * i - 1, False, False)
                    item(i, 1)
                    sums(2 * i, False, False)
                sums(KD - 1, False, True)

            def in_fills(l, b, i):
                t = TABLE["in", b]
                j, s = i

                def fill(c):
                    pe.wait_ge(g_free_act, ACT_FREES * l + t["u_in"] + 2 * NC * j + NC * s + c + 2)
                    product(B[(NC * s + c) % 2], s, KD, c, xh, xl, NRING * l + t["ring"] + 2 * j + s)\
                        .then_inc(g_full, 1)
                return fill

            def merge_start(l, b):
                t = TABLE["merge", b]
                pe.wait_ge(g_free_dve, DVE_FREES * l + t["u_z"] + t["u_out"] + 3)
                pe.wait_ge(y_ready, UNITS["z"] * l + t["u_z"] + 2)
                hold(pe, "pe")

            def merge_unit(l, b, j, c):
                t = TABLE["merge", b]
                q = t["u_merge"] + NC * j
                tile = NRING * l + t["ring"] + 2 * j
                pe.wait_ge(g_free_act, ACT_FREES * l + t["u_in"] + q + c + (3, 2, 2)[c])
                product(B[c % 2], 0, KD, c, xh, xl, tile).then_inc(g_full, 1)
                pe.wait_ge(p_free, P_UNITS * l + q + c + 2)
                product(B[2], 1, Y_TILES[b], c, yh, yl, tile + 1).then_inc(p_full, 1)

            def norm_sums():
                for c, (a, z) in enumerate(CHUNKS):
                    for j in range(KD):
                        last = mm(B[3 + c][:, 0:z - a], ones[:, :], merged[:, j, a:z], start=(j == 0), stop=(j == KD - 1))
                    last.then_inc(ln_sum, 1)

            def norm_squares(n):
                for c, (a, z) in enumerate(CHUNKS):
                    pe.wait_ge(ln_sq, NC * n + c + 1)
                    for j in range(KD):
                        last = mm(B[(6, 7, 3)[c]][:, 0:z - a], ones[:, :], A[:, j, a:z], start=(j == 0), stop=(j == KD - 1))
                    last.then_inc(ln_var, 1)

            def memory_products(l):
                W, M = memory_weights(), memory_inputs()
                pe.wait_ge(mkv_in, 16 * (l + 2))
                bk, bv = B[(0, 4)[l]], B[(1, 5)[l]]
                for p in range(2):
                    for k in range(KD):
                        mm(bk[:, 256 * p:256 * p + 256], W[:, k, P * p:P * p + P], M[:, k, :],
                           start=(k == 0), stop=(k == KD - 1))
                for p in range(2):
                    for k in range(KD):
                        last = mm(bv[:, 256 * p:256 * p + 256], M[:, k, P * p:P * p + P], W[:, k, 256:512],
                                  start=(k == 0), stop=(k == KD - 1))
                last.then_inc(mkv_ps, 1)

            def mem_pair(l, i, fill):
                for s in range(2):
                    pe.wait_ge(mem_q, 10 * l + 2 * i + s + 1)
                    for h in range(4):
                        p, e = h // 2, h % 2
                        last = mm(B[3 + 2 * s + e][:, 256 * p:256 * p + 256], m_q[s][64 * e:64 * e + 64, p, :],
                                  A[64 * e:64 * e + 64, 6, 256 * p:256 * p + 256], start=True, stop=True)
                    last.then_inc(mem_scores, 1)
                fill(0)
                for s in range(2):
                    pe.wait_ge(mem_prob, 10 * l + 2 * i + s + 1)
                    for m in range(4):
                        for st in range(2):
                            last = pe.transpose(B[3 + 2 * s + m // 2][:, (m % 2 * 2 + st) * P:(m % 2 * 2 + st + 1) * P],
                                                m_pr[s][:, m, st * P:st * P + P], ident[:, :])
                    last.then_inc(mem_pt, 1)
                fill(1)
                for s in range(2):
                    pe.wait_ge(mem_pta, NTT * l + 2 * i + s + 1)
                    pe.wait_ge(mem_ptd, 10 * l + 2 * i + s + 1)
                    for m in range(4):
                        e, p = m // 2, m % 2
                        for st in range(2):
                            last = mm(B[7][64 * e:64 * e + 64, 256 * s + P * p:256 * s + P * p + P],
                                      A[:, 6, 512 + 256 * st + 64 * (2 * p + e):512 + 256 * st + 64 * (2 * p + e) + 64],
                                      m_pt[s][:, 2 * m + st, :], start=(st == 0), stop=(st == 1))
                    last.then_inc(mem_o, 1)
                fill(2)

            def mem_samples(l):
                pe.wait_ge(mem_cache, 16 * (l + 1))
                hold(pe, "pe")
                for g in range(2):
                    pe.wait_ge(mem_q, 10 * l + NTT + g + 1)
                    for b in range(4):
                        for p in range(2):
                            last = mm(B[(5, 3)[g]][32 * b:32 * b + 32, 0:256], m_qbd[:, p, 4 * g + b, :],
                                      m_cache(g, b)[:, 256 * p:256 * p + 256], start=(p == 0), stop=(p == 1))
                    last.then_inc(mem_scores, 1)
                z_ahead(l, MEM, 0)
                for g in range(2):
                    pe.wait_ge(mem_prob, 10 * l + NTT + g + 1)
                    for st in range(2):
                        last = pe.transpose(B[(6, 4)[g]][:, st * P:st * P + P], m_pr[g][:, 0, st * P:st * P + P],
                                            ident[:, :])
                    last.then_inc(mem_pt, 1)
                for g in range(2):
                    pe.wait_ge(mem_ptd, 10 * l + NTT + g + 1)
                    for b in range(4):
                        for p in range(2):
                            for st in range(2):
                                last = mm(B[7][:, 256 * g + P * p + 32 * b:256 * g + P * p + 32 * b + 32],
                                          m_cache(g, b)[:, 512 + 256 * st + P * p:512 + 256 * st + P * p + P],
                                          m_pt[g][:, st, 32 * b:32 * b + 32], start=(st == 0), stop=(st == 1))
                    last.then_inc(mem_o, 1)

            def lru_step(l, ct, fill):
                n = 4 * l + ct + 1
                pe.wait_ge(lru_conv, n)
                for c, (a, z) in enumerate(CHUNKS):
                    if c:
                        pe.wait_ge(lru_act, 3 * 4 * l + 3 * ct + c)
                    mm(B[5][:, 0:z - a], l_w[:, LW_WR:LW_WR + P], A[:, 8, a:z], start=True, stop=True)
                    mm(B[6][:, 0:z - a], l_w[:, LW_WI:LW_WI + P], A[:, 8, a:z], start=True, stop=True)\
                        .then_inc(lru_ps, 1)
                    fill(c)
                for k in range(NC, 2 * NC):
                    fill(k)

            def swa_pair(l, i, fill):
                for s in range(2):
                    pe.wait_ge(swa_vst, STEPS * l + 2 * i + s + 1)
                    tok = bass.ds(2 * P * i + P * s, P)
                    mm(B[3 + 2 * s][:, :], s_rot[:, :], A[:, 0:4, tok], start=True, stop=True)
                    mm(B[4 + 2 * s][:, 0:P], s_rot[:, :], A[:, 4, tok], start=True, stop=True)
                    pe.transpose(B[4 + 2 * s][:, P:2 * P], s_v[s][:, :], ident[:, :]).then_inc(swa_rot, 1)
                fill(0)
                for r in range(2):
                    at = (2 * STEPS - 1) * l + 4 * i + 2 * r
                    for s in range(2):
                        if r == 0:
                            pe.wait_ge(swa_qk, STEPS * l + 2 * i + s + 1)
                        for m in range(2):
                            for e in range(2):
                                last = mm(B[3 + 2 * s + e][:, 256 * m:256 * m + 256],
                                          s_q[s][64 * e:64 * e + 64, 2 * r + m, :],
                                          s_k[64 * e:64 * e + 64, s:s + 2, :], start=True, stop=True)
                        last.then_inc(swa_scores, 1)
                    fill(1 + 2 * r)
                    fill(2 + 2 * r)
                    for s in range(2):
                        pe.wait_ge(swa_prob, at + s + 1)
                        for m in range(4):
                            for st in range(2):
                                last = pe.transpose(
                                    B[3 + 2 * s + m // 2][:, (m % 2 * 2 + st) * P:(m % 2 * 2 + st + 1) * P],
                                    s_pr[s][:, m, st * P:st * P + P], ident[:, :])
                        last.then_inc(swa_pt, 1)
                    for s in range(2):
                        pe.wait_ge(swa_pta, at + s + 1)
                        pe.wait_ge(swa_ptd, at + s + 1)
                        for m in range(4):
                            e, q = m // 2, m % 2
                            for st in range(2):
                                last = mm(B[7][64 * e:64 * e + 64, 256 * s + P * q:256 * s + P * q + P],
                                          s_vn[:, s + st, 64 * e:64 * e + 64],
                                          s_pt[s][:, 2 * m + st, :], start=(st == 0), stop=(st == 1))
                        last.then_inc(swa_o, 1)
                fill(5)

            def swa_samples(l):
                n = STEPS * l + STEPS
                pe.wait_ge(swa_vst, n)
                mm(B[3][:, 0:4 * NSAMP], s_rot[:, :], A[:, 0:4, SEQ:T], start=True, stop=True)
                mm(B[4][:, 0:NSAMP], s_rot[:, :], A[:, 4, SEQ:T], start=True, stop=True)
                pe.transpose(B[4][0:NSAMP, P:2 * P], s_v[0][:, 0:NSAMP], ident[:, :]).then_inc(swa_rot, 1)
                pe.wait_ge(swa_qk, n)
                pe.wait_ge(swa_cache, 16 * (l + 1))
                C = swa_caches()
                for u in range(4):
                    o = 256 * (u % 2)
                    for e in range(2):
                        b = 2 * u + e
                        mm(B[5 + u // 2][64 * e:64 * e + 64, o:o + P], s_qbd[:, b, :], C[:, b, 0:P],
                           start=True, stop=True)
                    last = mm(B[5 + u // 2][:, o + P:o + P + NSAMP],
                              s_qbd[:, 2 * u:2 * u + 2, :].rearrange("p b h -> p (b h)"), s_k[:, 0, 0:NSAMP],
                              start=True, stop=True)
                last.then_inc(swa_scores, 1)
                z_ahead(l, SWA, 0)
                m = (2 * STEPS - 1) * (l + 1)
                pe.wait_ge(swa_prob, m)
                for u in range(4):
                    pe.transpose(B[5][:, P * u:P * u + P], s_pr[0][:, u, 0:P], ident[:, :])
                for u in range(4):
                    last = pe.transpose(B[6][0:NSAMP, P * u:P * u + P], s_pr[0][:, u, P:P + NSAMP], ident[:, :])
                last.then_inc(swa_pt, 1)
                pe.wait_ge(swa_pta, m)
                pe.wait_ge(swa_ptd, m)
                for b in range(NB):
                    u, e = b // 2, b % 2
                    mm(B[7][:, 64 * b:64 * b + 64], C[:, b, P:2 * P], s_pt[0][:, u, 64 * e:64 * e + 64],
                       start=True, stop=False)
                    last = mm(B[7][:, 64 * b:64 * b + 64], s_vn[0:NSAMP, 1, :], s_pt[0][0:NSAMP, 4 + u, 64 * e:64 * e + 64],
                              start=False, stop=True)
                last.then_inc(swa_o, 1)

            def sgu_pair(l, i, fill):
                for s in range(2):
                    pe.wait_ge(sgu_vst, STEPS * l + 2 * i + s + 1)
                    for j in range(4):
                        last = pe.transpose(B[3 + 2 * s][:, P * j:P * j + P], g_v[s][:, j, :], ident[:, :])
                    last.then_inc(sgu_vt, 1)
                for k in range(3):
                    fill(k)
                for s in range(2):
                    pe.wait_ge(sgu_vn, STEPS * l + 2 * i + s + 1)
                    for j in range(4):
                        last = mm(B[4 + 2 * s][:, P * j:P * j + P], g_vn[s][:, P * j:P * j + P], g_w[:, j, :],
                                  start=True, stop=True)
                    last.then_inc(sgu_mix, 1)
                for k in range(3, 6):
                    fill(k)

            def sgu_samples(l):
                n = STEPS * l + STEPS
                pe.wait_ge(sgu_vst, n)
                hold(pe, "pe")
                for j in range(4):
                    last = pe.transpose(B[3][0:NSAMP, P * j:P * j + P], g_v[0][:, j, 0:NSAMP], ident[:, :])
                last.then_inc(sgu_vt, 1)
                z_ahead(l, SGU, 0)
                pe.wait_ge(sgu_vn, n)
                for j in range(4):
                    last = mm(B[4][:, NSAMP * j:NSAMP * j + NSAMP], g_vn[0][0:NSAMP, P * j:P * j + P],
                              g_ws[0:NSAMP, j, :], start=True, stop=True)
                last.then_inc(sgu_mix, 1)

            def gla_rank(l):
                t = TABLE["rank", GLA]
                tile = NRING * l + t["ring"]
                for c in range(NC):
                    pe.wait_ge(g_free_act, ACT_FREES * l + t["u_in"] + t["u_merge"] + c + (3, 2, 2)[c])
                    product(B[c % 2], 0, KD, c, xh, xl, tile).then_inc(g_full, 1)
                pe.drain()
                pe.wait_ge(split_full, 3 * (tile + 2))
                pe.sem_inc(split_free, 2)

            def gla_decays(l):
                pe.wait_ge(loaded[GLA], 16 * LOADS[GLA] * (l + 1))
                pe.wait_ge(g_free_act, ACT_FREES * l + TABLE["rank", GLA]["u_in"] + TABLE["rank", GLA]["u_merge"] + NC + 3)
                for c, (a, z) in enumerate(CHUNKS):
                    if c:
                        pe.wait_ge(gla_na, NC * l + c)
                    for p in range(2):
                        last = mm(B[3 + p][:, 0:z - a], a_wa[0:16, P * p:P * p + P], A[0:16, 8, a:z],
                                  start=True, stop=True)
                    last.then_inc(gla_x, 1)

            def gla_products(n, w, levels):
                pe.wait_ge(gla_qk, n)
                hold(pe, "pe")
                for v in range(levels):
                    for p in range(2):
                        for e in range(2):
                            last = mm(B[3 + e][0:w, 256 * v + P * p:256 * v + P * p + w],
                                      a_dk[64 * e:64 * e + 64, v, P * p:P * p + w],
                                      a_dq[64 * e:64 * e + 64, v, P * p:P * p + w], start=True, stop=True)
                last.then_inc(gla_att, 1)
                for p in range(2):
                    last = pe.transpose(B[5][0:w, P * p:P * p + P], a_dk[:, NLEV, P * p:P * p + w], ident[:, :])
                last.then_inc(gla_kt, 1)

            def gla_values(n, w):
                pe.wait_ge(gla_vst, n)
                hold(pe, "pe")
                for j in range(4):
                    last = pe.transpose(B[6][0:w, P * j:P * j + P], a_v[:, j, 0:w], ident[:, :])
                last.then_inc(gla_vt, 1)

            def gla_sumsq(n, bank):
                pe.wait_ge(gla_sqr, n)
                mm(B[bank][:, :], ones[:, :], a_rs, start=True, stop=True).then_inc(gla_ss, 1)

            def gla_step(l, i, fill):
                n = STEPS * l + i + 1
                gla_products(n, P, NLEV)
                fill(0)
                pe.wait_ge(gla_vn, n)
                pe.wait_ge(gla_attm, n)
                if not (isinstance(i, int) and i == 0):
                    pe.wait_ge(gla_oc, NTT * l + i)
                hold(pe, "pe")
                for h in range(4):
                    p, e = h // 2, h % 2
                    mm(B[7][:, P * h:P * h + P], a_vn[:, P * h:P * h + P], a_att[:, 2 * e + p, :], start=True, stop=False)
                    last = mm(B[7][:, P * h:P * h + P], a_S[:, h, :], a_dq[:, NLEV, P * p:P * p + P],
                              start=False, stop=True)
                last.then_inc(gla_o, 1)
                pe.wait_ge(gla_kn, n)
                for p in range(2):
                    last = mm(B[5][:, 256 * p:256 * p + 256], a_kn[:, p, :], a_vn[:, 256 * p:256 * p + 256],
                              start=True, stop=True)
                last.then_inc(gla_st, 1)
                if not (isinstance(i, int) and i == 0):
                    gla_sumsq(n - 1, 3)
                fill(1)
                gla_values(n + 1, NSAMP if isinstance(i, int) and i == NTT - 1 else P)
                fill(2)

            def gla_samples(l):
                n = STEPS * l + STEPS
                w = NSAMP
                gla_products(n, w, 1)
                z_ahead(l, GLA, 0)
                pe.wait_ge(gla_vn, n)
                pe.wait_ge(gla_attm, n)
                for h in range(4):
                    p, e = h // 2, h % 2
                    mm(B[7][:, P * h:P * h + w], a_vn[0:w, P * h:P * h + P], a_att[0:w, 2 * e + p, 0:w],
                       start=True, stop=True)
                gla_sumsq(n - 1, 6)
                pe.wait_ge(gla_s0, 16 * (l + 1))
                pe.wait_ge(gla_rec, n - 1)
                hold(pe, "pe")
                S0 = sample_states()
                for b in range(NB):
                    pe.wait_ge(gla_km, NB * l + b + 1)
                    for h in range(4):
                        mm(B[6][:, P * h + NS * b:P * h + NS * b + NS], S0[:, b, h, :],
                           a_dq[:, NLEV, P * (h // 2) + NS * b:P * (h // 2) + NS * b + NS], start=True, stop=True)
                    km = (a_km, a_dk[:, 0, :].rearrange("p (a b) -> p a b", a=2))[b % 2]
                    for p in range(2):
                        last = mm(B[(5, 3)[b % 2]][:, 256 * p:256 * p + 256], km[0:w, p, :],
                                  a_vn[0:w, 256 * p:256 * p + 256], start=True, stop=True)
                    last.then_inc(gla_sts, 1)
                pe.wait_ge(gla_sqr, n)
                for h in range(4):
                    last = mm(B[6][:, P * h:P * h + w], ones[:, :], a_rs[:, P * h:P * h + w], start=True, stop=True)
                last.then_inc(gla_ss, 1)

            def fills(l, b, j):
                def fill(k):
                    merge_unit(l, b, j + k // NC, k % NC)
                return fill

            pe.sem_inc(split_free, 4)
            pe.wait_ge(s_const, 16)
            pe.wait_ge(s_ones, 1)
            pe.wait_ge(x_loaded, 16)
            norm_sums()
            memory_products(0)
            norm_squares(0)
            memory_products(1)
            pe.wait_ge(mkv_sb, DEPTH)
            with pe.Fori(0, DEPTH) as l:
                dense(l, "in", MEM, g_free_act, ACT_FREES, 0, NC * l)
                pe.wait_ge(loaded[MEM], 32 * (l + 1))
                hold(pe, "pe")
                with pe.Fori(0, NTT // 4) as i:
                    for s in range(2):
                        mem_pair(l, 2 * i + s, in_fills(l, LRU, (i, s)))
                mem_samples(l)
                z_rest(l, MEM)
                for b in range(NBR):
                    merge_start(l, b)
                    if b + 1 == LRU:
                        with pe.Fori(0, 4) as i:
                            lru_step(l, i, fills(l, b, 2 * i))
                    if b + 1 == SWA:
                        swa_pair(l, 0, fills(l, b, 0))
                        with pe.Fori(1, NTT // 2) as i:
                            swa_pair(l, i, fills(l, b, 2 * i))
                        swa_samples(l)
                    if b + 1 == SGU:
                        with pe.Fori(0, NTT // 2) as i:
                            sgu_pair(l, i, fills(l, b, 2 * i))
                        sgu_samples(l)
                    if b + 1 == GLA:
                        gla_decays(l)
                        gla_values(STEPS * l + 1, P)
                        gla_step(l, 0, fills(l, b, 0))
                        with pe.Fori(1, NTT - 1) as i:
                            gla_step(l, i, fills(l, b, i))
                        gla_step(l, NTT - 1, fills(l, b, NTT - 1))
                        gla_samples(l)
                    if b + 1 == NBR:
                        with pe.Fori(0, KD) as i:
                            for c in range(NC):
                                merge_unit(l, b, i, c)
                    if b + 1 < NBR:
                        if b + 1 == LRU:
                            dense(l, "z", b + 1, g_free_dve, DVE_FREES, TABLE["z", b + 1]["u_z"])
                        else:
                            z_rest(l, b + 1)
                    if b + 2 < NBR:
                        t = TABLE["in", b + 2]
                        dense(l, "in", b + 2, g_free_act, ACT_FREES, t["u_in"] + t["u_merge"])
                    if b + 2 == GLA:
                        gla_rank(l)
                out_phase(l)
                norm_squares(l + 1)

        @block.scalar
        def _(act):
            a_ = act.activation

            def load(dst, src, s):
                act.dma_start(dst, src).then_inc(s, 16)

            def layer(src, l):
                names = "abcd"[:len(src.shape) - 2]
                return src[bass.ds(l, 1)].rearrange(f"o p {' '.join(names)} -> p (o {names[0]}) {' '.join(names[1:])}")

            def evac(l, kind, b, n):
                t = TABLE[kind, b]

                def tile(item, slot, s):
                    for c, (a, z) in enumerate(CHUNKS):
                        act.wait_ge(g_full, NG * l + NC * (t["w8"] + item) + c + 1)
                        dst = A[:, slot, a:z] if isinstance(slot, int) else \
                            A[:, bass.ds(slot, 1), a:z].rearrange("p o t -> p (o t)")
                        a_(dst, B[(NC * s + c) % 2][:, 0:z - a], ACT.Copy).then_inc(g_free_act, 1)
                if kind == "rank":
                    tile(0, 8, 0)
                    return
                with act.Fori(0, n // 2) as i:
                    for s in range(2):
                        tile(2 * i + s, 2 * i + s, s)

            def in_fills(l, b, i):
                t = TABLE["in", b]
                j, s = i

                def fill(c):
                    a, z = CHUNKS[c]
                    act.wait_ge(g_full, NG * l + NC * (t["w8"] + 2 * j + s) + c + 1)
                    a_(merged[:, bass.ds(4 + 2 * j + s, 1), a:z].rearrange("p o t -> p (o t)"),
                       B[(NC * s + c) % 2][:, 0:z - a], ACT.Copy).then_inc(g_free_act, 1)
                return fill

            def z_tanh(l, b):
                t = TABLE["z", b]
                act.wait_ge(p_free, P_UNITS * l + t["u_merge"] + 2)
                with act.Fori(0, t["n"] // 2) as i:
                    for s in range(2):
                        for c, (a, z) in enumerate(CHUNKS):
                            q = t["u_z"] + 2 * NC * i + NC * s
                            act.wait_ge(g_full, NG * l + NC * (t["w8"] + 2 * i + s) + c + 1)
                            act.wait_ge(y_ready, UNITS["z"] * l + q + (2, 1, 3)[c])
                            a_(th[:, c % 2, 0:z - a], B[(NC * s + c) % 2][:, 0:z - a], ACT.Tanh, scale=0.5)\
                                .then_inc(z_th, 1)

            def merge_start(l, b):
                act.wait_ge(y_ready, UNITS["z"] * l + TABLE["merge", b]["u_z"] + 2)

            def merge_unit(l, b, j, c):
                t = TABLE["merge", b]
                a, z = CHUNKS[c]
                act.wait_ge(g_full, NG * l + NC * (t["w8"] + j) + c + 1)
                act.wait_ge(p_free, P_UNITS * l + t["u_merge"] + NC * j + (2, 1, 3)[c])
                a_(th[:, c % 2, 0:z - a], B[c % 2][:, 0:z - a], ACT.Tanh, scale=0.5).then_inc(g_free_act, 1)

            def fills(l, b, j):
                def fill(k):
                    merge_unit(l, b, j + k // NC, k % NC)
                return fill

            def norm_start(n):
                for c, (a, z) in enumerate(CHUNKS):
                    act.wait_ge(ln_sum, NC * n + c + 1)
                    a_(ln_m[:, c, 0:z - a], B[3 + c][:, 0:z - a], ACT.Copy, scale=1.0 / D).then_inc(ln_mean, 1)
                for c, (a, z) in enumerate(CHUNKS):
                    act.wait_ge(ln_cent, NC * n + c + 1)
                    a_(A[:, 0:KD, a:z], merged[:, :, a:z], ACT.Square).then_inc(ln_sq, 1)

            def norm_end(n):
                def root(c):
                    w = CHUNKS[c][1] - CHUNKS[c][0]
                    act.wait_ge(ln_rec, NC * n + c + 1)
                    a_(ln_v[:, c, 0:w], ln_v[:, c, 0:w], ACT.Sqrt).then_inc(ln_rstd, 1)

                root(0)
                act.wait_ge(lnp_loaded, 16 * (n + 1))
                for c, (a, z) in enumerate(CHUNKS):
                    act.wait_ge(ln_norm, NC * n + c + 1)
                    for j in range(KD):
                        last = a_(merged[:, j, a:z], merged[:, j, a:z], ACT.Identity,
                                  scale=lnp[:, j:j + 1], bias=lnp[:, KD + j:KD + j + 1])
                    last.then_inc(ln_aff, 1)
                    if c + 1 < NC:
                        root(c + 1)
                    act.wait_ge(ln_aff, NC * n + c + 1)
                    a_(xh[:, :, a:z], merged[:, :, a:z], ACT.Copy).then_inc(x_high, 1)
                    act.dma_start(d["y"][:, :, a:z], merged[:, :, a:z]).then_inc(x_stored, 16)

            def mem_pair(l, i, fill):
                for s in range(2):
                    act.wait_ge(mem_max, 10 * l + 2 * i + s + 1)
                    for m in range(4):
                        last = a_(m_pr[s][:, m, :], B[3 + 2 * s + m // 2][:, 256 * (m % 2):256 * (m % 2) + 256], ACT.Exp,
                                  bias=m_mx[s][:, m:m + 1], scale=HEAD_SCALE, accum_out=m_sum[s][:, m:m + 1])
                    last.then_inc(mem_exp, 1)
                fill(0)
                for s in range(2):
                    act.wait_ge(mem_pt, 10 * l + 2 * i + s + 1)
                    a_(m_pt[s][:, 0:4, :].rearrange("p a b -> p (a b)"), B[3 + 2 * s][:, :], ACT.Copy)\
                        .then_inc(mem_pta, 1)
                fill(1)
                fill(2)

            def mem_samples(l):
                for g in range(2):
                    act.wait_ge(mem_max, 10 * l + NTT + g + 1)
                    a_(m_pr[g][:, 0, :], B[(5, 3)[g]][:, 0:256], ACT.Exp, bias=m_mx[g][:, 0:1], scale=HEAD_SCALE,
                       accum_out=m_sum[g][:, 0:1]).then_inc(mem_exp, 1)

            def lru_params(l, ct):
                load(l_w[:, :], d["lru"][bass.ds(4 * l + ct, 1)].rearrange("o p n -> p (o n)"), lru_w)

            def lru_exp(n):
                act.wait_ge(lru_e, n)
                a_(l_t[:, 1:2], l_t[:, 0:1], ACT.Exp).then_inc(lru_l, 1)

            def lru_step(l, ct, fill):
                n = 4 * l + ct + 1
                act.wait_ge(lru_i, n)
                for c, (a, z) in enumerate(CHUNKS):
                    act.wait_ge(lru_ps, 3 * (n - 1) + c + 1)
                    a_(A[:, 5, a:z], B[5][:, 0:z - a], ACT.Tanh, scale=0.5, bias=l_h[:, 0:1])
                    a_(A[:, 6, a:z], B[6][:, 0:z - a], ACT.Tanh, scale=0.5, bias=l_h[:, 1:2]).then_inc(lru_act, 1)
                    if c < NC - 1:
                        fill(c)
                act.drain()
                a_(A[:, 4, :], A[:, 5, :], ACT.Exp, scale=l_s4[:, 0:1], bias=l_s4[:, 0:1])
                a_(A[:, 7, :], A[:, 5, :], ACT.Tanh, scale=l_ns4[:, 0:1], bias=l_ns4[:, 0:1]).then_inc(lru_r, 1)
                fill(2)
                act.wait_ge(lru_w2, n)
                a_(A[:, 7, :], A[:, 7, :], ACT.Sqrt).then_inc(lru_sq, 1)
                final = isinstance(ct, int)
                if not final:
                    lru_params(l, ct + 1)
                fill(3)
                act.wait_ge(lru_done, n)
                act.dma_start(d["lru_tail"][bass.ds(n - 1, 1)].rearrange("o p n -> p (o n)"), l_tail[:, :])\
                    .then_inc(lru_tail, 16)
                fill(4)
                if not final:
                    lru_exp(n + 1)
                fill(5)
                act.wait_ge(lru_tail, 16 * n)

            def swa_exps(s, at, w):
                act.wait_ge(swa_max, at)
                for m in range(4):
                    a_(s_pr[s][:, m, 0:w], s_pr[s][:, m, 0:w], ACT.Exp, bias=s_nm[s][:, m:m + 1], scale=HEAD_SCALE,
                       accum_out=s_sum[s][:, m:m + 1])
                a_(s_es[s][:, :], s_es[s][:, :], ACT.Exp).then_inc(swa_exp, 1)

            def swa_copy(s, at, bank):
                act.wait_ge(swa_pt, at)
                a_(s_pt[s][:, 0:4, :].rearrange("p a b -> p (a b)"), B[bank][:, :], ACT.Copy).then_inc(swa_pta, 1)

            def swa_pair(l, i, fill):
                fill(0)
                if isinstance(i, int) and i == NTT // 2 - 1:
                    act.wait_ge(swa_qk, STEPS * l + NTT)
                    load(swa_caches(), d["swakv"][bass.ds(l, 1)].rearrange("o p b n -> p (o b) n"), swa_cache)
                for r in range(2):
                    at = (2 * STEPS - 1) * l + 4 * i + 2 * r
                    for s in range(2):
                        swa_exps(s, at + s + 1, 256)
                        fill(1 + 2 * r + s)
                    for s in range(2):
                        swa_copy(s, at + s + 1, 3 + 2 * s)
                fill(5)

            def swa_samples(l):
                n = STEPS * l + STEPS
                act.wait_ge(swa_qk, n)
                out = d["swa_new"][bass.ds(l, 1)].rearrange("o p n -> p (o n)")
                act.dma_start(out[:, 0:P], s_k[:, 2, :]).then_inc(stored, 16)
                act.dma_start(out[:, P:2 * P], A[:, 5, SEQ - P:SEQ]).then_inc(stored, 16)
                act.dma_start(out[:, 2 * P:2 * P + NSAMP], s_k[:, 0, 0:NSAMP]).then_inc(stored, 16)
                act.dma_start(out[:, 2 * P + NSAMP:2 * P + 2 * NSAMP], A[:, 5, SEQ:T]).then_inc(stored, 16)
                m = (2 * STEPS - 1) * (l + 1)
                swa_exps(0, m, 192)
                swa_copy(0, m, 5)

            def sgu_root(s, n, w):
                act.wait_ge(sgu_var, n)
                a_(g_rs[s][0:w, :], g_rs[s][0:w, :], ACT.Sqrt).then_inc(sgu_rstd, 1)

            def sgu_pair(l, i, fill):
                for s in range(2):
                    sgu_root(s, STEPS * l + 2 * i + s + 1, P)
                for k in range(6):
                    fill(k)

            def gla_decays(l):
                for c, (a, z) in enumerate(CHUNKS):
                    w = z - a
                    act.wait_ge(gla_na, NC * l + c + 1)
                    a_(a_e[:, :, 0:w], a_e[:, :, 0:w], ACT.Exp)
                    act.drain()
                    a_(a_e[:, :, 0:w], a_e[:, :, 0:w], ACT.Ln, bias=1.0).then_inc(gla_e, 1)

            def gla_exps(n, w, levels):
                act.wait_ge(gla_d, n)
                for ap in (a_dq, a_dk):
                    for k in range(levels):
                        a_(level(ap, k)[:, :, 0:w], level(ap, k)[:, :, 0:w], ACT.Exp, scale=1.0 / GLA_TAU)
                a_(level(a_dq, NLEV)[:, :, 0:w], a_b[:, :, 0:w], ACT.Exp, scale=1.0 / GLA_TAU)
                a_(level(a_dk, NLEV)[:, :, 0:w], level(a_dk, NLEV)[:, :, 0:w], ACT.Exp, scale=1.0 / GLA_TAU)
                a_(a_dec[:, :], a_dec[:, :], ACT.Exp, scale=1.0 / GLA_TAU).then_inc(gla_ex, 1)

            def gla_rows(n, w):
                act.wait_ge(gla_vt, n)
                a_(a_vn[0:w, :], B[6][0:w, :], ACT.Copy).then_inc(gla_vn, 1)

            def gla_keys(n, w):
                act.wait_ge(gla_kt, n)
                a_(a_kn[0:w, :, :], B[5][0:w, 0:2 * P].rearrange("p (h k) -> p h k", h=2), ACT.Copy).then_inc(gla_kn, 1)

            def gla_squares(l, i):
                act.wait_ge(gla_nd, NTT * l + i + 1)
                a_(a_rs.rearrange("p (h t) -> p h t", h=4), A[:, 4:8, bass.ds(P * i, P)], ACT.Square)\
                    .then_inc(gla_sqr, 1)

            def gla_root(n):
                act.wait_ge(gla_rec, n)
                a_(a_rs, a_rs, ACT.Sqrt).then_inc(gla_rstd, 1)

            def gla_step(l, i, fill):
                n = STEPS * l + i + 1
                first = isinstance(i, int) and i == 0
                w, levels = (NSAMP, 1) if isinstance(i, int) and i == NTT - 1 else (P, NLEV)
                gla_keys(n, P)
                if not first:
                    gla_squares(l, i - 1)
                fill(0)
                act.wait_ge(gla_o, NTT * l + i + 1)
                a_(A[:, 4:8, bass.ds(P * i, P)], B[7][:, :].rearrange("p (h t) -> p h t", h=4), ACT.Copy)\
                    .then_inc(gla_oc, 1)
                fill(1)
                gla_exps(n + 1, w, levels)
                gla_rows(n + 1, w)
                if not first:
                    gla_root(n - 1)
                act.drain()
                fill(2)

            def gla_samples(l):
                n = STEPS * l + STEPS
                w = NSAMP
                act.dma_start(d["gla_p"][bass.ds(l, 1)].rearrange("o p h v -> p (o h) v"), a_S[:, :, :])\
                    .then_inc(stored, 16)
                act.wait_ge(gla_kh, l + 1)
                load(sample_states(), d["gla_s0"][bass.ds(l, 1)].rearrange("o p b h v -> p (o b) h v"), gla_s0)
                gla_keys(n, w)
                gla_squares(l, NTT - 1)
                gla_root(n - 1)
                act.wait_ge(gla_os, l + 1)
                a_(a_rs.rearrange("p (h t) -> p h t", h=4)[:, :, 0:w],
                   a_vn[:, :].rearrange("p (h t) -> p h t", h=4)[:, :, 0:w], ACT.Square).then_inc(gla_sqr, 1)
                act.dma_start(d["gla_s"][bass.ds(l, 1)].rearrange("o p b h v -> p (o b) h v"), sample_states())\
                    .then_inc(gla_s0st, 16)
                gla_root(n)

            def mixer_loads(l, b):
                if b == SWA:
                    load(A[:, 6:8, :], d["rope"], loaded[b])
                    load(s_rot[:, :], d["rot"], loaded[b])
                    load(s_mask, d["swa_mask"], loaded[b])
                    load(s_smask, d["swa_smask"], loaded[b])
                    load(s_sink[:, :], layer(d["sink"], l), loaded[b])
                    load(s_sinkr[:, :], layer(d["sinkr"], l), loaded[b])
                if b == SGU:
                    act.wait_ge(stored, 16 * (5 * l + 4))
                    load(g_lng[:, :], d["sgu_g"][bass.ds(l, 1), :].broadcast_to([P, 512]), loaded[b])
                    load(g_lnb[:, :], d["sgu_b"][bass.ds(l, 1), :].broadcast_to([P, 512]), loaded[b])
                    load(g_w[:, :, :], d["sgu_w"][bass.ds(l, 1)].rearrange("o p g t -> p (o g) t"), loaded[b])
                    load(g_ws[0:NSAMP, :, :], d["sgu_ws"][bass.ds(l, 1)].rearrange("o p g t -> p (o g) t"), loaded[b])
                    load(g_b[:, :, :], d["sgu_bs"][bass.ds(l, 1)].broadcast_to([P, 4, P]), loaded[b])
                    load(g_bs[:, :, :], d["sgu_bss"][bass.ds(l, 1)].broadcast_to([P, 4, NSAMP]), loaded[b])
                    load(g_m[:, :], d["tril"], loaded[b])
                    load(g_ms[0:NSAMP, :], d["tril8"], loaded[b])
                if b == GLA:
                    act.wait_ge(sgu_stored, 16 * (l + 1))
                    load(a_wa[0:16, :], d["wa2"][bass.ds(l, 1)].rearrange("o p n -> p (o n)"), loaded[b])
                    load(a_ba[:, :], layer(d["ba"], l), loaded[b])
                    load(a_ng[:, :], layer(d["ng"], l), loaded[b])
                    load(a_mask, d["gla_mask"], loaded[b])
                    load(a_smask[0:NSAMP, :], d["tril8"], loaded[b])

            act.sem_inc(g_free_act, 3)
            load(ident[:, :], d["ident"], s_const)
            load(merged[:, :, :], d["x"], x_loaded)
            load(memory_inputs(), d["mem"].rearrange("p (k s) -> p k s", k=KD), mkv_in)
            load(memory_weights(), d["w_mem"][0].rearrange("p (k n) -> p k n", k=KD), mkv_in)
            load(lnp[:, :], d["lnp"][0], lnp_loaded)
            norm_start(0)

            def memory_copies(l):
                if l:
                    act.wait_ge(mkv_out, 16 * l)
                a_(A[:, 8, 0:512], B[(0, 4)[l]][:, :], ACT.Copy)
                a_(A[:, 8, 512:1024], B[(1, 5)[l]][:, :], ACT.Copy).then_inc(mkv_sb, 1)
                act.wait_ge(mkv_sb, l + 1)
                act.dma_start(d["mkv"][l], A[:, 8, 0:1024]).then_inc(mkv_out, 16)

            act.wait_ge(mkv_ps, 1)
            load(memory_weights(), d["w_mem"][1].rearrange("p (k n) -> p k n", k=KD), mkv_in)
            memory_copies(0)
            norm_end(0)
            act.dma_start(d["swa_old_k"], d["cache_k"][:, :, NS:, :]).then_inc(swa_old, 16)
            act.dma_start(d["swa_old_v"], d["cache_v"][:, :, NS:, :]).then_inc(swa_old, 16)
            act.wait_ge(mkv_ps, 2)
            memory_copies(1)
            act.wait_ge(mkv_out, 16 * DEPTH)
            with act.Fori(0, DEPTH) as l:
                act.wait_ge(ln_var, NC * (l + 1))
                act.wait_ge(x_ready, NC * (l + 1))
                load(lnp[:, :], d["lnp"][bass.ds(l + 1, 1)].rearrange("o p n -> p (o n)"), lnp_loaded)
                load(A[:, 6, 0:1024], d["mkv"][bass.ds(l, 1)].rearrange("o p n -> p (o n)"), loaded[MEM])
                load(A[:, 2:6, 0:1024], d["memkv"][bass.ds(NB * l, 4)].rearrange("b p n -> p b n"), loaded[MEM])
                lru_params(l, 0)
                evac(l, "in", MEM, 2)
                act.wait_ge(x_stored, 16 * NC * (l + 1))
                load(merged[:, 0:4, 0:1024], d["memkv"][bass.ds(NB * l + 4, 4)].rearrange("b p n -> p b n"), mem_cache)
                with act.Fori(0, NTT // 4) as i:
                    for s in range(2):
                        mem_pair(l, 2 * i + s, in_fills(l, LRU, (i, s)))
                lru_exp(4 * l + 1)
                mem_samples(l)
                z_tanh(l, MEM)
                for b in range(NBR):
                    merge_start(l, b)
                    if b + 1 == LRU:
                        with act.Fori(0, 3) as i:
                            lru_step(l, i, fills(l, b, 2 * i))
                        lru_step(l, 3, fills(l, b, 6))
                    if b + 1 == SWA:
                        swa_pair(l, 0, fills(l, b, 0))
                        with act.Fori(1, NTT // 2 - 1) as i:
                            swa_pair(l, i, fills(l, b, 2 * i))
                        swa_pair(l, NTT // 2 - 1, fills(l, b, NTT - 2))
                        swa_samples(l)
                    if b + 1 == SGU:
                        with act.Fori(0, NTT // 2) as i:
                            sgu_pair(l, i, fills(l, b, 2 * i))
                        sgu_root(0, STEPS * (l + 1), NSAMP)
                        act.wait_ge(sgu_vn, STEPS * (l + 1))
                        act.dma_start(d["sgu_v"][bass.ds(l, 1)].rearrange("o p n -> p (o n)"), g_vn[0][0:NSAMP, :])\
                            .then_inc(sgu_stored, 16)
                    if b + 1 == GLA:
                        gla_decays(l)
                        gla_exps(STEPS * l + 1, P, NLEV)
                        gla_rows(STEPS * l + 1, P)
                        gla_step(l, 0, fills(l, b, 0))
                        with act.Fori(1, NTT - 1) as i:
                            gla_step(l, i, fills(l, b, i))
                        gla_step(l, NTT - 1, fills(l, b, NTT - 1))
                        gla_samples(l)
                    if b + 1 == NBR:
                        with act.Fori(0, KD) as i:
                            for c in range(NC):
                                merge_unit(l, b, i, c)
                    if b + 1 < NBR:
                        z_tanh(l, b + 1)
                        act.wait_ge(y_ready, UNITS["z"] * l + TABLE["z", b + 1]["u_z"] + NC * Y_TILES[b + 1] + 2)
                    if b + 2 < NBR:
                        mixer_loads(l, b + 2)
                        evac(l, "in", b + 2, IN_TILES[b + 2])
                    if b + 2 == GLA:
                        evac(l, "rank", GLA, 1)
                    if b + 1 == GLA:
                        act.wait_ge(gla_s0st, 16 * (l + 1))
                        act.wait_ge(stored, 16 * 5 * (l + 1))
                        act.wait_ge(x_stored, 16 * NC * (l + 1))
                        load(A[:, 0:KD, :], d["y"], res_loaded)
                act.wait_ge(merged_sum, l + 1)
                for c, (a, z) in enumerate(CHUNKS):
                    a_(xh[:, :, a:z], merged[:, :, a:z], ACT.Copy, scale=0.5).then_inc(merged_high, 1)
                norm_start(l + 1)
                norm_end(l + 1)
            act.wait_ge(x_stored, 16 * NC * (DEPTH + 1))
            act.wait_ge(stored, 16 * 5 * DEPTH)
            act.wait_ge(gla_s0st, 16 * DEPTH)
            act.wait_ge(sgu_stored, 16 * DEPTH)
            act.wait_ge(lru_tail, 16 * 4 * DEPTH)
            act.wait_ge(mkv_out, 16 * DEPTH)
            act.wait_ge(swa_old, 32)

        @block.vector
        def _(v):
            tt, ts, stt, cp = v.tensor_tensor, v.tensor_scalar, v.scalar_tensor_tensor, v.tensor_copy

            def inputs_ready(l, kind, b):
                t = TABLE[kind, b]
                v.wait_ge(g_free_act, ACT_FREES * l + t["u_in"] + t["u_merge"] + NC * t["n"] + 3)
                hold(v, "dve")

            def z_phase(l, b):
                t = TABLE["z", b]

                def tile(item, slot, s):
                    for c, (a, z) in enumerate(CHUNKS):
                        w = z - a
                        o = A[:, bass.ds(OUT_SLOT[b] + slot, 1), a:z].rearrange("p o t -> p (o t)")
                        hi = yh[:, bass.ds(slot, 1), a:z].rearrange("p o t -> p (o t)")
                        lo = yl[:, bass.ds(slot, 1), a:z].rearrange("p o t -> p (o t)")
                        v.wait_ge(z_th, UNITS["z"] * l + t["u_z"] + NC * item + c + 1)
                        stt(tm[:, 0:w], th[:, c % 2, 0:w], 1.0, B[(NC * s + c) % 2][:, 0:w], ALU.add, ALU.mult)\
                            .then_inc(g_free_dve, 1)
                        v.drain()
                        stt(tm2[:, 0:w], tm[:, 0:w], 0.5, o, ALU.mult, ALU.mult)
                        v.drain()
                        cp(hi, tm2[:, 0:w])
                        v.drain()
                        tt(lo, tm2[:, 0:w], hi.bitcast(F32), ALU.subtract).then_inc(y_ready, 1)
                        v.drain()
                with v.Fori(0, t["n"] // 2) as i:
                    for s in range(2):
                        tile(2 * i + s, 2 * i + s, s)

            def merge_unit(l, b, j, c):
                t = TABLE["merge", b]
                a, z = CHUNKS[c]
                w = z - a
                q = NC * j + c
                m = merged[:, bass.ds(j, 1), a:z].rearrange("p o t -> p (o t)")
                v.wait_ge(g_free_act, ACT_FREES * l + t["u_in"] + t["u_merge"] + q + 4)
                v.wait_ge(p_full, P_UNITS * l + t["u_merge"] + q + 1)
                pb = B[2][:, 0:w]
                if b == MEM:
                    stt(m, th[:, c % 2, 0:w], 1.0, pb, ALU.add, ALU.mult).then_inc(p_free, 1)
                else:
                    stt(tm[:, 0:w], th[:, c % 2, 0:w], 1.0, pb, ALU.add, ALU.mult).then_inc(p_free, 1)
                    v.drain()
                    tt(m, m, tm[:, 0:w], ALU.add)
                    v.drain()

            def fills(l, b, j):
                def fill(k):
                    merge_unit(l, b, j + k // NC, k % NC)
                return fill

            def layer_norm(n):
                for c, (a, z) in enumerate(CHUNKS):
                    v.wait_ge(ln_mean, NC * n + c + 1)
                    tt(merged[:, :, a:z], merged[:, :, a:z], bc(ln_m[:, c, 0:z - a], KD), ALU.subtract)\
                        .then_inc(ln_cent, 1)
                for c, (a, z) in enumerate(CHUNKS):
                    v.wait_ge(ln_var, NC * n + c + 1)
                    ts(ln_v[:, c, 0:z - a], B[(6, 7, 3)[c]][:, 0:z - a], 1.0 / D, LN_EPS, ALU.mult, ALU.add)
                    v.drain()
                    v.reciprocal(ln_v[:, c, 0:z - a], ln_v[:, c, 0:z - a]).then_inc(ln_rec, 1)
                    v.wait_ge(ln_rstd, NC * n + c + 1)
                    tt(merged[:, :, a:z], merged[:, :, a:z], bc(ln_v[:, c, 0:z - a], KD), ALU.mult)\
                        .then_inc(ln_norm, 1)
                if isinstance(n, int):
                    v.wait_ge(mkv_ps, DEPTH)
                for c, (a, z) in enumerate(CHUNKS):
                    v.wait_ge(x_high, NC * n + c + 1)
                    tt(xl[:, :, a:z], merged[:, :, a:z], xh[:, :, a:z].bitcast(F32), ALU.subtract)\
                        .then_inc(x_ready, 1)

            def mem_pair(l, i):
                tok = lambda s: bass.ds(2 * P * i + P * s, P)
                n = lambda s: 10 * l + 2 * i + s + 1
                for s in range(2):
                    cp(m_q[s][:, :, :], A[:, 0:2, tok(s)]).then_inc(mem_q, 1)
                for s in range(2):
                    v.wait_ge(mem_scores, n(s))
                    for e in range(2):
                        v.tensor_reduce(m_mx[s][:, 2 * e:2 * e + 2],
                                        B[3 + 2 * s + e][:, :].rearrange("p (m s) -> p m s", m=2), AX_X, ALU.max)
                    v.drain()
                    ts(m_mx[s][:, :], m_mx[s][:, :], -HEAD_SCALE, None, ALU.mult).then_inc(mem_max, 1)
                for s in range(2):
                    v.wait_ge(mem_exp, n(s))
                    v.reciprocal(m_sum[s][:, :], m_sum[s][:, :])
                    v.drain()
                    tt(m_pr[s][:, :, :], m_pr[s][:, :, :], bl(m_sum[s][:, :], 256), ALU.mult).then_inc(mem_prob, 1)
                for s in range(2):
                    v.wait_ge(mem_pt, n(s))
                    cp(m_pt[s][:, 4:8, :].rearrange("p a b -> p (a b)"), B[4 + 2 * s][:, :]).then_inc(mem_ptd, 1)
                v.wait_ge(mem_o, n(1))
                hold(v, "dve")
                for s in range(2):
                    cp(A[:, 0:2, tok(s)], B[7][:, 256 * s:256 * s + 256].rearrange("p (m t) -> p m t", m=2))
                v.drain()

            def mem_samples(l):
                n = lambda g: 10 * l + NTT + g + 1
                for p in range(2):
                    for e in range(2):
                        r = slice(64 * e, 64 * e + 64)
                        h = 2 * p + e
                        cp(m_qbd[r, p, :, NS * h:NS * h + NS], A[r, p, SEQ:T].rearrange("p (b t) -> p b t", b=NB))
                v.drain()
                v.sem_inc(mem_q, 2)
                inputs_ready(l, "in", LRU)
                lru_conv_start(4 * l + 1, 0)
                lru_taps(lru_x(0), (1, 0), last=True)
                for g in range(2):
                    v.wait_ge(mem_scores, n(g))
                    v.reduce_max(m_mx[g][:, 0:1], B[(5, 3)[g]][:, 0:256], AX_X)
                    v.drain()
                    ts(m_mx[g][:, 0:1], m_mx[g][:, 0:1], -HEAD_SCALE, None, ALU.mult).then_inc(mem_max, 1)
                for g in range(2):
                    v.wait_ge(mem_exp, n(g))
                    v.reciprocal(m_sum[g][:, 0:1], m_sum[g][:, 0:1])
                    v.drain()
                    ts(m_pr[g][:, 0, :], m_pr[g][:, 0, :], m_sum[g][:, 0:1], None, ALU.mult).then_inc(mem_prob, 1)
                for g in range(2):
                    v.wait_ge(mem_pt, n(g))
                    cp(m_pt[g][:, 0:2, :].rearrange("p a b -> p (a b)"), B[(6, 4)[g]][:, 0:256]).then_inc(mem_ptd, 1)
                v.wait_ge(mem_o, n(1))
                hold(v, "dve")
                for g in range(2):
                    for p in range(2):
                        for e in range(2):
                            r = slice(64 * e, 64 * e + 64)
                            h = 2 * p + e
                            o = B[7][r, 256 * g + P * p:256 * g + P * p + P].rearrange("p (b h t) -> p b h t", b=4, h=4)
                            cp(A[r, p, SEQ + 32 * g:SEQ + 32 * g + 32].rearrange("p (b t) -> p b t", b=4), o[:, :, h, :])
                v.drain()

            def lru_x(ct):
                return merged[:, bass.ds(4 + ct, 1), :].rearrange("p o t -> p (o t)")

            xc = A[:, 8, :]
            xs = xc[:, SEQ:T].rearrange("p (b t) -> p b t", b=NB)
            col = lambda k: l_w[:, k:k + 1]

            def lru_taps(X, taps, last=False):
                for j in taps:
                    k = 3 - j
                    v.drain()
                    stt(xc[:, k:SEQ], X[:, 0:SEQ - k], col(LW_CW + j), xc[:, k:SEQ], ALU.mult, ALU.add)
                    done = stt(xs, l_pad[:, :, j:j + NS], col(LW_CW + j), xs, ALU.mult, ALU.add)
                if last:
                    done.then_inc(lru_conv, 1)

            def lru_conv_start(n, ct):
                X = lru_x(ct)
                v.wait_ge(lru_w, 16 * n)
                hold(v, "dve")
                stt(l_t[:, 0:1], col(LW_LAM), -1.0, col(LW_LAM), ALU.mult, ALU.min).then_inc(lru_e, 1)
                ts(xc[:, 0:SEQ], X[:, 0:SEQ], col(LW_CW + 3), col(LW_CB), ALU.mult, ALU.add)
                cp(l_pad[:, :, 0:3], l_w[:, LW_CONV:LW_CONV + 3 * NB].rearrange("p (b j) -> p b j", b=NB))
                cp(l_pad[:, :, 3:11], X[:, SEQ:T].rearrange("p (b t) -> p b t", b=NB))
                v.drain()
                ts(xs, l_pad[:, :, 3:11], col(LW_CW + 3), col(LW_CB), ALU.mult, ALU.add)
                lru_taps(X, (2,))

            def lru_decay(n):
                v.wait_ge(lru_l, n)
                ts(l_t[:, 2:3], l_t[:, 1:2], 2.0, None, ALU.add)
                ts(l_h[:, :], l_w[:, LW_BR:LW_BR + 2], 0.5, None, ALU.mult)
                v.drain()
                v.reciprocal(l_t[:, 2:3], l_t[:, 2:3])
                v.drain()
                tt(l_t[:, 3:4], l_t[:, 1:2], l_t[:, 2:3], ALU.mult)
                v.drain()
                tt(l_t[:, 4:5], l_t[:, 3:4], l_t[:, 3:4], ALU.mult)
                v.drain()
                ts(l_t[:, 5:6], l_t[:, 4:5], 1.0 / 17, 1.0 / 15, ALU.mult, ALU.add)
                for k in (13, 11, 9, 7, 5, 3, 1):
                    v.drain()
                    ts(l_t[:, 5:6], l_t[:, 5:6], l_t[:, 4:5], 1.0 / k, ALU.mult, ALU.add)
                v.drain()
                stt(l_t[:, 6:7], l_t[:, 3:4], 2.0, l_t[:, 5:6], ALU.mult, ALU.mult)
                v.drain()
                stt(l_t[:, 7:8], col(LW_LAM), 0.0, l_t[:, 6:7], ALU.min, ALU.subtract)
                v.drain()
                ts(l_s4[:, :], l_t[:, 7:8], 4.0, None, ALU.mult)
                ts(l_ns4[:, :], l_t[:, 7:8], -4.0, None, ALU.mult).then_inc(lru_i, 1)

            def lru_step(l, ct, fill):
                n = 4 * l + ct + 1
                final = isinstance(ct, int)
                X = lru_x(ct)
                O = A[:, bass.ds(ct, 1), :].rearrange("p o t -> p (o t)")
                fill(0)
                fill(1)
                v.wait_ge(lru_r, n)
                tt(A[:, 5, :], A[:, 4, :], A[:, 4, :], ALU.mult)
                cp(l_ub[:, :, 0:1], l_w[:, LW_H0:LW_H0 + NB].rearrange("p (b o) -> p b o", o=1))
                v.drain()
                stt(A[:, 7, :], A[:, 5, :], 1.0, A[:, 7, :], ALU.add, ALU.mult).then_inc(lru_w2, 1)
                stt(A[:, 6, :], A[:, 6, :], 1.0, xc, ALU.add, ALU.mult)
                cp(l_ab[:, :, 1:9], A[:, 4, SEQ:T].rearrange("p (b t) -> p b t", b=NB))
                v.memset(l_ab[:, :, 0:1], 0.0)
                v.drain()
                fill(2)
                v.wait_ge(lru_sq, n)
                stt(A[:, 7, :], A[:, 6, :], 0.5, A[:, 7, :], ALU.mult, ALU.mult)
                v.drain()
                v.tensor_tensor_scan(O[:, 0:SEQ], A[:, 4, 0:SEQ], A[:, 7, 0:SEQ], 0.0, ALU.mult, ALU.add)
                cp(l_ub[:, :, 1:9], A[:, 7, SEQ:T].rearrange("p (b t) -> p b t", b=NB))
                v.drain()
                fill(3)
                v.tensor_tensor_scan(l_hb[:, :, :].rearrange("p b t -> p (b t)"), l_ab[:, :, :].rearrange("p b t -> p (b t)"),
                                     l_ub[:, :, :].rearrange("p b t -> p (b t)"), 0.0, ALU.mult, ALU.add)
                cp(l_tail[:, 0:1], O[:, SEQ - 1:SEQ])
                cp(l_tail[:, 9:12], X[:, SEQ - 3:SEQ])
                cp(l_tail[:, 12:36].rearrange("p (b j) -> p b j", b=NB),
                   X[:, SEQ:T].rearrange("p (b t) -> p b t", b=NB)[:, :, NS - 3:NS])
                v.drain()
                cp(O[:, SEQ:T].rearrange("p (b t) -> p b t", b=NB), l_hb[:, :, 1:9])
                cp(l_tail[:, 1:9].rearrange("p (b o) -> p b o", o=1), l_hb[:, :, 8:9]).then_inc(lru_done, 1)
                if not final:
                    lru_conv_start(n + 1, ct + 1)
                v.drain()
                fill(4)
                if not final:
                    lru_taps(lru_x(ct + 1), (1, 0), last=True)
                fill(5)
                if not final:
                    lru_decay(n + 1)
                v.drain()

            def swa_rotate(s, n, tok, w):
                kk = s_k[:, s + 1, :] if w == P else s_k[:, 0, 0:w]
                C, S = (A[:, 6, tok], A[:, 7, tok]) if w == P else (s_tab[:, 0, :], s_tab[:, 1, :])
                tq, tk = s_tq[s], s_tk[s]
                v.wait_ge(swa_rot, n)
                tt(s_q[s][:, :, 0:w], A[:, 0:4, tok], bc(C, 4), ALU.mult)
                tt(tq[:, :, 0:w], B[3 + 2 * s][:, 0:4 * w].rearrange("p (m t) -> p m t", m=4), bc(S, 4), ALU.mult)
                tt(kk, A[:, 4, tok], C, ALU.mult)
                tt(tk[:, 0:w], B[4 + 2 * s][:, 0:w], S, ALU.mult)
                cp(s_vn[0:w, s + 1, :], B[4 + 2 * s][0:w, P:2 * P])
                v.drain()
                tt(s_q[s][:, :, 0:w], s_q[s][:, :, 0:w], tq[:, :, 0:w], ALU.add)
                last = tt(kk, kk, tk[:, 0:w], ALU.add)
                if w == P:
                    last.then_inc(swa_qk, 1)
                    return
                v.drain()
                for e in range(2):
                    r = slice(64 * e, 64 * e + 64)
                    last = cp(s_qbd[r, :, 32 * e:32 * e + 32].rearrange("p b (i t) -> p b i t", i=4),
                              s_q[s][r, :, 0:w].rearrange("p i (b t) -> p b i t", b=NB))
                last.then_inc(swa_qk, 1)

            def swa_maxima(s, w, sink):
                v.drain()
                v.tensor_reduce(s_mx[s][:, :], s_pr[s][:, :, 0:w], AX_X, ALU.max)
                v.drain()
                stt(s_mx[s][:, :], s_mx[s][:, :], HEAD_SCALE, sink, ALU.mult, ALU.max)
                v.drain()
                ts(s_nm[s][:, :], s_mx[s][:, :], -1.0, None, ALU.mult)
                tt(s_es[s][:, :], sink, s_mx[s][:, :], ALU.subtract).then_inc(swa_max, 1)

            def swa_normalise(s, at, w):
                v.wait_ge(swa_exp, at)
                tt(s_sum[s][:, :], s_sum[s][:, :], s_es[s][:, :], ALU.add)
                v.drain()
                v.reciprocal(s_sum[s][:, :], s_sum[s][:, :])
                v.drain()
                tt(s_pr[s][:, :, 0:w], s_pr[s][:, :, 0:w], bl(s_sum[s][:, :], w), ALU.mult).then_inc(swa_prob, 1)

            def swa_pair(l, i, fill):
                tok = lambda s: bass.ds(2 * P * i + P * s, P)
                start = isinstance(i, int)
                if start:
                    cp(s_tab[:, :, :], A[:, 6:8, SEQ:T])
                    v.memset(s_vn[:, 0, :], 0.0)
                    v.memset(s_k[:, 0, :], 0.0)
                else:
                    cp(s_vn[:, 0, :], s_vn[:, 2, :])
                    cp(s_k[:, 0, :], s_k[:, 2, :])
                for s in range(2):
                    cp(s_v[s][:, 0:P], A[:, 5, tok(s)]).then_inc(swa_vst, 1)
                v.drain()
                for s in range(2):
                    swa_rotate(s, STEPS * l + 2 * i + s + 1, tok(s), P)
                fill(0)
                for r in range(2):
                    at = (2 * STEPS - 1) * l + 4 * i + 2 * r
                    for s in range(2):
                        v.wait_ge(swa_scores, at + s + 1)
                        for e in range(2):
                            sc = B[3 + 2 * s + e][:, :].rearrange("p (m s) -> p m s", m=2)
                            pr = s_pr[s][:, 2 * e:2 * e + 2, :]
                            if start and s == 0:
                                v.memset(pr[:, :, 0:P], NEG)
                                tt(pr[:, :, P:2 * P], sc[:, :, P:2 * P], bc(s_mask[:, P:2 * P], 2), ALU.add)
                            else:
                                tt(pr, sc, bc(s_mask, 2), ALU.add)
                        swa_maxima(s, 2 * P, s_sink[:, 4 * r:4 * r + 4])
                    fill(1 + 2 * r)
                    for s in range(2):
                        swa_normalise(s, at + s + 1, 2 * P)
                    fill(2 + 2 * r)
                    for s in range(2):
                        v.wait_ge(swa_pt, at + s + 1)
                        cp(s_pt[s][:, 4:8, :].rearrange("p a b -> p (a b)"), B[4 + 2 * s][:, :]).then_inc(swa_ptd, 1)
                    v.wait_ge(swa_o, at + 2)
                    hold(v, "dve")
                    for s in range(2):
                        cp(A[:, 2 * r:2 * r + 2, tok(s)],
                           B[7][:, 256 * s:256 * s + 256].rearrange("p (m t) -> p m t", m=2))
                    v.drain()
                fill(5)

            def swa_samples(l):
                n = STEPS * (l + 1)
                m = (2 * STEPS - 1) * (l + 1)
                w = NSAMP
                cp(s_v[0][:, 0:w], A[:, 5, SEQ:T])
                v.memset(s_qbd[:, :, :], 0.0).then_inc(swa_vst, 1)
                v.drain()
                swa_rotate(0, n, slice(SEQ, T), w)
                v.wait_ge(swa_scores, m)
                for g in range(2):
                    tt(s_pr[0][:, 2 * g:2 * g + 2, 0:192], B[5 + g][:, :].rearrange("p (u s) -> p u s", u=2)[:, :, 0:192],
                       s_smask[:, 2 * g:2 * g + 2, :], ALU.add)
                swa_maxima(0, 192, s_sinkr[:, 0:1].broadcast_to([P, 4]))
                swa_normalise(0, m, 192)
                v.wait_ge(swa_pt, m)
                cp(s_pt[0][0:w, 4:8, :].rearrange("p a b -> p (a b)"), B[6][0:w, :]).then_inc(swa_ptd, 1)
                v.wait_ge(swa_o, m)
                for e in range(2):
                    r = slice(64 * e, 64 * e + 64)
                    cp(A[r, 0:4, SEQ:T].rearrange("p i (b t) -> p b i t", b=NB),
                       B[7][r, :].rearrange("p (b h t) -> p b h t", b=NB, h=8)[:, :, 4 * e:4 * e + 4, :])
                v.drain()

            def sgu_norm(s, n, w):
                rows = B[3 + 2 * s][0:w, :]
                v.wait_ge(sgu_vt, n)
                v.bn_stats(g_bn[s][0:w, :], rows)
                v.drain()
                v.bn_aggr(g_mv[s][0:w, :], g_bn[s][0:w, :])
                v.drain()
                ts(g_rs[s][0:w, :], g_mv[s][0:w, 1:2], LN_EPS, None, ALU.add)
                v.drain()
                v.reciprocal(g_rs[s][0:w, :], g_rs[s][0:w, :]).then_inc(sgu_var, 1)

            def sgu_affine(s, n, w):
                v.wait_ge(sgu_rstd, n)
                vn = g_vn[s][0:w, :]
                ts(vn, B[3 + 2 * s][0:w, :], g_mv[s][0:w, 0:1], g_rs[s][0:w, :], ALU.subtract, ALU.mult)
                v.drain()
                tt(vn, vn, g_lng[0:w, :], ALU.mult)
                v.drain()
                tt(vn, vn, g_lnb[0:w, :], ALU.add).then_inc(sgu_vn, 1)

            def sgu_gate(s, n, w, tok):
                v.wait_ge(sgu_mix, n)
                vs = g_vs[s][:, 0:4 * w].rearrange("p (g t) -> p g t", g=4)
                tt(vs, B[4 + 2 * s][:, 0:4 * w].rearrange("p (g t) -> p g t", g=4),
                   g_b[:, :, :] if w == P else g_bs[:, :, :], ALU.add)
                v.drain()
                tt(A[:, 0:4, tok], A[:, 0:4, tok], vs, ALU.mult)

            def sgu_pair(l, i, fill):
                tok = lambda s: bass.ds(2 * P * i + P * s, P)
                n = lambda s: STEPS * l + 2 * i + s + 1
                for s in range(2):
                    cp(g_v[s][:, :, :], A[:, 4:8, tok(s)]).then_inc(sgu_vst, 1)
                for s in range(2):
                    sgu_norm(s, n(s), P)
                for s in range(2):
                    sgu_affine(s, n(s), P)
                for k in range(3):
                    fill(k)
                for s in range(2):
                    sgu_gate(s, n(s), P, tok(s))
                for k in range(3, 6):
                    fill(k)
                v.drain()

            def sgu_samples(l):
                n = STEPS * (l + 1)
                w = NSAMP
                cp(g_v[0][:, :, 0:w], A[:, 4:8, SEQ:T]).then_inc(sgu_vst, 1)
                sgu_norm(0, n, w)
                sgu_affine(0, n, w)
                sgu_gate(0, n, w, slice(SEQ, T))
                v.drain()

            def ref(w, block, pos):
                s = a_b[:, :, 0:w].rearrange("p h (m t) -> p h m t", t=block)
                return s[:, :, :, pos:pos + 1].broadcast_to([P, 2, w // block, block])

            def blocks(ap, w, block):
                return ap[:, :, 0:w].rearrange("p h (m t) -> p h m t", t=block)

            def gla_decays(l):
                for c, (a, z) in enumerate(CHUNKS):
                    w = z - a
                    v.wait_ge(gla_x, NC * l + c + 1)
                    for p in range(2):
                        ts(a_x[:, p, 0:w], B[3 + p][:, 0:w], a_ba[:, p:p + 1], None, ALU.add)
                    v.drain()
                    stt(a_e[:, :, 0:w], a_x[:, :, 0:w], -1.0, a_x[:, :, 0:w], ALU.mult, ALU.min).then_inc(gla_na, 1)
                    v.wait_ge(gla_e, NC * l + c + 1)
                    for p, la in enumerate((A[:, 8, a:z], a_la[:, a:z])):
                        stt(la, a_x[:, p, 0:w], 0.0, a_e[:, p, 0:w], ALU.min, ALU.subtract)
                    v.drain()

            def gla_front(n, w, tok, levels, one, block):
                cp(a_v[:, :, 0:w], A[:, 4:8, tok]).then_inc(gla_vst, 1)
                v.tensor_tensor_scan(a_b[:, 0, 0:w], one, A[:, 8, tok], 0.0, ALU.mult, ALU.add)
                v.tensor_tensor_scan(a_b[:, 1, 0:w], one, a_la[:, tok], 0.0, ALU.mult, ALU.add)
                v.drain()
                for k, (size, pos) in enumerate(levels):
                    tt(blocks(level(a_dq, k), w, size), blocks(a_b, w, size), ref(w, size, pos), ALU.subtract)
                tt(blocks(level(a_dk, NLEV), w, block), ref(w, block, block - 1), blocks(a_b, w, block), ALU.subtract)
                m = w // block
                cp(a_dec[:, 0:2 * m].rearrange("p (h m o) -> p h m o", h=2, o=1),
                   blocks(a_b, w, block)[:, :, :, block - 1:block])
                v.drain()
                for k in range(len(levels)):
                    q, kk = level(a_dq, k)[:, :, 0:w], level(a_dk, k)[:, :, 0:w]
                    ts(kk, q, -1.0, CLAMP, ALU.mult, ALU.min)
                v.drain()
                for k in range(len(levels)):
                    q = level(a_dq, k)[:, :, 0:w]
                    last = ts(q, q, CLAMP, None, ALU.min)
                last.then_inc(gla_d, 1)

            def gla_scale(n, w, tok, levels):
                v.wait_ge(gla_ex, n)
                for k in [*range(levels), NLEV]:
                    q, kk = level(a_dq, k)[:, :, 0:w], level(a_dk, k)[:, :, 0:w]
                    stt(q, A[:, 0:2, tok], HEAD_SCALE, q, ALU.mult, ALU.mult)
                    last = tt(kk, A[:, 2:4, tok], kk, ALU.mult)
                last.then_inc(gla_qk, 1)

            def gla_attention(n, w, k, mask):
                v.wait_ge(gla_att, n)
                hold(v, "dve")
                ps = [B[3 + e][0:w, :].rearrange("p (k h t) -> p k h t", k=2, h=2)[:, :, :, 0:w] for e in range(2)]
                if k:
                    for e in range(2):
                        cp(a_att[0:HALF, 2 * e:2 * e + 2, HALF:w], ps[e][0:HALF, 0, :, HALF:w])
                    v.drain()
                for e in range(2):
                    last = v.copy_predicated(a_att[0:w, 2 * e:2 * e + 2, 0:w], bc(mask, 2).bitcast(U32), ps[e][:, k])
                last.then_inc(gla_attm, 1)

            four = lambda ap, w: ap.rearrange("p (h t) -> p h t", h=4)[:, :, 0:w]

            def gla_variance(n, w, bank):
                v.wait_ge(gla_ss, n)
                ts(four(a_rs, w), four(B[bank][:, :], w), 1.0 / P, RMS_EPS, ALU.mult, ALU.add)
                v.drain()
                v.reciprocal(four(a_rs, w), four(a_rs, w)).then_inc(gla_rec, 1)

            def gla_norm(n, i):
                v.wait_ge(gla_rstd, n)
                o = A[:, 4:8, bass.ds(P * i, P)]
                stt(o, o, a_ng[:, 0:1], four(a_rs, P), ALU.mult, ALU.mult).then_inc(gla_nd, 1)

            def gla_sample_front(l):
                v.memset(a_att[:, :, :], 0.0)
                v.memset(a_reset, 1.0)
                v.drain()
                v.memset(a_reset.rearrange("p (b t) -> p b t", t=NS)[:, :, 0:1], 0.0)
                v.drain()
                gla_front(STEPS * (l + 1), NSAMP, slice(SEQ, T), [(NS, NS // 2 - 1)], a_reset, NS)

            def gla_sample_scale(l):
                v.wait_ge(gla_ex, STEPS * (l + 1))
                hold(v, "dve")
                for k in (0, NLEV):
                    q, kk = level(a_dq, k)[:, :, 0:NSAMP], level(a_dk, k)[:, :, 0:NSAMP]
                    stt(q, A[:, 0:2, SEQ:T], HEAD_SCALE, q, ALU.mult, ALU.mult)
                    last = tt(kk, A[:, 2:4, SEQ:T], kk, ALU.mult)
                last.then_inc(gla_qk, 1)
                v.drain()
                v.sem_inc(gla_kh, 1)

            def gla_step(l, i, fill):
                n = STEPS * l + i + 1
                after = bass.ds(P * i + P, P)
                first = isinstance(i, int) and i == 0
                final = isinstance(i, int) and i == NTT - 1
                gla_attention(n, P, 1, a_mask)
                fill(0)
                v.wait_ge(gla_st, NTT * l + i + 1)
                hold(v, "dve")
                for h in range(4):
                    p, e = h // 2, h % 2
                    r = slice(64 * e, 64 * e + 64)
                    stt(a_S[r, h, :], a_S[r, h, :], a_dec[r, p:p + 1],
                        B[5][r, 256 * p + P * e:256 * p + P * e + P], ALU.mult, ALU.add)
                v.drain()
                if final:
                    gla_sample_front(l)
                else:
                    gla_front(n + 1, P, after, LEVELS, ones[:, :], P)
                fill(1)
                if not first:
                    gla_variance(n - 1, P, 3)
                if final:
                    gla_sample_scale(l)
                else:
                    gla_scale(n + 1, P, after, NLEV)
                fill(2)
                if not first:
                    gla_norm(n - 1, i - 1)
                v.drain()

            def gla_samples(l):
                n = STEPS * l + STEPS
                w = NSAMP
                tok = slice(SEQ, T)
                gla_attention(n, w, 0, a_smask[0:w, :])
                gla_variance(n - 1, P, 6)
                v.wait_ge(gla_kn, n)
                hold(v, "dve")
                S0 = sample_states()
                for b in range(NB):
                    km = (a_km, level(a_dk, 0))[b % 2]
                    ts(km[0:w, :, :], a_kn[0:w, :, :], a_smask[0:w, NS * b + NS - 1:NS * b + NS], None, ALU.mult).then_inc(gla_km, 1)
                    if b == 0:
                        v.wait_ge(gla_s0, 16 * (l + 1))
                        hold(v, "dve")
                    if b:
                        gla_sample_update(l, S0, b - 1)
                gla_sample_update(l, S0, NB - 1)
                gla_norm(n - 1, NTT - 1)
                v.drain()
                cp(four(a_rs, w), four(B[6][:, :], w))
                v.drain()
                tt(four(a_vn, w), four(B[7][:, :], w), four(a_rs, w), ALU.add).then_inc(gla_os, 1)
                gla_variance(n, w, 6)
                v.wait_ge(gla_rstd, n)
                stt(A[:, 4:8, tok], four(a_vn, w), a_ng[:, 0:1], four(a_rs, w), ALU.mult, ALU.mult)
                v.drain()

            def gla_sample_update(l, S0, b):
                v.wait_ge(gla_sts, NB * l + b + 1)
                for h in range(4):
                    p, e = h // 2, h % 2
                    r = slice(64 * e, 64 * e + 64)
                    stt(S0[r, b, h, :], S0[r, b, h, :], a_dec[r, NB * p + b:NB * p + b + 1],
                        B[(5, 3)[b % 2]][r, 256 * p + P * e:256 * p + P * e + P], ALU.mult, ALU.add)

            v.sem_inc(g_free_dve, 3)
            v.sem_inc(p_free, 2)
            v.sem_inc(y_ready, 2)
            v.sem_inc(gla_nd, 1)
            layer_norm(0)
            with v.Fori(0, DEPTH) as l:
                v.memset(m_qbd[:, :, :, :], 0.0)
                v.drain()
                inputs_ready(l, "in", MEM)
                with v.Fori(0, NTT // 2) as i:
                    mem_pair(l, i)
                mem_samples(l)
                z_phase(l, MEM)
                lru_decay(4 * l + 1)
                v.drain()
                for b in range(NBR):
                    if b + 1 == LRU:
                        with v.Fori(0, 3) as i:
                            lru_step(l, i, fills(l, b, 2 * i))
                        lru_step(l, 3, fills(l, b, 6))
                    if b + 1 == SWA:
                        swa_pair(l, 0, fills(l, b, 0))
                        with v.Fori(1, NTT // 2) as i:
                            swa_pair(l, i, fills(l, b, 2 * i))
                        swa_samples(l)
                    if b + 1 == SGU:
                        tt(g_w[:, :, :], g_w[:, :, :], bc(g_m[:, :], 4), ALU.mult)
                        tt(g_ws[0:NSAMP, :, :], g_ws[0:NSAMP, :, :], bc(g_ms[0:NSAMP, :], 4), ALU.mult)
                        v.drain()
                        with v.Fori(0, NTT // 2) as i:
                            sgu_pair(l, i, fills(l, b, 2 * i))
                        sgu_samples(l)
                    if b + 1 == GLA:
                        v.memset(a_S[:, :, :], 0.0)
                        v.memset(a_att[:, :, :], 0.0)
                        v.memset(a_dec[:, :], 0.0)
                        v.drain()
                        gla_decays(l)
                        gla_front(STEPS * l + 1, P, slice(0, P), LEVELS, ones[:, :], P)
                        gla_scale(STEPS * l + 1, P, slice(0, P), NLEV)
                        gla_step(l, 0, fills(l, b, 0))
                        with v.Fori(1, NTT - 1) as i:
                            gla_step(l, i, fills(l, b, i))
                        gla_step(l, NTT - 1, fills(l, b, NTT - 1))
                        gla_samples(l)
                    if b + 1 == NBR:
                        with v.Fori(0, KD) as i:
                            for c in range(NC):
                                merge_unit(l, b, i, c)
                    if b + 1 < NBR:
                        z_phase(l, b + 1)
                    if b + 2 < NBR:
                        inputs_ready(l, "in", b + 2)
                        if b + 2 == GLA:
                            inputs_ready(l, "rank", GLA)
                        v.wait_ge(loaded[b + 2], 16 * LOADS[b + 2] * (l + 1))
                        hold(v, "dve")
                v.drain()
                v.sem_inc(merged_sum, 1)
                for c, (a, z) in enumerate(CHUNKS):
                    v.wait_ge(merged_high, NC * l + c + 1)
                    stt(xl[:, :, a:z], merged[:, :, a:z], 0.5, xh[:, :, a:z].bitcast(F32), ALU.mult, ALU.subtract)\
                        .then_inc(m_ready, 1)
                v.drain()
                t = TABLE["out", 0]
                v.wait_ge(res_loaded, 16 * (l + 1))
                hold(v, "dve")
                with v.Fori(0, KD // 2) as i:
                  for s in range(2):
                    for c, (a, z) in enumerate(CHUNKS):
                        v.wait_ge(g_full, NG * l + NC * (t["w8"] + 2 * i + s) + c + 1)
                        one = lambda ap: ap[:, bass.ds(2 * i + s, 1), a:z].rearrange("p o t -> p (o t)")
                        stt(one(merged), one(A), DN_ALPHA, B[(NC * s + c) % 2][:, 0:z - a], ALU.mult, ALU.add).then_inc(g_free_dve, 1)
                layer_norm(l + 1)


OFF = dict(gq=0, gk=256, gv=512, glr=1024, gz=1040, lx=1552, lz=2064, sq=2576, sk=3088, sv=3216, sz=3344,
           su=3856, svv=4368, suz=4880, mq=5392, mz=5648, gates=5904)


def feature_tiles():
    import numpy as np
    span = lambda name, n: [np.arange(OFF[name] + P * i, OFF[name] + P * i + P) for i in range(n)]
    pairs = lambda name: [np.concatenate([np.arange(OFF[name] + 64 * h, OFF[name] + 64 * h + 64) for h in (i, 4 + i)])
                          for i in range(4)]
    inputs = [span("mq", 2), span("lx", 4), pairs("sq") + span("sk", 1) + span("sv", 1),
              span("su", 4) + span("svv", 4), span("gq", 2) + span("gk", 2) + span("gv", 4)]
    zs = [span("mz", 2), span("lz", 4), pairs("sz"), span("suz", 4), span("gz", 4)]
    tiles = []
    for kind, b, n in PHASES:
        if kind == "in":
            tiles += inputs[b]
        if kind == "z":
            tiles += zs[b]
        if kind == "rank":
            tiles.append(np.arange(OFF["glr"], OFF["glr"] + 16))
        if kind == "merge":
            g = OFF["gates"] + D * GATE_OF[b]
            tiles += [np.arange(g + P * j, g + P * j + P) for j in range(KD)]
        if kind == "out":
            tiles += [None] * KD
    return tiles


def constants():
    import numpy as np
    f = np.float32
    i, j = np.arange(P)[:, None], np.arange(P)[None, :]
    c = dict(ident=np.eye(P, dtype=f), tril=(i <= j).astype(f))
    a, b = np.arange(NSAMP)[:, None], np.arange(NSAMP)[None, :]
    c["tril8"] = ((a // NS == b // NS) & (a <= b)).astype(f)
    c["gla_mask"] = ((i // HALF == j // HALF) & (i <= j)).astype(f)
    c["swa_mask"] = np.concatenate([np.where(j >= i, 0, NEG), np.where(j <= i, 0, NEG)], axis=1).astype(f)
    sm = np.zeros((P, 4, P + NSAMP), f)
    for row in range(P):
        t = row % NS
        for u in range(4):
            seq = 2 * u + row // 64
            sm[row, u, :P] = np.where(np.arange(P) >= t, 0, NEG)
            sm[row, u, P:] = np.where((b[0] // NS == seq) & (b[0] % NS <= t), 0, NEG)
    c["swa_smask"] = sm
    rot = np.zeros((P, P), f)
    dd = np.arange(P)
    for m in dd[dd % 64 < 8]:
        rot[m + 8, m] = 1
        rot[m, m + 8] = 1
    c["rot"] = rot
    pos = np.concatenate([np.arange(SEQ), np.tile(2048 + np.arange(NS), NB)]).astype(f)
    inv = (f(500000.0) ** (-np.arange(8, dtype=f) / f(8))).astype(f)
    ang = (pos[None, :] * inv[:, None]).astype(f)
    rope = np.zeros((P, 2, T), f)
    rope[:, 0] = 1
    for base in (0, 64):
        rope[base:base + 8, 0] = rope[base + 8:base + 16, 0] = np.cos(ang.astype(np.float64))
        rope[base:base + 8, 1] = -np.sin(ang.astype(np.float64))
        rope[base + 8:base + 16, 1] = np.sin(ang.astype(np.float64))
    c["rope"] = rope
    return c


def kernel(**inputs):
    import numpy as np
    import concourse.bacc as bacc
    from concourse.bass_utils import run_bass_kernel_spmd

    g = {k: np.asarray(v) for k, v in inputs.items()}
    f = np.float32
    arrays = constants()

    def feature_major(x):
        return x.T.reshape(-1, P, x.shape[0]).transpose(1, 0, 2)

    def subtiles(w):
        return w.reshape(-1, P, w.shape[1]).transpose(1, 0, 2)

    arrays["x"] = feature_major(np.concatenate([g["x_prompt"][0], g["x_sample"].reshape(NSAMP, D)]))
    arrays["mem"] = feature_major(g["mem_prompt"][0]).reshape(P, -1)
    arrays["w_mem"] = np.stack([subtiles(w).reshape(P, -1) for w in g["w_mem_kv"]])
    tiles = feature_tiles()
    w8 = np.zeros((DEPTH, N8, P, KD, P), f)
    w4 = np.zeros((DEPTH, N4, P, 4, P), f)
    swa_rows = np.concatenate([np.arange(64 * h, 64 * h + 64) for i in range(4) for h in (i, 4 + i)])
    for l in range(DEPTH):
        win, wout = subtiles(g["w_in"][l]), subtiles(g["w_out"][l])
        j = 0
        for n, cols in enumerate(tiles):
            if cols is None:
                w8[l, n] = wout[:, :, P * j:P * j + P]
                j += 1
            else:
                w8[l, n, :, :, :len(cols)] = win[:, :, cols]
        for b in range(NBR):
            wbr = g["w_branch_mem"][l] if b == MEM else g["w_branch"][l, GATE_OF[b]]
            if b == SWA:
                wbr = wbr[swa_rows]
            for j in range(KD):
                w4[l, KD * b + j, :, :Y_TILES[b]] = subtiles(wbr)[:, :, P * j:P * j + P]
    arrays["w8"] = w8.reshape(DEPTH * N8, P, -1)
    arrays["w4"] = w4.reshape(DEPTH * N4, P, -1)

    def columns(v):
        return v.reshape(-1, P).T

    lnp = [np.concatenate([columns(g["ln_in_g"]), columns(g["ln_in_b"])], axis=1)]
    lnp += [np.concatenate([columns(g["ln_g"][l]), columns(g["ln_b"][l])], axis=1) for l in range(DEPTH)]
    arrays["lnp"] = np.stack(lnp)

    K, V = g["cache_mem_k"], g["cache_mem_v"]
    kt = K.transpose(0, 1, 3, 4, 2).reshape(DEPTH * NB, 2, P, N_MEM).transpose(0, 2, 1, 3)
    vv = V.reshape(DEPTH * NB, 2, P, 256).transpose(0, 2, 1, 3)
    arrays["memkv"] = np.concatenate([kt.reshape(-1, P, 512), vv.reshape(-1, P, 512)], axis=2)
    K, V = g["cache_swa_k"], g["cache_swa_v"]
    kt = K.transpose(0, 3, 4, 1, 2).reshape(DEPTH, P, NB, WINDOW)
    vv = V.reshape(DEPTH, NB, WINDOW, P).transpose(0, 2, 1, 3)
    arrays["swakv"] = np.concatenate([kt, vv], axis=3)
    arrays["cache_k"] = K.reshape(DEPTH, NB, WINDOW, P)
    arrays["cache_v"] = V.reshape(DEPTH, NB, WINDOW, P)
    sinks = g["swa_sinks"]
    order = [4 * e + 2 * r + m for r in range(2) for e in range(2) for m in range(2)]
    arrays["sink"] = np.broadcast_to(sinks[:, None, order], (DEPTH, P, 8))
    arrays["sinkr"] = sinks[:, (np.arange(P) % 64) // NS][:, :, None]

    arrays["sgu_g"], arrays["sgu_b"] = g["sgu_ln_g"], g["sgu_ln_b"]
    wt = g["sgu_w"].transpose(0, 3, 1, 2)
    arrays["sgu_w"] = wt
    ws = np.zeros((DEPTH, NB, NS, 4, NB, NS), f)
    for b in range(NB):
        ws[:, b, :, :, b, :] = wt[:, :NS, :, :NS]
    arrays["sgu_ws"] = ws.reshape(DEPTH, NSAMP, 4, NSAMP)
    arrays["sgu_bs"] = g["sgu_b"]
    arrays["sgu_bss"] = np.tile(g["sgu_b"][:, :, :NS], (1, 1, NB))

    arrays["wa2"] = g["gla_wa2"]
    arrays["ba"] = np.stack([columns(v) for v in g["gla_ba"]])
    arrays["ng"] = g["gla_norm_g"][:, :, None]
    s0 = np.zeros((DEPTH, P, NB, 4, P), f)
    for h in range(4):
        r = 64 * (h % 2)
        s0[:, r:r + 64, :, h] = g["state_gla"][:, :, h].transpose(0, 2, 1, 3)
    arrays["gla_s0"] = s0

    lru = np.zeros((DEPTH, 4, P, LW_N), f)
    for l in range(DEPTH):
        for ct in range(4):
            for e in range(2):
                r = slice(64 * e, 64 * e + 64)
                lru[l, ct, r, LW_WR + 64 * e:LW_WR + 64 * e + 64] = g["lru_wr"][l, 2 * ct + e]
                lru[l, ct, r, LW_WI + 64 * e:LW_WI + 64 * e + 64] = g["lru_wi"][l, 2 * ct + e]
            ch = slice(P * ct, P * ct + P)
            lru[l, ct, :, LW_CW:LW_CW + 4] = g["lru_conv_w"][l, :, ch].T
            for at, name in ((LW_CB, "lru_conv_b"), (LW_BR, "lru_br"), (LW_BI, "lru_bi"), (LW_LAM, "lru_L")):
                lru[l, ct, :, at] = g[name][l, ch]
            lru[l, ct, :, LW_H0:LW_H0 + NB] = g["state_lru_h"][l, :, ch].T
            lru[l, ct, :, LW_CONV:] = g["state_lru_conv"][l, :, :, ch].transpose(2, 0, 1).reshape(P, -1)
    arrays["lru"] = lru.reshape(DEPTH * 4, P, LW_N)

    outs = dict(y=(P, KD, T), mkv=(DEPTH, P, 1024), lru_tail=(DEPTH * 4, P, NTAIL),
                swa_new=(DEPTH, P, 2 * P + 2 * NSAMP), swa_old_k=(DEPTH, NB, WINDOW - NS, P),
                swa_old_v=(DEPTH, NB, WINDOW - NS, P), gla_p=(DEPTH, P, 4, P), gla_s=(DEPTH, P, NB, 4, P),
                sgu_v=(DEPTH, NSAMP, 512))
    nc = bacc.Bacc("TRN2", target_bir_lowering=False, num_devices=1)
    d, feed = {}, {}
    for name, a in arrays.items():
        feed["in_" + name] = np.ascontiguousarray(a)
        d[name] = nc.dram_tensor("in_" + name, a.shape, mybir.dt.from_np(a.dtype), kind="ExternalInput").ap()
    for name, shape in outs.items():
        d[name] = nc.dram_tensor("out_" + name, shape, F32, kind="ExternalOutput").ap()
    build(nc, d)
    got = run_bass_kernel_spmd(nc, [feed], core_ids=[0]).results[0]
    o = {name: np.asarray(got["out_" + name]) for name in outs}

    y = o["y"].transpose(1, 0, 2).reshape(D, T).T
    half = lambda h: slice(64 * (h % 2), 64 * (h % 2) + 64)
    gla_p = np.stack([o["gla_p"][:, half(h), h] for h in range(4)], axis=1)[:, None]
    gla_s = np.stack([o["gla_s"][:, half(h), :, h].transpose(0, 2, 1, 3) for h in range(4)], axis=2)
    tail = o["lru_tail"].reshape(DEPTH, 512, NTAIL)
    lru_p, lru_s = tail[:, :, 0][:, None], tail[:, :, 1:9].transpose(0, 2, 1)
    conv = tail[:, :, 9:].reshape(DEPTH, 512, 9, 3).transpose(0, 2, 3, 1)
    new = o["swa_new"]

    def window(at, n):
        return new[:, :, at:at + n].transpose(0, 2, 1)

    def swa_prompt(at):
        return window(at, P).reshape(DEPTH, 1, WINDOW, 2, 64)

    def swa_sample(at, old):
        return np.concatenate([old, window(at, NSAMP).reshape(DEPTH, NB, NS, P)], axis=2)\
            .reshape(DEPTH, NB, WINDOW, 2, 64)

    mk = o["mkv"][:, :, :512].reshape(DEPTH, P, 2, N_MEM).transpose(0, 3, 2, 1).reshape(DEPTH, 1, N_MEM, 4, 64)
    mv = o["mkv"][:, :, 512:].reshape(DEPTH, P, 2, 256).transpose(0, 2, 1, 3).reshape(DEPTH, 1, N_MEM, 4, 64)
    result = (y[:SEQ].reshape(1, SEQ, D), y[SEQ:].reshape(NB, NS, D), gla_p, gla_s, lru_p, lru_s,
              conv[:, 0:1], conv[:, 1:], swa_prompt(0), swa_sample(2 * P, o["swa_old_k"]),
              swa_prompt(P), swa_sample(2 * P + NSAMP, o["swa_old_v"]), mk, mv,
              o["sgu_v"].reshape(DEPTH, NB, NS, 512))
    return tuple(np.ascontiguousarray(a) for a in result)
```
